# Optimizing a Trainium2 kernel written in Bass

```python
import jax, jax.numpy as jnp
from jax import lax
import numpy as np

D_MODEL = 1024
BATCH = 1
SEQ = 512
DEPTH = 1

N_META = 16
N_HEADS = 8
HEAD_DIM = 128
ATTN_WIDTH = N_HEADS * HEAD_DIM
N_IDX_HEADS = 8
IDX_DIM = 64
TOPK_MAX = 256
CONV_WIDTH = D_MODEL
CONV_K = 3
D_FF = ((8 * D_MODEL // 3 + 255) // 256) * 256
Q_BLOCK = 128
EPS = 1e-6
IDX_SCALE = (N_IDX_HEADS ** -0.5) * (IDX_DIM ** -0.5)

_PROJ_SIZES = [ATTN_WIDTH, ATTN_WIDTH, ATTN_WIDTH,
               N_IDX_HEADS * IDX_DIM, IDX_DIM, N_IDX_HEADS,
               CONV_WIDTH, CONV_WIDTH, CONV_WIDTH,
               D_MODEL, D_MODEL]
PROJ_WIDTH = int(sum(_PROJ_SIZES))
PROJ_SPLITS = [int(s) for s in np.cumsum(_PROJ_SIZES)[:-1]]


def rmsnorm(x, g):
    xf = x.astype(jnp.float32)
    y = xf * lax.rsqrt(jnp.mean(xf * xf, axis=-1, keepdims=True) + EPS)
    return (y * g.astype(jnp.float32)).astype(x.dtype)

def dsa_attention(q, k, v, q_idx, k_idx, w_idx):
    b, l = q.shape[0], q.shape[1]
    topk = min(TOPK_MAX, l // 4)
    n_blk = -(-l // Q_BLOCK)
    lp = n_blk * Q_BLOCK

    def pad(a):
        return jnp.pad(a, [(0, 0), (0, lp - l)] + [(0, 0)] * (a.ndim - 2))

    q, k, v, q_idx, k_idx, w_idx = (pad(a) for a in (q, k, v, q_idx, k_idx, w_idx))
    key_pos = jnp.arange(lp)

    def to_blocks(a):
        return jnp.moveaxis(a.reshape((b, n_blk, Q_BLOCK) + a.shape[2:]), 1, 0)

    def one_block(args):
        q_b, qi_b, w_b, start = args
        q_pos = start + jnp.arange(Q_BLOCK)
        visible = key_pos[None, :] <= q_pos[:, None]
        rel = jax.nn.relu(jnp.einsum('bthd,bsd->bths', qi_b, k_idx).astype(jnp.float32))
        score = jnp.einsum('bths,bth->bts', rel, w_b.astype(jnp.float32) * IDX_SCALE)
        score = jnp.where(visible[None], score, -jnp.inf)
        _, sel = lax.top_k(score, topk)
        k_sel = jax.vmap(lambda kb, ib: kb[ib])(k, sel)
        v_sel = jax.vmap(lambda vb, ib: vb[ib])(v, sel)
        valid = sel <= q_pos[None, :, None]
        logits = jnp.einsum('bthd,btkhd->bthk', q_b, k_sel).astype(jnp.float32) * (HEAD_DIM ** -0.5)
        logits = jnp.where(valid[:, :, None, :], logits, -jnp.inf)
        p = jax.nn.softmax(logits, axis=-1).astype(v_sel.dtype)
        return jnp.einsum('bthk,btkhd->bthd', p, v_sel)

    starts = jnp.arange(n_blk) * Q_BLOCK
    out = lax.map(one_block, (to_blocks(q), to_blocks(q_idx), to_blocks(w_idx), starts))
    out = jnp.moveaxis(out, 0, 1).reshape(b, lp, N_HEADS, HEAD_DIM)
    return out[:, :l]

def short_conv(u, w):
    return lax.conv_general_dilated(
        u, w[:, None, :].astype(u.dtype), window_strides=(1,), padding=[(CONV_K - 1, 0)],
        dimension_numbers=('NWC', 'WIO', 'NWC'), feature_group_count=u.shape[-1])

def first_inputs(seed: int = 0) -> dict:
    key = jax.random.key(seed)
    ks = jax.random.split(key, 16)
    f32 = jnp.float32
    nrm = lambda k, shape, scale: (jax.random.normal(k, shape, f32) * scale)
    gain = lambda k: 1.0 + 0.02 * jax.random.normal(k, (DEPTH, D_MODEL), f32)
    return {
        "x": nrm(ks[0], (BATCH, SEQ, D_MODEL), 1.0),
        "meta_tokens": nrm(ks[1], (N_META, D_MODEL), 1.0),
        "norm_mix_g": gain(ks[2]),
        "w_in": nrm(ks[3], (DEPTH, D_MODEL, PROJ_WIDTH), D_MODEL ** -0.5),
        "w_attn_out": nrm(ks[4], (DEPTH, ATTN_WIDTH, D_MODEL), ATTN_WIDTH ** -0.5),
        "conv_w": nrm(ks[5], (DEPTH, CONV_K, CONV_WIDTH), CONV_K ** -0.5),
        "w_conv_out": nrm(ks[6], (DEPTH, CONV_WIDTH, D_MODEL), CONV_WIDTH ** -0.5),
        "w_out": nrm(ks[7], (DEPTH, D_MODEL, D_MODEL), D_MODEL ** -0.5),
        "norm_ffn_g": gain(ks[8]),
        "w_gate": nrm(ks[9], (DEPTH, D_MODEL, D_FF), D_MODEL ** -0.5),
        "w_up": nrm(ks[10], (DEPTH, D_MODEL, D_FF), D_MODEL ** -0.5),
        "w_down": nrm(ks[11], (DEPTH, D_FF, D_MODEL), D_FF ** -0.5),
        "norm_final_g": 1.0 + 0.02 * jax.random.normal(ks[12], (D_MODEL,), f32),
    }

def first_block(x, meta_tokens, norm_mix_g, w_in, w_attn_out, conv_w, w_conv_out, w_out,
              norm_ffn_g, w_gate, w_up, w_down, norm_final_g):
    b = x.shape[0]
    meta = jnp.broadcast_to(meta_tokens[None].astype(x.dtype), (b, N_META, x.shape[-1]))
    h = jnp.concatenate([meta, x], axis=1)
    l = h.shape[1]
    for i in range(DEPTH):
        a = rmsnorm(h, norm_mix_g[i])
        proj = a @ w_in[i]
        q, k, v, qi, ki, wi, cu, cb, cc, ga, gb = jnp.split(proj, PROJ_SPLITS, axis=-1)
        y_attn = dsa_attention(q.reshape(b, l, N_HEADS, HEAD_DIM),
                               k.reshape(b, l, N_HEADS, HEAD_DIM),
                               v.reshape(b, l, N_HEADS, HEAD_DIM),
                               qi.reshape(b, l, N_IDX_HEADS, IDX_DIM), ki, wi)
        y_attn = y_attn.reshape(b, l, ATTN_WIDTH) @ w_attn_out[i]
        y_conv = (cb * short_conv(cc * cu, conv_w[i])) @ w_conv_out[i]
        mixed = jax.nn.sigmoid(ga) * y_attn + jax.nn.sigmoid(gb) * y_conv
        h = h + mixed @ w_out[i]
        f = rmsnorm(h, norm_ffn_g[i])
        h = h + (jax.nn.silu(f @ w_gate[i]) * (f @ w_up[i])) @ w_down[i]
    out = rmsnorm(h, norm_final_g)
    return out[:, N_META:]


CHUNK = 64
MIX = D_MODEL
W_LRU = MIX // 2
LRU_BLOCKS = 8
LRU_BW = W_LRU // LRU_BLOCKS
LRU_C = 8.0
CONV_A = 4
SB_HEADS = 4
SB_DH = MIX // 4 // SB_HEADS
SB_W = SB_HEADS * SB_DH
DF_HEADS = 4
DF_DV = MIX // 4 // DF_HEADS
DF_DQK = DF_DV // 2
DF_W = DF_HEADS * DF_DV
D_FF_2 = ((8 * D_MODEL // 3 + 255) // 256) * 256
CONV_FF = 3
IN_SIZES = [W_LRU, W_LRU, SB_W, SB_W, SB_W, DF_W, DF_W, DF_W]
P_IN = sum(IN_SIZES)


def rmsnorm_2(x, g):
    xf = x.astype(jnp.float32)
    y = xf * lax.rsqrt(jnp.mean(xf * xf, axis=-1, keepdims=True) + EPS)
    return (y * g.astype(jnp.float32)).astype(x.dtype)

def causal_dwconv(x, w, b):
    k = w.shape[0]
    y = lax.conv_general_dilated(
        x, w[:, None, :], window_strides=(1,), padding=[(k - 1, 0)],
        dimension_numbers=('NWC', 'WIO', 'NWC'), feature_group_count=x.shape[-1])
    return y + b

def rg_lru(xa, w_r, b_r, w_i, b_i, lam):
    bn, s, c = xa.shape
    xb = xa.reshape(bn, s, LRU_BLOCKS, LRU_BW)
    r = jax.nn.sigmoid((jnp.einsum('bsnc,ncd->bsnd', xb, w_r).reshape(bn, s, c) + b_r).astype(jnp.float32))
    i = jax.nn.sigmoid((jnp.einsum('bsnc,ncd->bsnd', xb, w_i).reshape(bn, s, c) + b_i).astype(jnp.float32))
    log_a = -LRU_C * r * jax.nn.softplus(-lam.astype(jnp.float32))
    a = jnp.exp(log_a)
    u = jnp.sqrt(-jnp.expm1(2.0 * log_a)) * (i * xa.astype(jnp.float32))

    def combine(left, right):
        a1, b1 = left
        a2, b2 = right
        return a1 * a2, a2 * b1 + b2

    _, h = lax.associative_scan(combine, (a, u), axis=1)
    return h.astype(xa.dtype)

def to_heads(t, n_heads):
    bn, s, w = t.shape
    return t.reshape(bn, s, n_heads, w // n_heads).transpose(0, 2, 1, 3)

def from_blocks(o):
    nb, bn, h, qb, dh = o.shape
    return o.transpose(1, 0, 3, 2, 4).reshape(bn, nb * qb, h, dh)

def stick_breaking(q, k, v):
    s_len = q.shape[2]
    scale = SB_DH ** -0.5
    spos = jnp.arange(s_len)

    def block(start):
        qb = lax.dynamic_slice_in_dim(q, start, Q_BLOCK, axis=2)
        tpos = start + jnp.arange(Q_BLOCK)
        earlier = spos[None, :] < tpos[:, None]
        z = jnp.einsum('bhqd,bhkd->bhqk', qb, k).astype(jnp.float32) * scale
        log_1m = jnp.where(earlier, jax.nn.log_sigmoid(-z), 0.0)
        tail = lax.cumsum(log_1m, axis=3, reverse=True) - log_1m
        wts = jnp.where(earlier, jnp.exp(jax.nn.log_sigmoid(z) + tail), 0.0)
        return jnp.einsum('bhqk,bhkd->bhqd', wts.astype(v.dtype), v)

    starts = jnp.arange(s_len // Q_BLOCK, dtype=jnp.int32) * Q_BLOCK
    o = from_blocks(lax.map(block, starts))
    return o.reshape(o.shape[0], s_len, SB_W)

def diff_attention(q, k, v, lam, lam_init, g_sub):
    s_len = q.shape[2]
    scale = DF_DQK ** -0.5
    q1, q2 = q[..., :DF_DQK], q[..., DF_DQK:]
    k1, k2 = k[..., :DF_DQK], k[..., DF_DQK:]
    slopes = 2.0 ** (-8.0 * (jnp.arange(DF_HEADS, dtype=jnp.float32) + 1.0) / DF_HEADS)
    spos = jnp.arange(s_len)

    def block(start):
        qb1 = lax.dynamic_slice_in_dim(q1, start, Q_BLOCK, axis=2)
        qb2 = lax.dynamic_slice_in_dim(q2, start, Q_BLOCK, axis=2)
        tpos = start + jnp.arange(Q_BLOCK)
        allowed = (spos[None, :] // CHUNK) <= (tpos[:, None] // CHUNK)
        dist = jnp.abs(tpos[:, None] - spos[None, :]).astype(jnp.float32)
        bias = -slopes[:, None, None] * dist

        def probs(qb, kk):
            sc = jnp.einsum('bhqd,bhkd->bhqk', qb, kk).astype(jnp.float32) * scale + bias
            return jax.nn.softmax(jnp.where(allowed, sc, -jnp.inf), axis=-1)

        p = probs(qb1, k1) - lam * probs(qb2, k2)
        return jnp.einsum('bhqk,bhkd->bhqd', p.astype(v.dtype), v)

    starts = jnp.arange(s_len // Q_BLOCK, dtype=jnp.int32) * Q_BLOCK
    o = from_blocks(lax.map(block, starts))
    o = rmsnorm_2(o, g_sub) * (1.0 - lam_init)
    return o.reshape(o.shape[0], s_len, DF_W)

def second_inputs(seed: int = 0) -> dict:
    key = jax.random.key(seed)
    ks = jax.random.split(key, 24)
    f32 = jnp.float32

    def nrm(k, shape, fan_in):
        return jax.random.normal(k, shape, f32) * (fan_in ** -0.5)

    def gain(k, shape):
        return 1.0 + 0.02 * jax.random.normal(k, shape, f32)

    def small(k, shape):
        return 0.01 * jax.random.normal(k, shape, f32)

    a_c = jax.random.uniform(ks[8], (DEPTH, W_LRU), f32, minval=0.9, maxval=0.999)
    a_base = a_c ** (1.0 / LRU_C)
    return {
        'x': jax.random.normal(ks[0], (BATCH, SEQ, D_MODEL), f32),
        'norm1_g': gain(ks[1], (DEPTH, D_MODEL)),
        'w_in': nrm(ks[2], (DEPTH, D_MODEL, P_IN), D_MODEL),
        'conv_a_w': nrm(ks[3], (DEPTH, CONV_A, W_LRU), CONV_A),
        'conv_a_b': small(ks[4], (DEPTH, W_LRU)),
        'w_rgate': nrm(ks[5], (DEPTH, LRU_BLOCKS, LRU_BW, LRU_BW), LRU_BW),
        'b_rgate': small(ks[6], (DEPTH, W_LRU)),
        'w_igate': nrm(ks[7], (DEPTH, LRU_BLOCKS, LRU_BW, LRU_BW), LRU_BW),
        'b_igate': small(ks[9], (DEPTH, W_LRU)),
        'lru_lambda': jnp.log(a_base) - jnp.log1p(-a_base),
        'lam_q1': 0.1 * jax.random.normal(ks[10], (DEPTH, DF_DQK), f32),
        'lam_k1': 0.1 * jax.random.normal(ks[11], (DEPTH, DF_DQK), f32),
        'lam_q2': 0.1 * jax.random.normal(ks[12], (DEPTH, DF_DQK), f32),
        'lam_k2': 0.1 * jax.random.normal(ks[13], (DEPTH, DF_DQK), f32),
        'subln_g': gain(ks[14], (DEPTH, DF_DV)),
        'w_out': nrm(ks[15], (DEPTH, MIX, D_MODEL), MIX),
        'norm2_g': gain(ks[16], (DEPTH, D_MODEL)),
        'w_ff_up': nrm(ks[17], (DEPTH, D_MODEL, 2 * D_FF_2), D_MODEL),
        'conv_ff_w': nrm(ks[18], (DEPTH, CONV_FF, 2 * D_FF_2), CONV_FF),
        'conv_ff_b': small(ks[19], (DEPTH, 2 * D_FF_2)),
        'w_ff_down': nrm(ks[20], (DEPTH, D_FF_2, D_MODEL), D_FF_2),
        'final_g': gain(ks[21], (D_MODEL,)),
    }

def second_block(x, norm1_g, w_in, conv_a_w, conv_a_b, w_rgate, b_rgate, w_igate, b_igate,
              lru_lambda, lam_q1, lam_k1, lam_q2, lam_k2, subln_g, w_out, norm2_g,
              w_ff_up, conv_ff_w, conv_ff_b, w_ff_down, final_g):
    split_at = np.cumsum(IN_SIZES)[:-1].tolist()
    for l in range(DEPTH):
        h = rmsnorm_2(x, norm1_g[l])
        proj = h @ w_in[l]
        xa, ya, sq, sk, sv, dq, dk, dv = jnp.split(proj, split_at, axis=-1)

        xa = causal_dwconv(xa, conv_a_w[l], conv_a_b[l])
        out_a = rg_lru(xa, w_rgate[l], b_rgate[l], w_igate[l], b_igate[l], lru_lambda[l]) * jax.nn.gelu(ya)

        out_b = stick_breaking(to_heads(sq, SB_HEADS), to_heads(sk, SB_HEADS), to_heads(sv, SB_HEADS))

        lam_init = 0.8 - 0.6 * float(np.exp(-0.3 * l))
        lam = (jnp.exp(jnp.sum(lam_q1[l] * lam_k1[l]).astype(jnp.float32))
               - jnp.exp(jnp.sum(lam_q2[l] * lam_k2[l]).astype(jnp.float32)) + lam_init)
        out_c = diff_attention(to_heads(dq, DF_HEADS), to_heads(dk, DF_HEADS), to_heads(dv, DF_HEADS),
                               lam, lam_init, subln_g[l])

        mixed = jnp.concatenate([out_a, out_b.astype(out_a.dtype), out_c.astype(out_a.dtype)], axis=-1)
        x = x + mixed @ w_out[l]

        h2 = rmsnorm_2(x, norm2_g[l])
        u = causal_dwconv(h2 @ w_ff_up[l], conv_ff_w[l], conv_ff_b[l])
        gate, val = jnp.split(u, 2, axis=-1)
        x = x + (jax.nn.silu(gate) * val) @ w_ff_down[l]
    return rmsnorm_2(x, final_g)


def setup_inputs(seed=0):
    out = dict(first_inputs(seed))
    for name, value in second_inputs(seed + 1).items():
        if name != "x":
            out[name + "_2"] = value
    return out


def reference(
    x, meta_tokens, norm_mix_g, w_in, w_attn_out, conv_w, w_conv_out, w_out, norm_ffn_g, w_gate,
    w_up, w_down, norm_final_g, norm1_g_2, w_in_2, conv_a_w_2, conv_a_b_2, w_rgate_2, b_rgate_2,
    w_igate_2, b_igate_2, lru_lambda_2, lam_q1_2, lam_k1_2, lam_q2_2, lam_k2_2, subln_g_2,
    w_out_2, norm2_g_2, w_ff_up_2, conv_ff_w_2, conv_ff_b_2, w_ff_down_2, final_g_2,
):
    x = first_block(
        x, meta_tokens, norm_mix_g, w_in, w_attn_out, conv_w, w_conv_out, w_out, norm_ffn_g,
        w_gate, w_up, w_down, norm_final_g,
    )
    return second_block(
        x, norm1_g_2, w_in_2, conv_a_w_2, conv_a_b_2, w_rgate_2, b_rgate_2, w_igate_2,
        b_igate_2, lru_lambda_2, lam_q1_2, lam_k1_2, lam_q2_2, lam_k2_2, subln_g_2, w_out_2,
        norm2_g_2, w_ff_up_2, conv_ff_w_2, conv_ff_b_2, w_ff_down_2, final_g_2,
    )


_drawn_inputs = setup_inputs


def setup_inputs(seed=0):
    import zlib

    import numpy as np

    out = dict(_drawn_inputs(seed))
    spreads = {}
    factors = {'norm_ffn_g': 3.501,
     'norm1_g_2': 3.212,
     'conv_a_b_2': 8.476,
     'b_rgate_2': 35.903,
     'b_igate_2': 33.338,
     'lam_k1_2': 8.0,
     'subln_g_2': 28.665,
     'norm2_g_2': 11.413,
     'conv_ff_b_2': 23.593,
     'final_g_2': 22.953}
    for name, (base, spread) in spreads.items():
        noise = np.random.default_rng([zlib.crc32(name.encode()), seed]).standard_normal(out[name].shape)
        drawn = base * np.exp(spread * noise) if base else spread * noise
        out[name] = __import__('jax').numpy.asarray(drawn.astype(out[name].dtype))
    for name, factor in factors.items():
        out[name] = (out[name] * factor).astype(out[name].dtype)
    return out
```

```python
from contextlib import ExitStack

import numpy as np
import concourse.bass as bass
from concourse import mybir

F32 = mybir.dt.float32
F32R = mybir.dt.float32r
I32 = mybir.dt.int32
ALU = mybir.AluOpType
ACT = mybir.ActivationFunctionType
AX = mybir.AxisListType

P = 128
D = 1024
KC = D // P
T = 512
META = 16
N = T + META
HALF = N // 2
BANK = 512
QB = T // P
HEADS = 8
IDX_HEADS, IDX_DIM = 8, 64
TOPK = min(256, N // 4)
PADS = -TOPK % 8
ROUNDS = (TOPK + PADS) // 8
IDX_SCALE = (IDX_HEADS ** -0.5) * (IDX_DIM ** -0.5)
ATT_SCALE = P ** -0.5
EPS = 1e-6
FF = 2816
FFC = FF // P
GROUPS = [(0, 8), (8, 8), (16, 6)]
DF_SCALE = 32 ** -0.5
SB_SCALE = 64 ** -0.5
LAM_INIT = 0.8 - 0.6 * float(np.exp(-0.3 * 0))
SLOPES = [2.0 ** (-8.0 * (h + 1) / 4) for h in range(4)]
GELU_C = float(np.sqrt(2.0 / np.pi))
HIDDEN = -1e30
TAKEN = -3e38
SENTINEL = 3e38

C_Q, C_K, C_V, C_QI, C_KI, C_CU, C_CB, C_CC, C_GA, C_GB = 0, 1024, 2048, 3072, 3584, 3656, 4680, 5704, 6728, 7752

STAGES = [("ki", 1, "act"), ("qi", 4, "act"), ("q", 8, "act"), ("k", 8, "act"), ("v", 8, "act"),
          ("cu", 8, "act"), ("cc", 8, "dve"), ("gates", 24, "both"), ("co", 8, "dve"), ("ao", 8, "dve"), ("wo", 8, "dve"),
          ("gu0", 16, "dve"), ("dn0", 8, "dve"), ("gu1", 16, "dve"), ("dn1", 8, "dve"), ("gu2", 12, "dve"), ("dn2", 8, "dve"),
          ("xa", 4, "act"), ("ya", 4, "act"), ("sqk", 4, "act"), ("dqk", 4, "act"), ("sv", 2, "act"), ("dv", 2, "act"),
          ("wo2", 8, "dve"),
          ("gv0", 16, "dve"), ("ed0", 8, "dve"), ("gv1", 16, "dve"), ("ed1", 8, "dve"), ("gv2", 12, "dve"), ("ed2", 8, "dve")]
FIRST, COUNT, OWNER, LETGO = {}, {}, {}, {}
CREDIT = 2
_p, _n = 0, {"act": CREDIT, "dve": CREDIT}
for _name, _count, _owner in STAGES:
    FIRST[_name], COUNT[_name], OWNER[_name] = _p, _count, _owner
    LETGO[_name] = dict(_n)
    if _owner == "both":
        _n["dve"] += _count // 3
        _n["act"] += _count * 2 // 3
    else:
        _n[_owner] += _count
    _p += _count
PANELS = _p
ORDER = [s[0] for s in STAGES]
RAW_SLOTS, W_SLOTS = 4, 2

EXT = [META + P * (b + 1) for b in range(QB)]
SBW = [T - P * i for i in range(QB)]
SBO = [sum(SBW[:i]) for i in range(QB)]
SBT = sum(SBW)
SB_BANKS = [(0, SBO[0], SBW[0]), (1, SBO[1], SBW[1]), (2, SBO[2], SBW[2] + SBW[3])]

V_MIX, V_CW, V_FFN, V_FIN, V_N1, V_CAW, V_CAB, V_BR, V_BI, V_LAM, V_N2, V_FIN2, V_ROWS = 0, 8, 32, 40, 48, 56, 72, 76, 80, 84, 88, 96, 104


def two_blocks(nc, x, meta_tokens, norm_mix_g, w_in, w_attn_out, conv_w, w_conv_out, w_out, norm_ffn_g, w_gate,
               w_up, w_down, norm_final_g, norm1_g, w_in_2, conv_a_w, conv_a_b, w_rgate, b_rgate,
               w_igate, b_igate, lru_lambda, lam_q1, lam_k1, lam_q2, lam_k2, subln_g,
               w_out_2, norm2_g, w_ff_up, conv_ff_w, conv_ff_b, w_ff_down, final_g, out):
    with ExitStack() as ctx:
        def sem(name):
            return ctx.enter_context(nc.semaphore(name))

        top = [(nc.sbuf_base + 63) // 64 * 64]

        def region(nbytes):
            at = top[0]
            top[0] += (nbytes + 31) // 32 * 32
            return [at, top[0]]

        def place(reg, name, shape, dt=F32):
            nbytes = int(np.prod(shape[1:])) * 4
            t = nc.alloc_sbuf_tensor_at(name, shape, dt, offset=reg[0])
            reg[0] += (nbytes + 31) // 32 * 32
            assert reg[0] <= reg[1], (name, reg)
            return t

        def again(reg, start):
            return [start, reg[1]]

        def solo(name, shape, dt=F32):
            return place(region(int(np.prod(shape[1:])) * 4), name, shape, dt)

        r_weights = region(4 * (RAW_SLOTS + 2 * W_SLOTS) * KC * P)
        RAW = place(r_weights, "RAW", [P, RAW_SLOTS, KC, P])
        WH = place(r_weights, "WH", [P, W_SLOTS, KC, P], F32R)
        WL = place(r_weights, "WL", [P, W_SLOTS, KC, P], F32R)
        ident = solo("ident", [P, P])
        ones = solo("ones", [P, P])
        tri = solo("tri", [P, P])
        before = solo("before", [P, P])
        hide = solo("hide", [P, P])
        VEC = solo("VEC", [P, 3, P])
        eps_t = solo("eps_t", [P, 1])
        WQ = solo("WQ", [P, QB, IDX_HEADS])
        MX8 = solo("MX8", [P, 8])
        NMX = solo("NMX", [P, 2])
        RS = solo("RS", [P, 2])
        RINV = solo("RINV", [P, 4])
        small = solo("small", [P, 128])
        DIST = solo("DIST", [P, T])
        GSUB = solo("GSUB", [P, 64])
        LAMV = solo("LAMV", [P, 4, 32])

        r_a = region(2 * 4 * KC * N)
        a0 = r_a[0]
        AH = place(r_a, "AH", [P, KC, N], F32R)
        AL = place(r_a, "AL", [P, KC, N], F32R)
        ra2 = again(r_a, a0)
        Z = place(ra2, "Z", [P, 2, SBT])
        LN = place(ra2, "LN", [P, SBT])
        LG = place(ra2, "LG", [P, SBT])
        L1 = place(ra2, "L1", [P, 2, T])
        L2 = place(ra2, "L2", [P, 2, T])
        PT2 = place(ra2, "PT2", [P, 2, T])

        r_b = region(4 * (HEADS * N + 5 * D))
        b0 = r_b[0]
        KT = place(r_b, "KT", [P, HEADS, N])
        V = place(r_b, "V", [P, 5, D])
        rb2 = again(r_b, b0)
        XR = place(rb2, "XR", [P, QB, D])
        XM = place(rb2, "XM", [META, D])
        VR = place(rb2, "VR", [P, 3, P])
        rb3 = again(r_b, b0)
        BH = place(rb3, "BH", [P, KC, T], F32R)
        BL = place(rb3, "BL", [P, KC, T], F32R)
        half_b = 4 * (KC // 2) * T
        RP = place(again(r_b, b0 + half_b), "RP", [P, 4, T])
        IP = place(again(r_b, b0 + 2 * half_b), "IP", [P, 4, T])
        TH = place(again(r_b, b0 + 3 * half_b), "TH", [P, 4, T])
        rb4 = again(r_b, b0)
        OUT = place(rb4, "OUT", [P, QB, D])

        r_q = region(4 * KC * T + 64)
        q0 = r_q[0]
        QT = place(r_q, "QT", [P, HEADS, T])
        rq2 = again(r_q, q0)
        XA = place(rq2, "XA", [P, 4, T + 3])
        YA = place(rq2, "YA", [P, 4, T])

        r_x = region(4 * KC * N)
        x0 = r_x[0]
        H0 = place(r_x, "H0", [P, KC, N])
        rx2 = again(r_x, x0)
        GB = place(rx2, "GB", [P, KC, T])
        rx3 = again(r_x, x0)
        SQK = place(rx3, "SQK", [P, 4, T])
        DQK = place(rx3, "DQK", [P, 4, T])

        r_u = region(4 * KC * N)
        u0 = r_u[0]
        U = place(r_u, "U", [P, KC, N])
        ru2 = again(r_u, u0)
        H = place(ru2, "H", [P, KC, T])

        r_g = region(4 * KC * T)
        g0 = r_g[0]
        GA = place(r_g, "GA", [P, KC, T])
        rg2 = again(r_g, g0)
        QI = place(rg2, "QI", [P, 4, T])
        KI = place(rg2, "KI", [P, N])
        WIT = place(rg2, "WIT", [P, N])
        rg3 = again(r_g, g0)
        V2 = place(rg3, "V2", [P, QB, 512])
        GY = place(rg3, "GY", [P, 4, T])

        r_s = region(4 * QB * (PADS + N))
        s0 = r_s[0]
        S = place(r_s, "S", [P, QB, PADS + N])
        rs2 = again(r_s, s0)
        BIAS = place(rs2, "BIAS", [P, T])
        WR = place(rs2, "WR", [P, 2, 4, P])

        r_t = region(4 * (4 * N + 2 * T + 5 * P * 2 + 2 * P * 2))
        t0 = r_t[0]
        SQ = place(r_t, "SQ", [P, 2, N])
        TN = place(r_t, "TN", [P, 2, N])
        RT = place(r_t, "RT", [P, N])
        RSTD = place(r_t, "RSTD", [P, N])
        rt2 = again(r_t, t0)
        RL = place(rt2, "RL", [P, 2, N])
        VTT = place(rt2, "VTT", [P, 2, N])
        rt3 = again(r_t, t0)
        LT = place(rt3, "LT", [P, 2, N])
        CT = place(rt3, "CT", [P, 2, T])
        PT = place(rt3, "PT", [P, 2, 5 * P])
        QS = place(rt3, "QS", [P, 2, P])
        YS = place(rt3, "YS", [P, 2, P])
        rt4 = again(r_t, t0)
        SG = place(rt4, "SG", [P, 2, T])
        T1 = place(rt4, "T1", [P, 4, T])
        T2 = place(rt4, "T2", [P, 2, T])
        rt5 = again(r_t, t0)
        XC = place(rt5, "XC", [P, 4, T])
        OC = place(rt5, "OC", [P, QB, 256])
        OSQ = place(rt5, "OSQ", [P, QB, 256])
        rt8 = again(r_t, t0)
        DISTI = place(rt8, "DISTI", [P, T], I32)
        assert top[0] <= nc.sbuf_usable_end, top

        PJ = ctx.enter_context(nc.psum_tensor("PJ", [P, 2, 2, BANK], F32))
        PX = ctx.enter_context(nc.psum_tensor("PX", [P, 2, BANK], F32))
        PB6 = ctx.enter_context(nc.psum_tensor("PB6", [P, BANK], F32))
        PB7 = ctx.enter_context(nc.psum_tensor("PB7", [P, BANK], F32))
        TURNED_Y, TAIL_P = PJ[:, 0, 1, :], PJ[:, 1, 1, :]
        SB_BANK = [PJ[:, 0, 0, :], PJ[:, 0, 1, :], PJ[:, 1, 0, :]]
        SB_OUT = PJ[:, 1, 1, :]
        PX_flat = PX[:, :, :].rearrange("p a n -> p (a n)")

        h_scratch = nc.dram_tensor("h_scratch", (P, KC, T), F32).ap()

        raw_loaded = [sem(f"raw_loaded{i}") for i in range(RAW_SLOTS)]
        w_hi = sem("w_hi")
        w_ready = sem("w_ready")
        pool_seen = sem("pool_seen")
        dve_seen, act_seen = sem("dve_seen"), sem("act_seen")
        panel_done = sem("panel_done")
        freed = {"act": sem("freed_act"), "dve": sem("freed_dve")}
        consts_ready = sem("consts_ready")
        const_step = sem("const_step")
        x_loaded, meta_loaded, vec_loaded = sem("x_loaded"), sem("meta_loaded"), sem("vec_loaded")
        xt_done, h0_ready = sem("xt_done"), sem("h0_ready")
        vec_done, vec_ready = sem("vec_done"), sem("vec_ready")
        NORMS = ["mix", "ffn", "fin", "n1", "n2", "fin2"]
        sq_ready = {n: sem(f"sq_ready_{n}") for n in NORMS}
        ms_added = {n: sem(f"ms_added_{n}") for n in NORMS}
        rt_ready = {n: sem(f"rt_ready_{n}") for n in NORMS}
        rstd_ready = {n: sem(f"rstd_ready_{n}") for n in NORMS}
        normed = {n: sem(f"normed_{n}") for n in NORMS}
        a_hi, a_lo = sem("a_hi"), sem("a_lo")
        b_hi, b_lo = sem("b_hi"), sem("b_lo")
        h_stored, h_loaded = sem("h_stored"), sem("h_loaded")
        ki_ready, ki_twin = sem("ki_ready"), sem("ki_twin")
        wq_done, wq_ready = sem("wq_done"), sem("wq_ready")
        idx_done, relu_done, score_step = sem("idx_done"), sem("relu_done"), sem("score_step")
        topk_step, mask_ready = sem("topk_step"), sem("mask_ready")
        v_turned, v_ready = sem("v_turned"), sem("v_ready")
        u_ready, conv_step = sem("u_ready"), sem("conv_step")
        qs_ready, qk_done, logits_ready, max_ready = sem("qs_ready"), sem("qk_done"), sem("logits_ready"), sem("max_ready")
        exp_done, rinv_ready, p_turned, pt_ready = sem("exp_done"), sem("rinv_ready"), sem("p_turned"), sem("pt_ready")
        pv_done, ys_ready, y_turned, y_ready = sem("pv_done"), sem("ys_ready"), sem("y_turned"), sem("y_ready")
        mixed_ready = sem("mixed_ready")
        tanh_ready, ff_step, conv_base = sem("tanh_ready"), sem("ff_step"), sem("conv_base")
        small_loaded, wr_cleared = sem("small_loaded"), sem("wr_cleared")
        act_step, dve_step = sem("act_step"), sem("dve_step")
        cl_ready, lam_e, lam_ready, gate_half = sem("cl_ready"), sem("lam_e"), sem("lam_ready"), sem("gate_half")
        lam_sum, cl_exp = sem("lam_sum"), sem("cl_exp")
        xa_ready, xc_ready, rg_done, rg_tanh = sem("xa_ready"), sem("xc_ready"), sem("rg_done"), sem("rg_tanh")
        lru_a, lru_q, lru_root = sem("lru_a"), sem("lru_q"), sem("lru_root")
        gelu_in, gelu_t = sem("gelu_in"), sem("gelu_t")
        outa_ready = sem("outa_ready")
        z_done, z_ready, sb_ln, sb_log, tail_done, sb_sum, sb_w, sb_masked, sb_pv = (
            sem(n) for n in ("z_done", "z_ready", "sb_ln", "sb_log", "tail_done", "sb_sum", "sb_w", "sb_masked", "sb_pv"))
        bias_step, df_qk, df_max, df_exp, df_p, df_turned, df_pt, df_pv, df_o = (
            sem(n) for n in ("bias_step", "df_qk", "df_max", "df_exp", "df_p", "df_turned", "df_pt", "df_pv", "df_o"))
        df_lt, df_r = sem("df_lt"), sem("df_r")
        oc_sq, oc_root, oc_ready, oc_turned = sem("oc_sq"), sem("oc_root"), sem("oc_ready"), sem("oc_turned")
        out_turned, out_ready, stored = sem("out_turned"), sem("out_ready"), sem("stored")

        block = ctx.enter_context(nc.Block())

        def pick(t, i):
            return t[:, bass.ds(i, 1)].rearrange("p o n -> p (o n)")

        def cols(ap, w):
            return ap.rearrange("p (a n) -> p a n", a=2) if w == N else ap

        A_USE = {n: KC * i for i, n in enumerate(["mix", "conv", "mixed", "ffn", "n1", "n2"])}
        M2_PIECES = 1 + 4 + 2
        B_USE, _b = {}, 0
        for _n_, _c in [("y", 8), ("act0", 8), ("act1", 8), ("act2", 6), ("m2", M2_PIECES), ("ff0", 8), ("ff1", 8), ("ff2", 6)]:
            B_USE[_n_] = _b
            _b += _c
        @block.sync
        def _(sp):
            sp.dma_start(XR[:], x[0].rearrange("(t p) d -> p t d", p=P)).then_inc(x_loaded, 16)
            sp.dma_start(XM[:], meta_tokens).then_inc(meta_loaded, 16)

            def load(slot, src, free):
                if free is not None:
                    sp.wait_ge(w_ready, free)
                k = src.shape[0] // P
                sp.dma_start(RAW[:, slot, 0:k], src.rearrange("(k p) c -> p k c", p=P)).then_inc(raw_loaded[slot], 16)

            def run(first, blocks, src):
                with sp.Fori(0, blocks) as i:
                    for j in range(RAW_SLOTS):
                        load((first + j) % RAW_SLOTS, src(i, j), first - RAW_SLOTS + 1 + j + i * RAW_SLOTS)

            def columns(w, c0):
                return lambda i, j: w[:, bass.ds(i * (4 * P) + (c0 + j * P), P)]

            def pairs(wa, ca, wb, cb):
                return lambda i, j: (wa if j % 2 == 0 else wb)[:, bass.ds(i * (2 * P) + ((ca if j % 2 == 0 else cb) + j // 2 * P), P)]

            def gate_up(name, wa, ca, wb, cb, g):
                c0, n = GROUPS[g]
                run(FIRST[name], n // 2, pairs(wa, ca + c0 * P, wb, cb + c0 * P))

            def down(name, w, g):
                c0, n = GROUPS[g]
                run(FIRST[name], 2, columns(w[c0 * P:(c0 + n) * P], 0))

            w1, w2 = w_in[0], w_in_2[0]
            load(0, w1[:, C_KI:C_KI + P], None)
            for p in range(1, 5):
                load(p % RAW_SLOTS, w1[:, C_QI + (p - 1) * P:C_QI + p * P], p - RAW_SLOTS + 1 if p >= RAW_SLOTS else None)
            for name, c0 in (("q", C_Q), ("k", C_K), ("v", C_V), ("cu", C_CU), ("cc", C_CC)):
                run(FIRST[name], 2, columns(w1, c0))
            with sp.Fori(0, 2) as i:
                for j in range(12):
                    c0 = (C_CB, C_GA, C_GB)[j % 3]
                    load((FIRST["gates"] + j) % RAW_SLOTS, w1[:, bass.ds(i * (4 * P) + (c0 + j // 3 * P), P)],
                         FIRST["gates"] + j - RAW_SLOTS + 1 + i * 12)
            for name, w in (("co", w_conv_out), ("ao", w_attn_out), ("wo", w_out)):
                run(FIRST[name], 2, columns(w[0], 0))
                if name == "co":
                    sp.wait_ge(h_stored, 16)
                    sp.wait_ge(a_lo, A_USE["conv"] + KC)
                    sp.dma_start(H[:], h_scratch).then_inc(h_loaded, 16)
            for g in range(3):
                gate_up(f"gu{g}", w_gate[0], 0, w_up[0], 0, g)
                down(f"dn{g}", w_down[0], g)
            run(FIRST["xa"], 2, columns(w2, 0))
            run(FIRST["sqk"], 1, columns(w2, 1024))
            run(FIRST["dqk"], 1, columns(w2, 1792))
            for j in range(4):
                p = FIRST["sv"] + j
                c0 = (1536, 1664, 2304, 2432)[j]
                load(p % RAW_SLOTS, w2[:, c0:c0 + P], p - RAW_SLOTS + 1)
            run(FIRST["wo2"], 2, columns(w_out_2[0], 0))
            for g in range(3):
                gate_up(f"gv{g}", w_ff_up[0], 0, w_ff_up[0], FF, g)
                down(f"ed{g}", w_ff_down[0], g)
            for b in range(QB):
                sp.wait_ge(out_ready, b + 1)
                sp.dma_start(out[0, b * P:(b + 1) * P, :], OUT[:, b]).then_inc(stored, 16)
            sp.wait_ge(stored, 16 * QB)

        @block.gpsimd
        def _(pool):
            pool.memset(ident[:], 0.0).then_inc(const_step, 1)
            pool.memset(ones[:], 1.0).then_inc(const_step, 1)
            pool.memset(hide[:], 0.0).then_inc(const_step, 1)
            pool.memset(eps_t[:], EPS).then_inc(const_step, 1)
            pool.wait_ge(const_step, 4)
            pool.iota(DISTI[:], [[-1, T]], base=T - P, channel_multiplier=1).then_inc(consts_ready, 1)
            pool.affine_select(out=ident[:], in_=ident[:], compare_op=ALU.not_equal, fill=1.0, base=0,
                               pattern=[[-1, P]], channel_multiplier=1).then_inc(consts_ready, 1)
            pool.affine_select(out=tri[:], in_=ones[:], compare_op=ALU.is_ge, fill=0.0, base=0,
                               pattern=[[-1, P]], channel_multiplier=1).then_inc(consts_ready, 1)
            pool.affine_select(out=before[:], in_=ones[:], compare_op=ALU.is_gt, fill=0.0, base=0,
                               pattern=[[1, P]], channel_multiplier=-1).then_inc(consts_ready, 1)
            pool.affine_select(out=hide[:], in_=hide[:], compare_op=ALU.is_ge, fill=HIDDEN, base=0,
                               pattern=[[-1, P]], channel_multiplier=1).then_inc(consts_ready, 1)

            def split(slot, w, loaded, used, p):
                pool.wait_ge(raw_loaded[slot], loaded)
                if used is not None:
                    pool.wait_ge(panel_done, used)
                pool.sem_inc(pool_seen, 1)
                nc.gpsimd.tensor_scalar(WH[:, w], RAW[:, slot], 1.0, 1.0, ALU.mult, ALU.mult).then_inc(w_hi, 1)
                pool.wait_ge(w_hi, p + 1)
                nc.gpsimd.tensor_tensor(WL[:, w], RAW[:, slot], WH[:, w].bitcast(F32), ALU.subtract).then_inc(w_ready, 1)

            PEEL = 5
            for p in range(PEEL):
                split(p % RAW_SLOTS, p % W_SLOTS, 16 * (p // RAW_SLOTS + 1), p - 1 if p >= 2 else None, p)
            with pool.Fori(0, (PANELS - PEEL) // RAW_SLOTS) as i:
                for j in range(RAW_SLOTS):
                    p = PEEL + j
                    split(p % RAW_SLOTS, p % W_SLOTS, i * 16 + 16 * (p // RAW_SLOTS + 1), i * RAW_SLOTS + (p - 1), i * RAW_SLOTS + p)

        @block.tensor
        def _(pe):
            mm = nc.tensor.matmul

            def slot_of(name, i):
                return (FIRST[name] + i) % 2

            def panel(name, i, at, rhs, ready, wide=False, rows=P, kc=KC, half=None, turned=False, owner=None):
                s = slot_of(name, i)
                rh, rl = rhs
                if half in (None, 0):
                    pe.wait_ge(w_ready, at + (FIRST[name] + 1))
                    who = owner or OWNER[name]
                    if owner is None:
                        pe.wait_ge(freed[who], at + (LETGO[name][who] - 1))
                parts = [(WH, rh), (WH, rl), (WL, rh)]
                last = None
                ks = range(kc) if half is None else range(half * kc // 2, (half + 1) * kc // 2)
                for k in ks:
                    pe.wait_ge(ready[0], ready[1] + k + 1)
                    for n, (w, a) in enumerate(parts):
                        st, sp_ = k == 0 and n == 0, k == kc - 1 and n == 2
                        if turned:
                            for t in range(QB):
                                last = mm(PJ[:, s, 0, t * P:(t + 1) * P], a[:, k, t * P:(t + 1) * P], w[:, s, k, :],
                                          start=st and t == 0, stop=sp_, skip_group_check=True)
                        elif wide:
                            for h in range(2):
                                last = mm(PJ[0:rows, s, h, 0:HALF], w[:, s, k, 0:rows], a[:, k, h * HALF:(h + 1) * HALF], start=st, stop=sp_)
                        else:
                            last = mm(PJ[0:rows, s, 0, 0:T], w[:, s, k, 0:rows], a[:, k, :], start=st, stop=sp_)
                if half in (None, 1):
                    last.then_inc(panel_done, 1)

            def enter(name):
                prev = ORDER[ORDER.index(name) - 1]
                if OWNER[prev] != OWNER[name]:
                    for who in ("act", "dve"):
                        pe.wait_ge(freed[who], LETGO[name][who])

            def stage(name, rhs, ready, **kw):
                enter(name)
                with pe.Fori(0, COUNT[name] // 2) as i:
                    for j in range(2):
                        panel(name, j, i * 2 + j, rhs, ready, **kw)

            def norm(name, width):
                for k in range(KC):
                    pe.wait_ge(sq_ready[name], k + 1)
                    if width == N:
                        mm(PX[:, 0, 0:HALF], ones[:], SQ[:, k % 2, 0:HALF], start=k == 0, stop=k == KC - 1)
                        last = mm(PX[:, 1, 0:HALF], ones[:], SQ[:, k % 2, HALF:N], start=k == 0, stop=k == KC - 1)
                    else:
                        last = mm(PX[:, 0, 0:T], ones[:], SQ[:, k % 2, 0:T], start=k == 0, stop=k == KC - 1)
                    last.then_inc(ms_added[name], 1)

            a_wide = (AH[:, :, :], AL[:, :, :])
            a_x = (AH[:, :, META:N], AL[:, :, META:N])
            a_t = (AH[:, :, 0:T], AL[:, :, 0:T])
            b_t = (BH[:, :, :], BL[:, :, :])

            pe.wait_ge(consts_ready, 5)
            pe.wait_ge(vec_loaded, 16 * 15)
            for t, rows in enumerate((V_ROWS, 88, 88)):
                last = nc.tensor.transpose(PB6[:, t * P:t * P + rows], VR[0:rows, t, :], ident[0:rows, 0:rows])
            last.then_inc(vec_done, 1)
            pe.wait_ge(x_loaded, 16)
            pe.wait_ge(meta_loaded, 16)
            for k in range(KC):
                if k >= 2:
                    pe.wait_ge(h0_ready, k - 1)
                for t in range(QB):
                    nc.tensor.transpose(PJ[:, k % 2, 0, t * P:(t + 1) * P], XR[:, t, k * P:(k + 1) * P], ident[:])
                nc.tensor.transpose(PJ[:, k % 2, 1, 0:META], XM[:, k * P:(k + 1) * P], ident[0:META, 0:META]).then_inc(xt_done, 1)
            norm("mix", N)

            mix = (a_lo, A_USE["mix"])
            panel("ki", 0, 0, a_wide, mix, wide=True, rows=IDX_DIM + IDX_HEADS)
            stage("qi", a_x, mix)
            pe.wait_ge(freed["act"], LETGO["qi"]["act"])
            for b in range(QB):
                last = nc.tensor.transpose(PB6[:, b * 8:b * 8 + 8], WIT[64:72, META + b * P:META + (b + 1) * P], ident[64:72, 64:72])
            last.then_inc(wq_done, 1)
            pe.wait_ge(freed["act"], LETGO["q"]["act"])
            pe.wait_ge(ki_twin, 16)
            for b in range(QB):
                for h in range(IDX_HEADS):
                    n, r = b * IDX_HEADS + h, 64 * (h % 2)
                    if n >= 2:
                        pe.wait_ge(relu_done, n - 1)
                    dst = (PX_flat, PJ[:, 0].rearrange("p a n -> p (a n)"))[n % 2]
                    lhs = QI[r:r + 64, h // 2, b * P:(b + 1) * P]
                    last = mm(dst[:, 0:min(EXT[b], BANK)], lhs, KI[r:r + 64, 0:min(EXT[b], BANK)], start=True, stop=True)
                    if EXT[b] > BANK:
                        last = mm(dst[:, BANK:EXT[b]], lhs, KI[r:r + 64, BANK:EXT[b]], start=True, stop=True)
                    last.then_inc(idx_done, 1)
            pe.wait_ge(relu_done, QB * IDX_HEADS)
            stage("q", a_x, mix)
            stage("k", a_wide, mix, wide=True)
            with pe.Fori(0, 4) as i:
                for j in range(2):
                    panel("v", j, i * 2 + j, a_wide, mix, wide=True)
                for j in range(2):
                    pe.wait_ge(freed["act"], i * 2 + (LETGO["v"]["act"] + j + 1))
                    pe.wait_ge(v_ready, i * 2 + (j + 1))
                    for t in range(4):
                        nc.tensor.transpose(PX[:, 0, t * P:(t + 1) * P], VTT[:, j, t * P:(t + 1) * P], ident[:])
                    nc.tensor.transpose(PX[0:META, 1, 0:P], VTT[:, j, T:N], ident[:]).then_inc(v_turned, 1)
            stage("cu", a_wide, mix, wide=True)
            stage("cc", a_wide, mix, wide=True)

            enter("gates")
            pe.wait_ge(v_ready, HEADS + 1)
            units = [(j, b) for j in range(2) for b in range(QB)]
            NU = len(units)

            def qk(i, u):
                j, b = units[u]
                pe.wait_ge(qs_ready, i * NU + (u + 1))
                pe.wait_ge(logits_ready, i * NU + (u + 1))
                head = KT[:, bass.ds(i * 2 + j, 1), :].rearrange("p o n -> p (o n)")
                last = mm(PX[:, 0, 0:min(EXT[b], BANK)], QS[:, u % 2], head[:, 0:min(EXT[b], BANK)], start=True, stop=True)
                if EXT[b] > BANK:
                    last = mm(PX[:, 1, 0:EXT[b] - BANK], QS[:, u % 2], head[:, BANK:EXT[b]], start=True, stop=True)
                last.then_inc(qk_done, 1)

            def turn_p(i, u):
                j, b = units[u]
                pe.wait_ge(exp_done, i * NU + (u + 1))
                pe.wait_ge(pt_ready, i * NU + (u + 1))
                for t in range(b + 1):
                    nc.tensor.transpose(PB6[:, t * P:(t + 1) * P], LT[:, u % 2, t * P:(t + 1) * P], ident[:])
                nc.tensor.transpose(TAIL_P[0:META, 0:P], LT[:, u % 2, (b + 1) * P:EXT[b]], ident[:]).then_inc(p_turned, 1)

            def pv(i, u):
                j, b = units[u]
                pe.wait_ge(pt_ready, i * NU + (u + 2))
                pe.wait_ge(ys_ready, i * NU + (u + 1))
                for t in range(b + 1):
                    mm(PB7[:, 0:P], PT[:, u % 2, t * P:(t + 1) * P], V[:, t, bass.ds((i * 2 + j) * P, P)], start=t == 0, stop=False)
                mm(PB7[:, 0:P], PT[0:META, u % 2, 4 * P:5 * P], V[0:META, b + 1, bass.ds((i * 2 + j) * P, P)],
                   start=False, stop=True).then_inc(pv_done, 1)

            def turn_y(i, u):
                pe.wait_ge(ys_ready, i * NU + (u + 2))
                pe.wait_ge(y_ready, i * NU + (u + 1))
                nc.tensor.transpose(TURNED_Y[:, 0:P], YS[:, u % 2], ident[:]).then_inc(y_turned, 1)

            with pe.Fori(0, 4) as i:
                for half in range(12):
                    j = half // 2
                    if half % 2 == 0:
                        who = "dve" if j % 3 == 2 else "act"
                        base = LETGO["gates"]
                        if who == "dve":
                            pe.wait_ge(freed["dve"], i * 2 + (base["dve"] + j // 3 + 1))
                        else:
                            pe.wait_ge(freed["act"], i * 4 + (base["act"] + (0, 0, None, 1, 2)[j] - (1 if j == 0 else 0)))
                    panel("gates", j, i * 6 + j, a_x, mix, half=half % 2, owner="here")
                    if half - 3 >= 0 and half - 3 < NU:
                        turn_y(i, half - 3)
                    if half - 2 >= 0 and half - 2 < NU:
                        pv(i, half - 2)
                    if half - 1 >= 0 and half - 1 < NU:
                        turn_p(i, half - 1)
                    if half < NU:
                        qk(i, half)
            stage("co", a_t, (a_lo, A_USE["conv"]))
            stage("ao", b_t, (b_lo, B_USE["y"]))
            stage("wo", a_t, (a_lo, A_USE["mixed"]))
            norm("ffn", T)
            for g, (c0, n) in enumerate(GROUPS):
                stage(f"gu{g}", a_t, (a_lo, A_USE["ffn"]))
                stage(f"dn{g}", b_t, (b_lo, B_USE[f"act{g}"]), kc=n)
            norm("fin", T)
            norm("n1", T)

            n1 = (a_lo, A_USE["n1"])
            stage("xa", a_t, n1)
            stage("ya", a_t, n1)
            pe.wait_ge(small_loaded, 16 * (5 + 4))
            for c in range(4):
                panel("sqk", c, c, a_t, n1)
                pe.wait_ge(xc_ready, c + 1)
                if c >= 1:
                    pe.wait_ge(rg_tanh, 2 * c)
                for g in range(2):
                    mm(PX[:, g, :], WR[:, g, c, :], XC[:, c, :], start=True, stop=True).then_inc(rg_done, 1)
            stage("dqk", a_t, n1)
            for name in ("sv", "dv"):
                for j in range(2):
                    panel(name, j, j, a_t, n1, turned=True)

            def sb_logits(n):
                r, c = 64 * (n % 2), n // 2
                if n >= 1:
                    pe.wait_ge(sb_sum, 3 * n)
                for m, (i0, o, w) in enumerate(SB_BANKS):
                    for i in ((i0,) if m < 2 else (2, 3)):
                        at = SBO[i] - o
                        last = mm(SB_BANK[m][:, at:at + SBW[i]], SQK[r:r + 64, 2 + c, i * P:(i + 1) * P], SQK[r:r + 64, c, i * P:T],
                                  start=i == i0, stop=True, skip_group_check=True)
                    last.then_inc(z_done, 1)

            def sb_tails(n):
                pe.wait_ge(sb_log, n + 1)
                for m, (i0, o, w) in enumerate(SB_BANKS):
                    for i in ((i0,) if m < 2 else (2, 3)):
                        at = SBO[i] - o
                        last = mm(SB_BANK[m][:, at:at + SBW[i]], tri[:], LG[:, SBO[i]:SBO[i] + SBW[i]],
                                  start=i == i0, stop=True, skip_group_check=True)
                        for j in range(i + 1, QB):
                            last = mm(SB_BANK[m][:, at + (j - i) * P:at + SBW[i]], ones[:], LG[:, SBO[j]:SBO[j] + SBW[j]],
                                      start=False, stop=True, skip_group_check=True)
                    last.then_inc(tail_done, 1)

            def sb_out(n):
                r = 64 * (n % 2)
                pe.wait_ge(sb_masked, n + 1)
                if n >= 1:
                    pe.wait_ge(b_lo, B_USE["m2"] + 1 + n)
                for i in range(QB):
                    last = mm(SB_OUT[r:r + 64, i * P:T], V2[:, i, n * 64:(n + 1) * 64], Z[:, n % 2, SBO[i]:SBO[i] + SBW[i]],
                              start=i == 0, stop=True, skip_group_check=True)
                last.then_inc(sb_pv, 1)

            du = [(n, b) for n in range(4) for b in range(QB)]

            def df_scores(u):
                n, b = du[u]
                if u >= 1:
                    pe.wait_ge(df_lt, 2 * u)
                for m in range(2):
                    r = 32 * (2 * (n % 2) + m)
                    mm(PX[:, m, 0:(b + 1) * P], DQK[r:r + 32, n // 2, b * P:(b + 1) * P], DQK[r:r + 32, 2 + n // 2, 0:(b + 1) * P],
                       start=True, stop=True).then_inc(df_qk, 1)

            def df_turn(u):
                n, b = du[u]
                pe.wait_ge(df_p, u + 1)
                if u >= 1:
                    pe.wait_ge(df_pt, u)
                for t in range(b + 1):
                    last = nc.tensor.transpose(PB6[:, t * P:(t + 1) * P], L1[:, u % 2, t * P:(t + 1) * P], ident[:])
                last.then_inc(df_turned, 1)

            def df_out(u):
                n, b = du[u]
                pe.wait_ge(df_pt, u + 1)
                if u >= 1:
                    pe.wait_ge(df_o, u)
                for t in range(b + 1):
                    last = mm(PB7[:, 0:64], PT2[:, u % 2, t * P:(t + 1) * P], V2[:, t, 256 + n * 64:256 + (n + 1) * 64],
                              start=t == 0, stop=t == b)
                last.then_inc(df_pv, 1)

            def df_step(u):
                if u < len(du):
                    df_scores(u)
                if 1 <= u <= len(du):
                    df_turn(u - 1)
                if u >= 2:
                    df_out(u - 2)

            pe.wait_ge(freed["act"], LETGO["wo2"]["act"])
            for n in range(4):
                sb_logits(n)
                df_step(4 * n)
                df_step(4 * n + 1)
                sb_tails(n)
                df_step(4 * n + 2)
                df_step(4 * n + 3)
                sb_out(n)
            df_step(16)
            df_step(17)
            pe.wait_ge(oc_ready, 1)
            pe.wait_ge(b_lo, B_USE["m2"] + 1 + 4)
            for c in range(2):
                for b in range(QB):
                    last = nc.tensor.transpose(PX[:, c, b * P:(b + 1) * P], OC[:, b, c * P:(c + 1) * P], ident[:])
                last.then_inc(oc_turned, 1)
            pe.wait_ge(b_lo, B_USE["m2"] + M2_PIECES)
            stage("wo2", b_t, (b_lo, B_USE["m2"] + M2_PIECES - KC))
            norm("n2", T)
            for g, (c0, n) in enumerate(GROUPS):
                stage(f"gv{g}", a_t, (a_lo, A_USE["n2"]))
                stage(f"ed{g}", b_t, (b_lo, B_USE[f"ff{g}"]), kc=n)
            norm("fin2", T)
            for b in range(QB):
                for k in range(KC):
                    pe.wait_ge(normed["fin2"], k + 1)
                    if b >= 2 and k == 0:
                        pe.wait_ge(out_ready, b - 1)
                    last = nc.tensor.transpose(PJ[:, b % 2, k // 4, k % 4 * P:(k % 4 + 1) * P], H[:, k, b * P:(b + 1) * P], ident[:])
                last.then_inc(out_turned, 1)

        @block.scalar
        def _(act):
            go = nc.scalar.activation
            for e, credit in ((freed["act"], CREDIT), (v_ready, 1), (pt_ready, 1), (y_ready, 1)):
                act.sem_inc(e, credit)

            def rows(at, tile, src, n):
                act.dma_start(VR[at:at + n, tile, :], src).then_inc(vec_loaded, 16)

            def flat(v):
                return v.rearrange("o (c p) -> (o c) p", p=P)

            for at, v in ((V_MIX, norm_mix_g), (V_FFN, norm_ffn_g), (V_N1, norm1_g), (V_CAB, conv_a_b), (V_BR, b_rgate),
                          (V_BI, b_igate), (V_LAM, lru_lambda), (V_N2, norm2_g)):
                rows(at, 0, flat(v), v.shape[1] // P)
            for at, v in ((V_FIN, norm_final_g), (V_FIN2, final_g)):
                rows(at, 0, v.rearrange("(c p) -> c p", p=P), KC)
            rows(V_CW, 0, conv_w.rearrange("o j (c p) -> (o j c) p", p=P), 3 * KC)
            rows(V_CAW, 0, conv_a_w.rearrange("o j (c p) -> (o j c) p", p=P), 4 * 4)
            taps = conv_ff_w.rearrange("o j (c p) -> (o j c) p", p=P)
            rows(0, 1, taps[0:4 * FFC], 4 * FFC)
            rows(0, 2, taps[4 * FFC:6 * FFC], 2 * FFC)
            rows(2 * FFC, 2, flat(conv_ff_b), 2 * FFC)
            act.dma_start(GSUB[:], subln_g[0].partition_broadcast(P)).then_inc(small_loaded, 16)
            for n, v in enumerate((lam_q1, lam_k1, lam_q2, lam_k2)):
                act.dma_start(LAMV[:, n, :], v[0].partition_broadcast(P)).then_inc(small_loaded, 16)

            act.wait_ge(vec_done, 1)
            for t, n in enumerate((V_ROWS, 4 * FFC, 4 * FFC)):
                last = go(VEC[:, t, 0:n], PB6[:, t * P:t * P + n], ACT.Copy)
            last.then_inc(vec_ready, 1)
            act.wait_ge(cl_ready, 1)
            go(small[:, 4:8], small[:, 0:4], ACT.Exp, scale=-1.0).then_inc(cl_exp, 1)
            act.wait_ge(lam_sum, 1)
            go(small[:, 42:44], small[:, 40:42], ACT.Exp).then_inc(lam_e, 1)
            for k in range(KC):
                act.wait_ge(xt_done, k + 1)
                go(H0[:, k, META:N], PJ[:, k % 2, 0, :], ACT.Copy)
                go(H0[:, k, 0:META], PJ[:, k % 2, 1, 0:META], ACT.Copy).then_inc(h0_ready, 1)
            act.wait_ge(h0_ready, KC)
            act.dma_start(h_scratch, H0[:, :, META:N]).then_inc(h_stored, 16)

            def norm(name, src, width, src_ready, split):
                for k in range(KC):
                    act.wait_ge(src_ready[0], src_ready[1] + k + 1)
                    if k >= 2:
                        act.wait_ge(ms_added[name], k - 1)
                    go(SQ[:, k % 2, 0:width], src[:, k, :], ACT.Square).then_inc(sq_ready[name], 1)
                act.wait_ge(ms_added[name], KC)
                ms = PX[:, :, 0:HALF] if width == N else PX[:, 0, 0:T]
                go(cols(RT[:, 0:width], width), ms, ACT.Sqrt, bias=eps_t[:], scale=1.0 / D).then_inc(rt_ready[name], 1)
                if split:
                    for k in range(KC):
                        act.wait_ge(normed[name], k + 1)
                        go(AH[:, k, 0:width], TN[:, k % 2, 0:width], ACT.Copy).then_inc(a_hi, 1)

            norm("mix", H0, N, (h0_ready, 0), True)

            def slot_of(name, i):
                return (FIRST[name] + i) % 2

            def after(name, at):
                act.wait_ge(panel_done, at + (FIRST[name] + 1))

            after("ki", 0)
            go(cols(KI[0:64, :], N), PJ[0:64, 0, :, 0:HALF], ACT.Copy).then_inc(ki_ready, 1)
            go(cols(WIT[64:72, :], N), PJ[64:72, 0, :, 0:HALF], ACT.Copy).then_inc(freed["act"], 1)
            act.wait_ge(ki_ready, 1)
            act.dma_start(KI[64:128, :], KI[0:64, :]).then_inc(ki_twin, 16)

            def copies(name, dst, wide=False):
                with act.Fori(0, COUNT[name] // 2) as i:
                    for j in range(2):
                        s = slot_of(name, j)
                        after(name, i * 2 + j)
                        if wide:
                            go(cols(dst(i * 2 + j), N), PJ[:, s, :, 0:HALF], ACT.Copy).then_inc(freed["act"], 1)
                        else:
                            go(dst(i * 2 + j), PJ[:, s, 0, :], ACT.Copy).then_inc(freed["act"], 1)

            copies("qi", lambda c: pick(QI, c))
            for n in range(QB * IDX_HEADS):
                b = n // IDX_HEADS
                act.wait_ge(idx_done, n + 1)
                if n >= 2:
                    act.wait_ge(score_step, n - 1)
                src = (PX_flat, PJ[:, 0].rearrange("p a n -> p (a n)"))[n % 2]
                go(RL[:, n % 2, 0:EXT[b]], src[:, 0:EXT[b]], ACT.Relu).then_inc(relu_done, 1)
            copies("q", lambda c: pick(QT, c))
            copies("k", lambda c: pick(KT, c), wide=True)
            with act.Fori(0, 4) as i:
                for j in range(2):
                    after("v", i * 2 + j)
                    go(cols(VTT[:, j, :], N), PJ[:, slot_of("v", j), :, 0:HALF], ACT.Copy).then_inc(freed["act"], 1)
                for j in range(2):
                    act.wait_ge(v_turned, i * 2 + (j + 1))
                    go(V[:, 0:4, bass.ds((i * 2 + j) * P, P)], PX[:, 0, :].rearrange("p (t d) -> p t d", t=4), ACT.Copy)
                    go(V[0:META, 4, bass.ds((i * 2 + j) * P, P)], PX[0:META, 1, 0:P], ACT.Copy).then_inc(v_ready, 1)
            copies("cu", lambda c: pick(U, c), wide=True)

            units = [(j, b) for j in range(2) for b in range(QB)]
            NU = len(units)
            act.wait_ge(h_stored, 16)
            with act.Fori(0, 4) as i:
                def stage_q(u):
                    j, b = units[u]
                    g = i * NU + u
                    if u >= 2:
                        act.wait_ge(qk_done, i * NU + (u - 1))
                    go(QS[:, u % 2], QT[:, bass.ds(i * 2 + j, 1), b * P:(b + 1) * P].rearrange("p o n -> p (o n)"),
                       ACT.Copy, scale=ATT_SCALE).then_inc(qs_ready, 1)

                stage_q(0)
                stage_q(1)
                for s in range(NU + 4):
                    j = s // 2
                    if s % 2 == 1 and j < 6 and j % 3 != 0:
                        act.wait_ge(panel_done, i * 6 + (FIRST["gates"] + j + 1))
                        go(pick(GA if j % 3 == 1 else GB, i * 2 + j // 3), PJ[:, slot_of("gates", j), 0, :],
                           ACT.Tanh, scale=0.5).then_inc(freed["act"], 1)
                    if 0 <= s - 3 < NU:
                        u = s - 3
                        act.wait_ge(y_turned, i * NU + (u + 1))
                        act.sem_inc(act_seen, 1)
                        go(QT[:, bass.ds(i * 2 + units[u][0], 1), units[u][1] * P:(units[u][1] + 1) * P].rearrange("p o n -> p (o n)"),
                           TURNED_Y[:, 0:P], ACT.Copy).then_inc(y_ready, 1)
                    if 0 <= s - 1 < NU:
                        u = s - 1
                        b = units[u][1]
                        act.wait_ge(p_turned, i * NU + (u + 1))
                        go(PT[:, u % 2, 0:(b + 1) * P], PB6[:, 0:(b + 1) * P], ACT.Copy)
                        go(PT[0:META, u % 2, 4 * P:5 * P], TAIL_P[0:META, 0:P], ACT.Copy).then_inc(pt_ready, 1)
                    if s < NU:
                        b = units[s][1]
                        act.wait_ge(max_ready, i * NU + (s + 1))
                        go(LT[:, s % 2, 0:EXT[b]], LT[:, s % 2, 0:EXT[b]], ACT.Exp, bias=NMX[:, s % 2:s % 2 + 1],
                           accum_out=RS[:, s % 2:s % 2 + 1]).then_inc(exp_done, 1)
                    if s + 2 < NU:
                        stage_q(s + 2)

            act.wait_ge(panel_done, FIRST["co"])
            act.wait_ge(freed["dve"], LETGO["co"]["dve"])
            for k in range(KC):
                go(AH[:, k, 0:T], U[:, k, META:N], ACT.Copy).then_inc(a_hi, 1)
            act.wait_ge(y_ready, 1 + HEADS * QB)
            for k in range(KC):
                go(BH[:, k], QT[:, k], ACT.Copy).then_inc(b_hi, 1)
            act.wait_ge(wr_cleared, 1)
            for g, w in enumerate((w_rgate, w_igate)):
                for r in range(2):
                    act.dma_start(WR[64 * r:64 * r + 64, g, :, 64 * r:64 * r + 64],
                                  w[0].rearrange("(c r) i o -> r i c o", r=2)[r]).then_inc(small_loaded, 16)
            with act.Fori(0, 4) as i:
                for j in range(2):
                    act.wait_ge(mixed_ready, i * 2 + (j + 1))
                    go(AH[:, bass.ds(i * 2 + j, 1), 0:T].rearrange("p o n -> p (o n)"), pick(GB, i * 2 + j), ACT.Copy).then_inc(a_hi, 1)

            norm("ffn", H, T, (freed["dve"], LETGO["wo"]["dve"]), True)
            for g, (c0, n) in enumerate(GROUPS):
                name = f"gu{g}"
                with act.Fori(0, n // 2) as i:
                    for j in range(2):
                        q = i * 2 + j
                        after(name, i * 4 + 2 * j)
                        go(SG[:, j], PJ[:, slot_of(name, 0), 0, :], ACT.Tanh, scale=0.5).then_inc(tanh_ready, 1)
                        act.wait_ge(freed["dve"], i * 4 + (LETGO[name]["dve"] + 2 * j + 2))
                        go(pick(BH, q), T2[:, j], ACT.Copy).then_inc(b_hi, 1)
            norm("fin", H, T, (freed["dve"], LETGO["dn2"]["dve"]), False)
            norm("n1", H, T, (normed["fin"], 0), True)

            copies("xa", lambda c: XA[:, bass.ds(c, 1), 3:T + 3].rearrange("p o n -> p (o n)"))
            copies("ya", lambda c: pick(YA, c))
            for c in range(4):
                after("sqk", c)
                go(SQK[:, c], PJ[:, slot_of("sqk", c), 0, :], ACT.Copy).then_inc(freed["act"], 1)
                for g in range(2):
                    act.wait_ge(rg_done, 2 * c + g + 1)
                    go((RP, IP)[g][:, c], PX[:, g, :], ACT.Tanh, bias=small[:, 24 + 4 * g + c:25 + 4 * g + c], scale=0.5).then_inc(rg_tanh, 1)
            act.wait_ge(gelu_in, 1)
            go(GY[:], GY[:], ACT.Tanh, scale=GELU_C).then_inc(gelu_t, 1)
            act.wait_ge(rg_tanh, 8)
            for c in range(4):
                go(TH[:, c], RP[:, c], ACT.Tanh, bias=small[:, 20 + c:21 + c], scale=small[:, 20 + c:21 + c]).then_inc(lru_a, 1)
            for c in range(4):
                after("dqk", c)
                go(DQK[:, c], PJ[:, slot_of("dqk", c), 0, :], ACT.Copy).then_inc(freed["act"], 1)
                act.wait_ge(lru_a, 4 + c)
                go(RP[:, c], RP[:, c], ACT.Exp, bias=small[:, 16 + c:17 + c], scale=small[:, 16 + c:17 + c]).then_inc(lru_a, 1)
            for j in range(4):
                name = ("sv", "dv")[j // 2]
                after(name, j % 2)
                go(V2[:, :, j * P:(j + 1) * P], PJ[:, slot_of(name, j % 2), 0, :].rearrange("p (t d) -> p t d", t=QB),
                   ACT.Copy).then_inc(freed["act"], 1)
                if j == 0:
                    act.wait_ge(lru_q, 1)
                    go(TH[:], TH[:], ACT.Sqrt, scale=0.25).then_inc(lru_root, 1)

            def recurrence_hi():
                act.wait_ge(outa_ready, 1)
                go(BH[:, 0:4, :], XC[:], ACT.Copy).then_inc(b_hi, 1)

            def sb_hi(n):
                r, c = 64 * (n % 2), n // 2
                act.wait_ge(sb_pv, n + 1)
                go(BH[r:r + 64, 4 + c, :], SB_OUT[r:r + 64, :], ACT.Copy).then_inc(b_hi, 1)

            du = [(n, b) for n in range(4) for b in range(QB)]

            def df_step(u):
                if u >= 2:
                    n, b = du[u - 2]
                    act.wait_ge(df_pv, u - 1)
                    go(OC[:, b, n * 64:(n + 1) * 64], PB7[:, 0:64], ACT.Copy).then_inc(df_o, 1)
                if 1 <= u <= len(du):
                    n, b = du[u - 1]
                    act.wait_ge(df_turned, u)
                    go(PT2[:, (u - 1) % 2, 0:(b + 1) * P], PB6[:, 0:(b + 1) * P], ACT.Copy).then_inc(df_pt, 1)
                if u < len(du):
                    n, b = du[u]
                    for m, l in enumerate((L1, L2)):
                        at = 2 * (u % 2) + m
                        act.wait_ge(df_max, 2 * u + m + 1)
                        go(l[:, u % 2, 0:(b + 1) * P], l[:, u % 2, 0:(b + 1) * P], ACT.Exp, bias=small[:, 48 + at:49 + at],
                           accum_out=small[:, 52 + at:53 + at]).then_inc(df_exp, 1)

            for n in range(4):
                z = Z[:, n % 2]
                if n >= 1:
                    sb_hi(n - 1)
                for m, (i0, o, w) in enumerate(SB_BANKS):
                    act.wait_ge(z_done, 3 * n + m + 1)
                    go(z[:, o:o + w], SB_BANK[m][:, 0:w], ACT.Copy, scale=SB_SCALE).then_inc(z_ready, 1)
                act.wait_ge(z_ready, 3 * (n + 1))
                go(LN[:], z, ACT.Abs).then_inc(act_step, 1)
                act.wait_ge(act_step, 2 * n + 1)
                go(LN[:], LN[:], ACT.Exp, scale=-1.0).then_inc(act_step, 1)
                act.wait_ge(act_step, 2 * n + 2)
                go(LN[:], LN[:], ACT.Ln, bias=ones[:, 0:1]).then_inc(sb_ln, 1)
                if n == 0:
                    recurrence_hi()
                df_step(4 * n)
                df_step(4 * n + 1)
                act.wait_ge(sb_sum, 3 * (n + 1))
                go(z, z, ACT.Exp).then_inc(sb_w, 1)
                df_step(4 * n + 2)
                df_step(4 * n + 3)
            sb_hi(3)
            df_step(16)
            df_step(17)
            act.wait_ge(oc_sq, 1)
            go(small[:, 80:96], small[:, 64:80], ACT.Sqrt, bias=eps_t[:], scale=1.0 / 64).then_inc(oc_root, 1)
            for c in range(2):
                act.wait_ge(oc_turned, c + 1)
                go(BH[:, 6 + c, :], PX[:, c, :], ACT.Copy).then_inc(b_hi, 1)

            norm("n2", H, T, (freed["dve"], LETGO["wo2"]["dve"]), True)
            for g, (c0, n) in enumerate(GROUPS):
                name = f"gv{g}"
                with act.Fori(0, n // 2) as i:
                    for j in range(2):
                        q = i * 2 + j
                        for m in range(2):
                            after(name, i * 4 + (2 * j + m))
                            go(T1[:, 2 * j + m], PJ[:, slot_of(name, m), 0, :], ACT.Identity,
                               bias=VEC[:, 2, bass.ds(q + (2 * FFC + FFC * m + c0), 1)],
                               scale=VEC[:, 2, bass.ds(q + (FFC * m + c0), 1)]).then_inc(conv_base, 1)
                            if m == 0:
                                act.wait_ge(freed["dve"], i * 4 + (LETGO[name]["dve"] + 2 * j + 1))
                                go(SG[:, j], T1[:, 2 * j], ACT.Tanh, scale=0.5).then_inc(tanh_ready, 1)
                        act.wait_ge(ff_step, q + (c0 + 1))
                        go(pick(BH, q), T2[:, j], ACT.Copy).then_inc(b_hi, 1)
            norm("fin2", H, T, (freed["dve"], LETGO["ed2"]["dve"]), False)
            for b in range(QB):
                act.wait_ge(out_turned, b + 1)
                go(OUT[:, b], PJ[:, b % 2].rearrange("p a n -> p (a n)"), ACT.Copy).then_inc(out_ready, 1)

        @block.vector
        def _(dve):
            ts, tt, stt = nc.vector.tensor_scalar, nc.vector.tensor_tensor, nc.vector.scalar_tensor_tensor
            for e, credit in ((freed["dve"], CREDIT), (logits_ready, 1), (ys_ready, 1)):
                dve.sem_inc(e, credit)
            steps = [0]

            def step(ins):
                ins.then_inc(dve_step, 1)
                steps[0] += 1

            def settled():
                dve.wait_ge(dve_step, steps[0])

            dve.wait_ge(consts_ready, 5)
            step(nc.vector.tensor_copy(DIST[:], DISTI[:]))
            settled()
            step(stt(out=DIST[:], in0=DIST[:], scalar=-1.0, in1=DIST[:], op0=ALU.mult, op1=ALU.max))
            dve.wait_ge(vec_ready, 1)
            lam = VEC[:, 0, V_LAM:V_LAM + 4]
            stt(out=small[:, 0:4], in0=lam, scalar=-1.0, in1=lam, op0=ALU.mult, op1=ALU.max).then_inc(cl_ready, 1)
            dve.wait_ge(small_loaded, 16 * 5)
            step(tt(LAMV[:, 0, :], LAMV[:, 0, :], LAMV[:, 1, :], ALU.mult))
            step(tt(LAMV[:, 2, :], LAMV[:, 2, :], LAMV[:, 3, :], ALU.mult))
            settled()
            nc.vector.tensor_reduce(small[:, 40:42], LAMV[:, 0:4:2, :], AX.X, ALU.add).then_inc(lam_sum, 1)
            dve.wait_ge(cl_exp, 1)
            e, z, z2, q = small[:, 4:8], small[:, 8:12], small[:, 12:16], small[:, 28:32]
            z = small[:, 32:36]
            z2 = small[:, 36:40]
            q = small[:, 8:12]
            step(ts(q, e, 2.0, None, ALU.add))
            settled()
            step(nc.vector.reciprocal(z, q))
            settled()
            step(tt(z, z, e, ALU.mult))
            settled()
            step(tt(z2, z, z, ALU.mult))
            settled()
            step(ts(q, z2, 1.0 / 15, None, ALU.mult))
            for m in (13, 11, 9, 7, 5, 3):
                settled()
                step(stt(out=q, in0=q, scalar=1.0 / m, in1=z2, op0=ALU.add, op1=ALU.mult))
            settled()
            step(stt(out=q, in0=q, scalar=1.0, in1=z, op0=ALU.add, op1=ALU.mult))
            step(ts(small[:, 12:16], lam, -1.0, 0.0, ALU.mult, ALU.max))
            settled()
            step(stt(out=q, in0=q, scalar=2.0, in1=small[:, 12:16], op0=ALU.mult, op1=ALU.add))
            settled()
            step(ts(small[:, 16:20], q, -4.0, None, ALU.mult))
            step(ts(small[:, 20:24], q, 4.0, None, ALU.mult))
            step(ts(small[:, 24:28], VEC[:, 0, V_BR:V_BR + 4], 0.5, None, ALU.mult))
            step(ts(small[:, 28:32], VEC[:, 0, V_BI:V_BI + 4], 0.5, None, ALU.mult))
            step(ts(GSUB[:], GSUB[:], 1.0 - LAM_INIT, None, ALU.mult))
            dve.wait_ge(lam_e, 1)
            step(tt(small[:, 44:45], small[:, 43:44], small[:, 42:43], ALU.subtract))
            settled()
            step(ts(small[:, 44:45], small[:, 44:45], LAM_INIT, None, ALU.subtract))
            settled()

            def norm(name, src, gain, width, split):
                dve.wait_ge(rt_ready[name], 1)
                nc.vector.reciprocal(RSTD[:, 0:width], RT[:, 0:width]).then_inc(rstd_ready[name], 1)
                dve.wait_ge(rstd_ready[name], 1)
                for k in range(KC + 1):
                    if k < KC:
                        dst = TN[:, k % 2, 0:width] if split else src[:, k, :]
                        if split and k >= 2:
                            dve.wait_ge(a_lo, A_USE[name] + k - 1)
                        stt(out=dst, in0=src[:, k, :], scalar=VEC[:, 0, gain + k:gain + k + 1], in1=RSTD[:, 0:width],
                            op0=ALU.mult, op1=ALU.mult).then_inc(normed[name], 1)
                    if k >= 1 and split:
                        dve.wait_ge(a_hi, A_USE[name] + k)
                        tt(AL[:, k - 1, 0:width], TN[:, (k - 1) % 2, 0:width], AH[:, k - 1, 0:width].bitcast(F32),
                           ALU.subtract).then_inc(a_lo, 1)

            norm("mix", H0, V_MIX, N, True)

            def slot_of(name, i):
                return (FIRST[name] + i) % 2

            def after(name, at):
                dve.wait_ge(panel_done, at + (FIRST[name] + 1))

            dve.wait_ge(wq_done, 1)
            ts(WQ[:].rearrange("p b h -> p (b h)"), PB6[:, 0:QB * IDX_HEADS], IDX_SCALE, None, ALU.mult).then_inc(wq_ready, 1)
            dve.wait_ge(wq_ready, 1)
            for b in range(QB):
                sc = S[:, b, PADS:PADS + EXT[b]]
                for h in range(IDX_HEADS):
                    n = b * IDX_HEADS + h
                    dve.wait_ge(relu_done, n + 1)
                    if h == 0:
                        ts(sc, RL[:, n % 2, 0:EXT[b]], WQ[:, b, h:h + 1], None, ALU.mult).then_inc(score_step, 1)
                    else:
                        dve.wait_ge(score_step, n)
                        stt(out=sc, in0=RL[:, n % 2, 0:EXT[b]], scalar=WQ[:, b, h:h + 1], in1=sc,
                            op0=ALU.mult, op1=ALU.add).then_inc(score_step, 1)
            dve.wait_ge(score_step, QB * IDX_HEADS)
            for b in range(QB):
                own = S[:, b, PADS + EXT[b] - P:PADS + EXT[b]]
                tt(own, own, hide[:], ALU.add).then_inc(topk_step, 1)
                nc.vector.memset(S[:, b, 0:PADS], SENTINEL).then_inc(topk_step, 1)
            for b in range(QB):
                base = 2 * QB + b * 2 * ROUNDS
                row = S[:, b, 0:PADS + EXT[b]]
                with dve.Fori(0, ROUNDS) as i:
                    dve.wait_ge(topk_step, i * 2 + base)
                    dve.sem_inc(dve_seen, 1)
                    nc.vector.max(MX8[:], row).then_inc(topk_step, 1)
                    dve.wait_ge(topk_step, i * 2 + (base + 1))
                    dve.sem_inc(dve_seen, 1)
                    nc.vector.match_replace(row, MX8[:], row, TAKEN).then_inc(topk_step, 1)
            dve.wait_ge(topk_step, 2 * QB * (1 + ROUNDS // 1))
            for b in range(QB):
                m = S[:, b, PADS:PADS + EXT[b]]
                ts(m, m, TAKEN / 1.5, HIDDEN, ALU.is_gt, ALU.mult).then_inc(mask_ready, 1)
            dve.wait_ge(mask_ready, QB)
            for b in range(QB):
                own = S[:, b, PADS + EXT[b] - P:PADS + EXT[b]]
                tt(own, own, hide[:], ALU.min).then_inc(mask_ready, 1)

            dve.wait_ge(freed["act"], LETGO["cc"]["act"])
            with dve.Fori(0, 4) as i:
                for j in range(2):
                    after("cc", i * 2 + j)
                    u = cols(pick(U, i * 2 + j), N)
                    tt(u, u, PJ[:, slot_of("cc", j), :, 0:HALF], ALU.mult).then_inc(freed["dve"], 1)

            dve.wait_ge(mask_ready, 2 * QB)
            dve.wait_ge(freed["dve"], LETGO["gates"]["dve"])
            units = [(j, b) for j in range(2) for b in range(QB)]
            NU = len(units)
            with dve.Fori(0, 4) as i:
                def conv(j):
                    c = i * 2 + j
                    def tap(t):
                        return VEC[:, 0, bass.ds(c + (V_CW + t * KC), 1)]
                    def seen(t):
                        return U[:, bass.ds(c, 1), META - 2 + t:N - 2 + t].rearrange("p o n -> p (o n)")
                    dve.wait_ge(freed["dve"], i * 2 + (LETGO["gates"]["dve"] - 1 + j))
                    ts(CT[:, j], seen(2), tap(2), None, ALU.mult).then_inc(conv_step, 1)
                    for t in (1, 0):
                        dve.wait_ge(conv_step, i * 6 + (3 * j + 2 - t))
                        stt(out=CT[:, j], in0=seen(t), scalar=tap(t), in1=CT[:, j], op0=ALU.mult, op1=ALU.add).then_inc(conv_step, 1)

                for s in range(NU + 2):
                    if s in (1, 7):
                        j = s // 6
                        after("gates", i * 6 + 3 * j)
                        dve.wait_ge(conv_step, i * 6 + 3 * (j + 1))
                        tt(U[:, bass.ds(i * 2 + j, 1), META:N].rearrange("p o n -> p (o n)"), CT[:, j],
                           PJ[:, slot_of("gates", 3 * j), 0, :], ALU.mult).then_inc(freed["dve"], 1)
                    if 0 <= s - 1 < NU:
                        u = s - 1
                        dve.wait_ge(exp_done, i * NU + (u + 1))
                        nc.vector.reciprocal(RINV[:, u % 4:u % 4 + 1], RS[:, u % 2:u % 2 + 1]).then_inc(rinv_ready, 1)
                    if 0 <= s - 2 < NU:
                        u = s - 2
                        dve.wait_ge(rinv_ready, i * NU + (u + 1))
                        dve.wait_ge(pv_done, i * NU + (u + 1))
                        ts(YS[:, u % 2], PB7[:, 0:P], RINV[:, u % 4:u % 4 + 1], None, ALU.mult).then_inc(ys_ready, 1)
                    if s < NU:
                        b = units[s][1]
                        dve.wait_ge(qk_done, i * NU + (s + 1))
                        tt(LT[:, s % 2, 0:EXT[b]], PX_flat[:, 0:EXT[b]], S[:, b, PADS:PADS + EXT[b]], ALU.add).then_inc(logits_ready, 1)
                        dve.wait_ge(logits_ready, i * NU + (s + 2))
                        nc.vector.tensor_reduce(NMX[:, s % 2:s % 2 + 1], LT[:, s % 2, 0:EXT[b]], AX.X, ALU.max, negate=True).then_inc(max_ready, 1)
                    if s in (0, 5):
                        conv(s // 5)

            for k in range(KC):
                dve.wait_ge(a_hi, A_USE["conv"] + k + 1)
                tt(AL[:, k, 0:T], U[:, k, META:N], AH[:, k, 0:T].bitcast(F32), ALU.subtract).then_inc(a_lo, 1)
            for k in range(KC):
                dve.wait_ge(b_hi, B_USE["y"] + k + 1)
                tt(BL[:, k], QT[:, k], BH[:, k].bitcast(F32), ALU.subtract).then_inc(b_lo, 1)
            dve.wait_ge(b_lo, B_USE["y"] + KC)
            nc.vector.memset(WR[:], 0.0).then_inc(wr_cleared, 1)
            step(nc.vector.memset(XA[:, :, 0:3], 0.0))

            with dve.Fori(0, 4) as i:
                for j in range(2):
                    after("co", i * 2 + j)
                    g = pick(GB, i * 2 + j)
                    stt(out=g, in0=g, scalar=1.0, in1=PJ[:, slot_of("co", j), 0, :], op0=ALU.add, op1=ALU.mult).then_inc(freed["dve"], 1)
            with dve.Fori(0, 4) as i:
                for j in range(2):
                    c = i * 2 + j
                    after("ao", c)
                    ga, gb = pick(GA, c), pick(GB, c)
                    stt(out=ga, in0=ga, scalar=1.0, in1=PJ[:, slot_of("ao", j), 0, :], op0=ALU.add, op1=ALU.mult).then_inc(freed["dve"], 1)
                    dve.wait_ge(freed["dve"], c + (LETGO["ao"]["dve"] + 1))
                    tt(gb, ga, gb, ALU.add).then_inc(mixed_ready, 1)
                    dve.wait_ge(a_hi, c + (A_USE["mixed"] + 1))
                    tt(AL[:, bass.ds(c, 1), 0:T].rearrange("p o n -> p (o n)"), gb,
                       AH[:, bass.ds(c, 1), 0:T].rearrange("p o n -> p (o n)").bitcast(F32), ALU.subtract).then_inc(a_lo, 1)

            def residual(name, scale):
                with dve.Fori(0, COUNT[name] // 2) as i:
                    for j in range(2):
                        after(name, i * 2 + j)
                        h = pick(H, i * 2 + j)
                        stt(out=h, in0=PJ[:, slot_of(name, j), 0, :], scalar=scale, in1=h, op0=ALU.mult, op1=ALU.add).then_inc(freed["dve"], 1)

            dve.wait_ge(h_loaded, 16)
            residual("wo", 0.5)
            norm("ffn", H, V_FFN, T, True)
            for g, (c0, n) in enumerate(GROUPS):
                name = f"gu{g}"
                with dve.Fori(0, n // 2) as i:
                    for j in range(2):
                        q = i * 2 + j
                        dve.wait_ge(tanh_ready, q + (c0 + 1))
                        stt(out=T1[:, j], in0=SG[:, j], scalar=1.0, in1=PJ[:, slot_of(name, 0), 0, :],
                            op0=ALU.add, op1=ALU.mult).then_inc(freed["dve"], 1)
                        after(name, i * 4 + (2 * j + 1))
                        dve.wait_ge(freed["dve"], i * 4 + (LETGO[name]["dve"] + 2 * j + 1))
                        dve.wait_ge(b_lo, q + (B_USE[f"act{g}"] - 1))
                        tt(T2[:, j], T1[:, j], PJ[:, slot_of(name, 1), 0, :], ALU.mult).then_inc(freed["dve"], 1)
                        dve.wait_ge(b_hi, q + (B_USE[f"act{g}"] + 1))
                        tt(pick(BL, q), T2[:, j], pick(BH, q).bitcast(F32), ALU.subtract).then_inc(b_lo, 1)
                residual(f"dn{g}", 0.5)
            norm("fin", H, V_FIN, T, False)
            dve.wait_ge(normed["fin"], KC)
            norm("n1", H, V_N1, T, True)

            dve.wait_ge(freed["act"], LETGO["ya"]["act"])
            for c in range(4):
                def tap(t):
                    return VEC[:, 0, V_CAW + 4 * t + c:V_CAW + 4 * t + c + 1]
                step(ts(XC[:, c], XA[:, c, 3:T + 3], tap(3), VEC[:, 0, V_CAB + c:V_CAB + c + 1], ALU.mult, ALU.add))
                for t in (2, 1, 0):
                    settled()
                    ins = stt(out=XC[:, c], in0=XA[:, c, t:T + t], scalar=tap(t), in1=XC[:, c], op0=ALU.mult, op1=ALU.add)
                    if t:
                        step(ins)
                    else:
                        ins.then_inc(xc_ready, 1)
            dve.wait_ge(freed["act"], LETGO["sqk"]["act"])
            step(tt(GY[:], YA[:], YA[:], ALU.mult))
            settled()
            step(ts(GY[:], GY[:], 0.044715, 1.0, ALU.mult, ALU.add))
            settled()
            tt(GY[:], GY[:], YA[:], ALU.mult).then_inc(gelu_in, 1)
            dve.wait_ge(gelu_t, 1)
            step(stt(out=GY[:], in0=GY[:], scalar=1.0, in1=YA[:], op0=ALU.add, op1=ALU.mult))
            dve.wait_ge(lru_a, 8)
            settled()
            step(tt(YA[:], RP[:], RP[:], ALU.mult))
            settled()
            stt(out=TH[:], in0=YA[:], scalar=1.0, in1=TH[:], op0=ALU.add, op1=ALU.mult).then_inc(lru_q, 1)
            dve.wait_ge(xc_ready, 4)
            step(stt(out=IP[:], in0=IP[:], scalar=1.0, in1=XC[:], op0=ALU.add, op1=ALU.mult))
            settled()
            dve.wait_ge(lru_root, 1)
            step(tt(IP[:], IP[:], TH[:], ALU.mult))
            settled()
            for c in range(4):
                step(nc.vector.tensor_tensor_scan(XC[:, c], RP[:, c], IP[:, c], 0.0, ALU.mult, ALU.add))
            settled()
            stt(out=XC[:], in0=XC[:], scalar=0.5, in1=GY[:], op0=ALU.mult, op1=ALU.mult).then_inc(outa_ready, 1)

            def recurrence_lo():
                dve.wait_ge(b_hi, B_USE["m2"] + 1)
                tt(BL[:, 0:4, :], XC[:], BH[:, 0:4, :].bitcast(F32), ALU.subtract).then_inc(b_lo, 1)

            def sb_lo(n):
                r, c = 64 * (n % 2), n // 2
                dve.wait_ge(b_hi, B_USE["m2"] + 1 + n + 1)
                tt(BL[r:r + 64, 4 + c, :], SB_OUT[r:r + 64, :], BH[r:r + 64, 4 + c, :].bitcast(F32), ALU.subtract).then_inc(b_lo, 1)

            du = [(n, b) for n in range(4) for b in range(QB)]

            def df_step(u):
                if u < len(du):
                    n, b = du[u]
                    E = (b + 1) * P
                    if b == 0:
                        step(ts(BIAS[:], DIST[:], -SLOPES[n], None, ALU.mult))
                        settled()
                        step(nc.vector.memset(BIAS[0:64, T - 64:T], HIDDEN))
                        settled()
                    for m, l in enumerate((L1, L2)):
                        at = 2 * (u % 2) + m
                        dve.wait_ge(df_qk, 2 * u + m + 1)
                        stt(out=l[:, u % 2, 0:E], in0=PX[:, m, 0:E], scalar=DF_SCALE, in1=BIAS[:, T - E:T],
                            op0=ALU.mult, op1=ALU.add).then_inc(df_lt, 1)
                        dve.wait_ge(df_lt, 2 * u + m + 1)
                        nc.vector.tensor_reduce(small[:, 48 + at:49 + at], l[:, u % 2, 0:E], AX.X, ALU.max, negate=True).then_inc(df_max, 1)
                if u >= 1:
                    v = u - 1
                    E = (du[v][1] + 1) * P
                    at = 2 * (v % 2)
                    r1, r2 = small[:, 56 + at:57 + at], small[:, 57 + at:58 + at]
                    dve.wait_ge(df_exp, 2 * v + 2)
                    step(nc.vector.reciprocal(small[:, 56 + at:58 + at], small[:, 52 + at:54 + at]))
                    settled()
                    step(tt(r2, r2, small[:, 44:45], ALU.mult))
                    step(ts(L1[:, v % 2, 0:E], L1[:, v % 2, 0:E], r1, None, ALU.mult))
                    settled()
                    stt(out=L1[:, v % 2, 0:E], in0=L2[:, v % 2, 0:E], scalar=r2, in1=L1[:, v % 2, 0:E],
                        op0=ALU.mult, op1=ALU.add).then_inc(df_p, 1)

            for n in range(4):
                z = Z[:, n % 2]
                if n >= 1:
                    sb_lo(n - 1)
                dve.wait_ge(z_ready, 3 * (n + 1))
                step(ts(LG[:], z, 0.0, None, ALU.max))
                if n == 0:
                    recurrence_lo()
                df_step(4 * n)
                settled()
                dve.wait_ge(sb_ln, n + 1)
                step(stt(out=LG[:], in0=LG[:], scalar=-1.0, in1=LN[:], op0=ALU.mult, op1=ALU.subtract))
                settled()
                for i in range(QB):
                    last = tt(LG[:, SBO[i]:SBO[i] + P], LG[:, SBO[i]:SBO[i] + P], before[:], ALU.mult)
                last.then_inc(sb_log, 1)
                df_step(4 * n + 1)
                for m, (i0, o, w) in enumerate(SB_BANKS):
                    dve.wait_ge(tail_done, 3 * n + m + 1)
                    tt(z[:, o:o + w], SB_BANK[m][:, 0:w], z[:, o:o + w], ALU.add).then_inc(sb_sum, 1)
                df_step(4 * n + 2)
                dve.wait_ge(sb_w, n + 1)
                for i in range(QB):
                    last = tt(z[:, SBO[i]:SBO[i] + P], z[:, SBO[i]:SBO[i] + P], before[:], ALU.mult)
                last.then_inc(sb_masked, 1)
                df_step(4 * n + 3)
            sb_lo(3)
            df_step(16)
            dve.wait_ge(df_o, len(du))
            oc = OC[:].rearrange("p b (n d) -> p (b n) d", d=64)
            osq = OSQ[:].rearrange("p b (n d) -> p (b n) d", d=64)
            step(tt(osq, oc, oc, ALU.mult))
            settled()
            nc.vector.tensor_reduce(small[:, 64:80], osq, AX.X, ALU.add).then_inc(oc_sq, 1)
            dve.wait_ge(oc_root, 1)
            step(nc.vector.reciprocal(small[:, 96:112], small[:, 80:96]))
            settled()
            step(tt(oc, oc, small[:, 96:112].unsqueeze(2).to_broadcast([P, 16, 64]), ALU.mult))
            settled()
            tt(oc, oc, GSUB[:].unsqueeze(1).to_broadcast([P, 16, 64]), ALU.mult).then_inc(oc_ready, 1)
            for c in range(2):
                dve.wait_ge(b_hi, B_USE["m2"] + 5 + c + 1)
                tt(BL[:, 6 + c, :], PX[:, c, :], BH[:, 6 + c, :].bitcast(F32), ALU.subtract).then_inc(b_lo, 1)

            residual("wo2", 1.0)
            norm("n2", H, V_N2, T, True)
            for g, (c0, n) in enumerate(GROUPS):
                name = f"gv{g}"
                with dve.Fori(0, n // 2) as i:
                    for j in range(2):
                        q = i * 2 + j
                        for m in range(2):
                            t1, ps = T1[:, 2 * j + m], PJ[:, slot_of(name, m), 0, :]
                            dve.wait_ge(conv_base, i * 4 + (2 * c0 + 2 * j + m + 1))
                            stt(out=t1[:, 1:T], in0=ps[:, 0:T - 1], scalar=VEC[:, 1, bass.ds(q + (2 * FFC + FFC * m + c0), 1)],
                                in1=t1[:, 1:T], op0=ALU.mult, op1=ALU.add).then_inc(conv_step, 1)
                            dve.wait_ge(conv_step, i * 4 + (24 + 2 * c0 + 2 * j + m + 1))
                            stt(out=t1[:, 2:T], in0=ps[:, 0:T - 2], scalar=VEC[:, 1, bass.ds(q + (FFC * m + c0), 1)],
                                in1=t1[:, 2:T], op0=ALU.mult, op1=ALU.add).then_inc(freed["dve"], 1)
                        dve.wait_ge(tanh_ready, q + (FFC + c0 + 1))
                        stt(out=SG[:, j], in0=SG[:, j], scalar=1.0, in1=T1[:, 2 * j], op0=ALU.add, op1=ALU.mult).then_inc(dve_seen, 1)
                        dve.wait_ge(dve_seen, q + (2 * QB * ROUNDS + c0 + 1))
                        dve.wait_ge(freed["dve"], i * 4 + (LETGO[name]["dve"] + 2 * j + 2))
                        dve.wait_ge(b_lo, q + (B_USE[f"ff{g}"] - 1))
                        tt(T2[:, j], SG[:, j], T1[:, 2 * j + 1], ALU.mult).then_inc(ff_step, 1)
                        dve.wait_ge(b_hi, q + (B_USE[f"ff{g}"] + 1))
                        tt(pick(BL, q), T2[:, j], pick(BH, q).bitcast(F32), ALU.subtract).then_inc(b_lo, 1)
                residual(f"ed{g}", 0.5)
            norm("fin2", H, V_FIN2, T, False)


_INS = ["x", "meta_tokens", "norm_mix_g", "w_in", "w_attn_out", "conv_w", "w_conv_out", "w_out", "norm_ffn_g", "w_gate",
        "w_up", "w_down", "norm_final_g", "norm1_g_2", "w_in_2", "conv_a_w_2", "conv_a_b_2", "w_rgate_2", "b_rgate_2",
        "w_igate_2", "b_igate_2", "lru_lambda_2", "lam_q1_2", "lam_k1_2", "lam_q2_2", "lam_k2_2", "subln_g_2",
        "w_out_2", "norm2_g_2", "w_ff_up_2", "conv_ff_w_2", "conv_ff_b_2", "w_ff_down_2", "final_g_2"]


def kernel(**inputs):
    import concourse.bacc as _bacc
    from concourse.bass_utils import run_bass_kernel_spmd as _run

    nc = _bacc.Bacc("TRN2", target_bir_lowering=False, num_devices=1)
    arrays, args = {}, []
    for name in _INS:
        a = np.ascontiguousarray(inputs[name])
        arrays[f"in_{name}_dram"] = a
        args.append(nc.dram_tensor(f"in_{name}_dram", a.shape, mybir.dt.from_np(a.dtype), kind="ExternalInput").ap())
    args.append(nc.dram_tensor("out_0_dram", (1, T, D), F32, kind="ExternalOutput").ap())
    two_blocks(nc, *args)
    r = _run(nc, [arrays], core_ids=[0])
    return r.results[0]["out_0_dram"]
```

```python
from contextlib import ExitStack

import numpy as np
import concourse.bass as bass
from concourse import mybir

F32 = mybir.dt.float32
F32R = mybir.dt.float32r
I32 = mybir.dt.int32
ALU = mybir.AluOpType
ACT = mybir.ActivationFunctionType
AX = mybir.AxisListType

P = 128
D = 1024
KC = D // P
T = 512
META = 16
N = T + META
HALF = N // 2
BANK = 512
QB = T // P
HEADS = 8
IDX_HEADS, IDX_DIM = 8, 64
TOPK = min(256, N // 4)
PADS = -TOPK % 8
ROUNDS = (TOPK + PADS) // 8
IDX_SCALE = (IDX_HEADS ** -0.5) * (IDX_DIM ** -0.5)
ATT_SCALE = P ** -0.5
EPS = 1e-6
FF = 2816
FFC = FF // P
GROUPS = [(0, 8), (8, 8), (16, 6)]
DF_SCALE = 32 ** -0.5
SB_SCALE = 64 ** -0.5
LAM_INIT = 0.8 - 0.6 * float(np.exp(-0.3 * 0))
SLOPES = [2.0 ** (-8.0 * (h + 1) / 4) for h in range(4)]
GELU_C = float(np.sqrt(2.0 / np.pi))
HIDDEN = -1e30
TAKEN = -3e38
SENTINEL = 3e38

C_Q, C_K, C_V, C_QI, C_KI, C_CU, C_CB, C_CC, C_GA, C_GB = 0, 1024, 2048, 3072, 3584, 3656, 4680, 5704, 6728, 7752

STAGES = [("ki", 1, "act"), ("qi", 4, "act"), ("q", 8, "act"), ("k", 8, "act"), ("v", 8, "act"),
          ("cu", 8, "act"), ("cc", 8, "dve"), ("gates", 24, "both"), ("co", 8, "dve"), ("ao", 8, "dve"), ("wo", 8, "dve"),
          ("gu0", 16, "dve"), ("dn0", 8, "dve"), ("gu1", 16, "dve"), ("dn1", 8, "dve"), ("gu2", 12, "dve"), ("dn2", 8, "dve"),
          ("dqk", 4, "act"), ("dv", 2, "act"), ("xa", 4, "act"), ("ya", 4, "act"), ("sqk", 4, "act"), ("sv", 2, "act"),
          ("wo2a", 4, "dve"), ("wo2b", 4, "dve"),
          ("gv0", 16, "dve"), ("ed0", 8, "dve"), ("gv1", 16, "dve"), ("ed1", 8, "dve"), ("gv2", 12, "dve"), ("ed2", 8, "dve")]
FIRST, COUNT, OWNER, LETGO = {}, {}, {}, {}
CREDIT = 2
_p, _n = 0, {"act": CREDIT, "dve": CREDIT}
for _name, _count, _owner in STAGES:
    FIRST[_name], COUNT[_name], OWNER[_name] = _p, _count, _owner
    LETGO[_name] = dict(_n)
    if _owner == "both":
        _n["dve"] += _count // 3
        _n["act"] += _count * 2 // 3
    else:
        _n[_owner] += _count
    _p += _count
PANELS = _p
ORDER = [s[0] for s in STAGES]
RAW_SLOTS, W_SLOTS = 4, 2

BESIDE = [(n, c) for n, k in (("xa", 4), ("ya", 4), ("sqk", 4), ("sv", 2)) for c in range(k)]
DF_UNITS = [(n, b) for n in range(4) for b in range(QB)]

EXT = [META + P * (b + 1) for b in range(QB)]
SBW = [T - P * i for i in range(QB)]
SBO = [sum(SBW[:i]) for i in range(QB)]
SBT = sum(SBW)
SB_BANKS = [(0, SBO[0], SBW[0]), (1, SBO[1], SBW[1]), (2, SBO[2], SBW[2] + SBW[3])]

V_MIX, V_CW, V_FFN, V_FIN, V_N1, V_CAW, V_CAB, V_BR, V_BI, V_LAM, V_N2, V_FIN2, V_ROWS = 0, 8, 32, 40, 48, 56, 72, 76, 80, 84, 88, 96, 104


def two_blocks(nc, x, meta_tokens, norm_mix_g, w_in, w_attn_out, conv_w, w_conv_out, w_out, norm_ffn_g, w_gate,
               w_up, w_down, norm_final_g, norm1_g, w_in_2, conv_a_w, conv_a_b, w_rgate, b_rgate,
               w_igate, b_igate, lru_lambda, lam_q1, lam_k1, lam_q2, lam_k2, subln_g,
               w_out_2, norm2_g, w_ff_up, conv_ff_w, conv_ff_b, w_ff_down, final_g, out):
    with ExitStack() as ctx:
        def sem(name):
            return ctx.enter_context(nc.semaphore(name))

        top = [(nc.sbuf_base + 63) // 64 * 64]

        def region(nbytes):
            at = top[0]
            top[0] += (nbytes + 31) // 32 * 32
            return [at, top[0]]

        def place(reg, name, shape, dt=F32):
            nbytes = int(np.prod(shape[1:])) * 4
            t = nc.alloc_sbuf_tensor_at(name, shape, dt, offset=reg[0])
            reg[0] += (nbytes + 31) // 32 * 32
            assert reg[0] <= reg[1], (name, reg)
            return t

        def again(reg, start):
            return [start, reg[1]]

        def solo(name, shape, dt=F32):
            return place(region(int(np.prod(shape[1:])) * 4), name, shape, dt)

        r_weights = region(4 * (RAW_SLOTS + 2 * W_SLOTS) * KC * P)
        RAW = place(r_weights, "RAW", [P, RAW_SLOTS, KC, P])
        WH = place(r_weights, "WH", [P, W_SLOTS, KC, P], F32R)
        WL = place(r_weights, "WL", [P, W_SLOTS, KC, P], F32R)
        ident = solo("ident", [P, P])
        ones = solo("ones", [P, P])
        tri = solo("tri", [P, P])
        before = solo("before", [P, P])
        hide = solo("hide", [P, P])
        VEC = solo("VEC", [P, 3, P])
        eps_t = solo("eps_t", [P, 1])
        zero_t = solo("zero_t", [P, 1])
        WQ = solo("WQ", [P, QB, IDX_HEADS])
        MX8 = solo("MX8", [P, 8])
        NMX = solo("NMX", [P, 2])
        RS = solo("RS", [P, 2])
        RINV = solo("RINV", [P, 4])
        small = solo("small", [P, 128])
        DIST = solo("DIST", [P, T])
        GSUB = solo("GSUB", [P, 64])
        LAMV = solo("LAMV", [P, 4, 32])

        r_a = region(2 * 4 * KC * N)
        a0 = r_a[0]
        AH = place(r_a, "AH", [P, KC, N], F32R)
        AL = place(r_a, "AL", [P, KC, N], F32R)
        ra2 = again(r_a, a0)
        Z = place(ra2, "Z", [P, 2, SBT])
        LN = place(ra2, "LN", [P, SBT])
        LG = place(ra2, "LG", [P, SBT])


        r_b = region(4 * (HEADS * N + 5 * D))
        b0 = r_b[0]
        KT = place(r_b, "KT", [P, HEADS, N])
        V = place(r_b, "V", [P, 5, D])
        rb2 = again(r_b, b0)
        XR = place(rb2, "XR", [P, QB, D])
        XM = place(rb2, "XM", [META, D])
        VR = place(rb2, "VR", [P, 3, P])
        rb3 = again(r_b, b0)
        BH = place(rb3, "BH", [P, KC, T], F32R)
        BL = place(rb3, "BL", [P, KC, T], F32R)
        half_b = 4 * (KC // 2) * T
        RP = place(again(r_b, b0 + half_b), "RP", [P, 4, T])
        IP = place(again(r_b, b0 + 2 * half_b), "IP", [P, 4, T])
        TH = place(again(r_b, b0 + 3 * half_b), "TH", [P, 4, T])
        PT2 = place(again(r_b, b0 + 4 * half_b), "PT2", [P, 2, T])
        rb4 = again(r_b, b0)
        OUT = place(rb4, "OUT", [P, QB, D])

        r_q = region(4 * KC * T + 64)
        q0 = r_q[0]
        QT = place(r_q, "QT", [P, HEADS, T])
        rq2 = again(r_q, q0)
        XA = place(rq2, "XA", [P, 4, T + 3])
        YA = place(rq2, "YA", [P, 4, T])

        r_x = region(4 * KC * N)
        x0 = r_x[0]
        H0 = place(r_x, "H0", [P, KC, N])
        rx2 = again(r_x, x0)
        GB = place(rx2, "GB", [P, KC, T])
        rx3 = again(r_x, x0)
        SQK = place(rx3, "SQK", [P, 4, T])
        DQK = place(rx3, "DQK", [P, 4, T])

        r_u = region(4 * KC * N)
        u0 = r_u[0]
        U = place(r_u, "U", [P, KC, N])
        ru2 = again(r_u, u0)
        H = place(ru2, "H", [P, KC, T])

        r_g = region(4 * KC * T)
        g0 = r_g[0]
        GA = place(r_g, "GA", [P, KC, T])
        rg2 = again(r_g, g0)
        QI = place(rg2, "QI", [P, 4, T])
        KI = place(rg2, "KI", [P, N])
        WIT = place(rg2, "WIT", [P, N])
        rg3 = again(r_g, g0)
        V2 = place(rg3, "V2", [P, QB, 512])
        GY = place(rg3, "GY", [P, 4, T])

        r_s = region(4 * QB * (PADS + N))
        s0 = r_s[0]
        S = place(r_s, "S", [P, QB, PADS + N])
        rs2 = again(r_s, s0)
        BIAS = place(rs2, "BIAS", [P, T])
        WR = place(rs2, "WR", [P, 2, 4, P])
        R = place(rs2, "R", [P, T])

        r_t = region(4 * (4 * T + QB * 256 + 2 * T + 4 * T))
        t0 = r_t[0]
        SQ = place(r_t, "SQ", [P, 2, N])
        TN = place(r_t, "TN", [P, 2, N])
        RT = place(r_t, "RT", [P, N])
        RSTD = place(r_t, "RSTD", [P, N])
        rt2 = again(r_t, t0)
        RL = place(rt2, "RL", [P, 2, N])
        VTT = place(rt2, "VTT", [P, 2, N])
        rt3 = again(r_t, t0)
        LT = place(rt3, "LT", [P, 2, N])
        CT = place(rt3, "CT", [P, 2, T])
        PT = place(rt3, "PT", [P, 2, 5 * P])
        QS = place(rt3, "QS", [P, 2, P])
        YS = place(rt3, "YS", [P, 2, P])
        rt4 = again(r_t, t0)
        SG = place(rt4, "SG", [P, 2, T])
        T1 = place(rt4, "T1", [P, 4, T])
        T2 = place(rt4, "T2", [P, 2, T])
        US = place(again(r_t, rt4[0]), "US", [P, 4, T])
        SQT = place(rt4, "SQT", [P, 2, T])
        SS = place(rt4, "SS", [P, T])
        ROOT = place(rt4, "ROOT", [P, T])
        rt5 = again(r_t, t0)
        XC = place(rt5, "XC", [P, 4, T])
        OC = place(rt5, "OC", [P, QB, 256])
        L = place(rt5, "L", [P, 2, 2, T])
        rt6 = again(r_t, rt5[0])
        A2 = place(again(r_t, rt5[0]), "A2", [P, 2, T])
        OSQ = place(rt5, "OSQ", [P, QB, 256])
        VT2 = place(rt6, "VT2", [P, 2, T])
        rt8 = again(r_t, t0)
        DISTI = place(rt8, "DISTI", [P, T], I32)
        assert top[0] <= nc.sbuf_usable_end, top

        PJ = ctx.enter_context(nc.psum_tensor("PJ", [P, 2, 2, BANK], F32))
        PX = ctx.enter_context(nc.psum_tensor("PX", [P, 2, BANK], F32))
        PB6 = ctx.enter_context(nc.psum_tensor("PB6", [P, BANK], F32))
        PB7 = ctx.enter_context(nc.psum_tensor("PB7", [P, BANK], F32))
        TURNED_Y, TAIL_P = PJ[:, 0, 1, :], PJ[:, 1, 1, :]
        SB_Z = [PX[:, 0, :], PX[:, 1, :], PB6[:, :]]
        SB_TAIL = [PB7[:, :], PJ[:, 0, 1, :], PJ[:, 1, 1, :]]
        SB_OUT = PX[:, 0, :]
        SIDE = [PJ[:, 0, 1, :], PJ[:, 1, 1, :]]
        PX_flat = PX[:, :, :].rearrange("p a n -> p (a n)")

        h_scratch = nc.dram_tensor("h_scratch", (P, KC, T), F32).ap()

        raw_loaded = [sem(f"raw_loaded{i}") for i in range(RAW_SLOTS)]
        w_hi = sem("w_hi")
        w_ready = sem("w_ready")
        pool_seen = sem("pool_seen")
        dve_seen, act_seen = sem("dve_seen"), sem("act_seen")
        panel_done = sem("panel_done")
        freed = {"act": sem("freed_act"), "dve": sem("freed_dve")}
        consts_ready = sem("consts_ready")
        const_step = sem("const_step")
        x_loaded, meta_loaded, vec_loaded = sem("x_loaded"), sem("meta_loaded"), sem("vec_loaded")
        xt_done, h0_ready = sem("xt_done"), sem("h0_ready")
        vec_done, vec_ready = sem("vec_done"), sem("vec_ready")
        NORMS = ["mix", "ffn", "fin", "n1", "n2", "fin2"]
        sq_ready = {n: sem(f"sq_ready_{n}") for n in NORMS}
        ms_added = {n: sem(f"ms_added_{n}") for n in NORMS}
        rt_ready = {n: sem(f"rt_ready_{n}") for n in NORMS}
        rstd_ready = {n: sem(f"rstd_ready_{n}") for n in NORMS}
        normed = {n: sem(f"normed_{n}") for n in NORMS}
        LATE = ["ffn", "n2", "fin2"]
        ss_added = {n: sem(f"ss_added_{n}") for n in LATE}
        ss_summed = {n: sem(f"ss_summed_{n}") for n in LATE}
        gate_scaled, silu_ready, taps_done = sem("gate_scaled"), sem("silu_ready"), sem("taps_done")
        a_hi, a_lo = sem("a_hi"), sem("a_lo")
        b_hi, b_lo = sem("b_hi"), sem("b_lo")
        h_stored, h_loaded = sem("h_stored"), sem("h_loaded")
        ki_ready, ki_twin = sem("ki_ready"), sem("ki_twin")
        wq_done, wq_ready = sem("wq_done"), sem("wq_ready")
        idx_done, relu_done, score_step = sem("idx_done"), sem("relu_done"), sem("score_step")
        topk_step, mask_ready = sem("topk_step"), sem("mask_ready")
        v_turned, v_ready = sem("v_turned"), sem("v_ready")
        u_ready, conv_step = sem("u_ready"), sem("conv_step")
        qs_ready, qk_done, logits_ready, max_ready = sem("qs_ready"), sem("qk_done"), sem("logits_ready"), sem("max_ready")
        exp_done, rinv_ready, p_turned, pt_ready = sem("exp_done"), sem("rinv_ready"), sem("p_turned"), sem("pt_ready")
        pv_done, ys_ready, y_turned, y_ready = sem("pv_done"), sem("ys_ready"), sem("y_turned"), sem("y_ready")
        mixed_ready = sem("mixed_ready")
        tanh_ready, ff_step, conv_base = sem("tanh_ready"), sem("ff_step"), sem("conv_base")
        small_loaded, wr_cleared = sem("small_loaded"), sem("wr_cleared")
        act_step, dve_step = sem("act_step"), sem("dve_step")
        cl_ready, lam_e, lam_ready, gate_half = sem("cl_ready"), sem("lam_e"), sem("lam_ready"), sem("gate_half")
        lam_sum, cl_exp = sem("lam_sum"), sem("cl_exp")
        xa_ready, xc_ready, rg_done, rg_tanh = sem("xa_ready"), sem("xc_ready"), sem("rg_done"), sem("rg_tanh")
        lru_a, lru_q, lru_root = sem("lru_a"), sem("lru_q"), sem("lru_root")
        v2_turned, v2_ready = sem("v2_turned"), sem("v2_ready")
        gelu_in, gelu_t = sem("gelu_in"), sem("gelu_t")
        outa_ready = sem("outa_ready")
        z_done, z_ready, sb_ln, sb_log, tail_done, sb_sum, sb_w, sb_masked, sb_pv = (
            sem(n) for n in ("z_done", "z_ready", "sb_ln", "sb_log", "tail_done", "sb_sum", "sb_w", "sb_masked", "sb_pv"))
        bias_step, df_qk, df_max, df_exp, df_p, df_turned, df_pt, df_pv, df_o = (
            sem(n) for n in ("bias_step", "df_qk", "df_max", "df_exp", "df_p", "df_turned", "df_pt", "df_pv", "df_o"))
        df_lt, df_r = sem("df_lt"), sem("df_r")
        oc_sq, oc_root, oc_ready, oc_turned = sem("oc_sq"), sem("oc_root"), sem("oc_ready"), sem("oc_turned")
        out_turned, out_ready, stored = sem("out_turned"), sem("out_ready"), sem("stored")

        block = ctx.enter_context(nc.Block())

        def pick(t, i):
            return t[:, bass.ds(i, 1)].rearrange("p o n -> p (o n)")

        def chunk_of(t, i):
            return t[:, bass.ds(i, 1), 0:T].rearrange("p o n -> p (o n)")

        def cols(ap, w):
            return ap.rearrange("p (a n) -> p a n", a=2) if w == N else ap

        A_USE, B_USE = {}, {}
        for _use, _pieces in ((A_USE, [("mix", KC), ("conv", KC), ("mixed", KC), ("act0", 8), ("act1", 8), ("act2", 6), ("n1", KC), ("n2", KC)]),
                              (B_USE, [("y", KC), ("ffn", KC), ("m2", 7), ("ff0", 8), ("ff1", 8), ("ff2", 6)])):
            _b = 0
            for _n_, _c in _pieces:
                _use[_n_] = _b
                _b += _c
        M2 = {piece: i + 1 for i, piece in enumerate(["lru", "sb0", "sb1", "df0", "df1", "sb2", "sb3"])}
        M2_PIECES = len(M2)

        @block.sync
        def _(sp):
            sp.dma_start(XR[:], x[0].rearrange("(t p) d -> p t d", p=P)).then_inc(x_loaded, 16)
            sp.dma_start(XM[:], meta_tokens).then_inc(meta_loaded, 16)

            def load(slot, src, free):
                if free is not None:
                    sp.wait_ge(w_ready, free)
                k, b = src.shape[0] // P, src.shape[1] // P
                sp.dma_start(RAW[:, slot, 0:k * b].rearrange("p (k b) c -> p k (b c)", b=b),
                             src.rearrange("(k p) c -> p k c", p=P)).then_inc(raw_loaded[slot], 16)

            def run(first, blocks, src):
                with sp.Fori(0, blocks) as i:
                    for j in range(RAW_SLOTS):
                        load((first + j) % RAW_SLOTS, src(i, j), first - RAW_SLOTS + 1 + j + i * RAW_SLOTS)

            def columns(w, c0, width=P):
                return lambda i, j: w[:, bass.ds(i * (4 * width) + (c0 + j * width), width)]

            def pairs(wa, ca, wb, cb):
                return lambda i, j: (wa if j % 2 == 0 else wb)[:, bass.ds(i * (2 * P) + ((ca if j % 2 == 0 else cb) + j // 2 * P), P)]

            def gate_up(name, wa, ca, wb, cb, g):
                c0, n = GROUPS[g]
                run(FIRST[name], n // 2, pairs(wa, ca + c0 * P, wb, cb + c0 * P))

            def down(name, w, g):
                c0, n = GROUPS[g]
                run(FIRST[name], 2, columns(w[c0 * P:(c0 + n) * P], 0))

            w1, w2 = w_in[0], w_in_2[0]
            load(0, w1[:, C_KI:C_KI + P], None)
            for p in range(1, 5):
                load(p % RAW_SLOTS, w1[:, C_QI + (p - 1) * P:C_QI + p * P], p - RAW_SLOTS + 1 if p >= RAW_SLOTS else None)
            for name, c0 in (("q", C_Q), ("k", C_K), ("v", C_V), ("cu", C_CU), ("cc", C_CC)):
                run(FIRST[name], 2, columns(w1, c0))
            with sp.Fori(0, 2) as i:
                for j in range(12):
                    c0 = (C_CB, C_GA, C_GB)[j % 3]
                    load((FIRST["gates"] + j) % RAW_SLOTS, w1[:, bass.ds(i * (4 * P) + (c0 + j // 3 * P), P)],
                         FIRST["gates"] + j - RAW_SLOTS + 1 + i * 12)
            for name, w in (("co", w_conv_out), ("ao", w_attn_out), ("wo", w_out)):
                run(FIRST[name], 2, columns(w[0], 0))
                if name == "co":
                    sp.wait_ge(h_stored, 16)
                    sp.wait_ge(a_lo, A_USE["conv"] + KC)
                    sp.dma_start(H[:], h_scratch).then_inc(h_loaded, 16)
            for g in range(3):
                gate_up(f"gu{g}", w_gate[0], 0, w_up[0], 0, g)
                down(f"dn{g}", w_down[0], g)
            def two(name, c0):
                for j in range(2):
                    p = FIRST[name] + j
                    load(p % RAW_SLOTS, w2[:, c0 + j * P:c0 + (j + 1) * P], p - RAW_SLOTS + 1)

            run(FIRST["dqk"], 1, columns(w2, 1792))
            two("dv", 2304)
            run(FIRST["xa"], 2, columns(w2, 0))
            run(FIRST["sqk"], 1, columns(w2, 1024))
            two("sv", 1536)
            run(FIRST["wo2a"], 1, columns(w_out_2[0][0:D // 2], 0, 2 * P))
            run(FIRST["wo2b"], 1, columns(w_out_2[0][D // 2:D], 0, 2 * P))
            for g in range(3):
                gate_up(f"gv{g}", w_ff_up[0], 0, w_ff_up[0], FF, g)
                down(f"ed{g}", w_ff_down[0], g)
            for b in range(QB):
                sp.wait_ge(out_ready, b + 1)
                sp.dma_start(out[0, b * P:(b + 1) * P, :], OUT[:, b]).then_inc(stored, 16)
            sp.wait_ge(stored, 16 * QB)

        @block.gpsimd
        def _(pool):
            pool.memset(ident[:], 0.0).then_inc(const_step, 1)
            pool.memset(ones[:], 1.0).then_inc(const_step, 1)
            pool.memset(hide[:], 0.0).then_inc(const_step, 1)
            pool.memset(eps_t[:], EPS).then_inc(const_step, 1)
            pool.memset(zero_t[:], 0.0).then_inc(const_step, 1)
            pool.wait_ge(const_step, 5)
            pool.iota(DISTI[:], [[-1, T]], base=T - P, channel_multiplier=1).then_inc(consts_ready, 1)
            pool.affine_select(out=ident[:], in_=ident[:], compare_op=ALU.not_equal, fill=1.0, base=0,
                               pattern=[[-1, P]], channel_multiplier=1).then_inc(consts_ready, 1)
            pool.affine_select(out=tri[:], in_=ones[:], compare_op=ALU.is_ge, fill=0.0, base=0,
                               pattern=[[-1, P]], channel_multiplier=1).then_inc(consts_ready, 1)
            pool.affine_select(out=before[:], in_=ones[:], compare_op=ALU.is_gt, fill=0.0, base=0,
                               pattern=[[1, P]], channel_multiplier=-1).then_inc(consts_ready, 1)
            pool.affine_select(out=hide[:], in_=hide[:], compare_op=ALU.is_ge, fill=HIDDEN, base=0,
                               pattern=[[-1, P]], channel_multiplier=1).then_inc(consts_ready, 1)

            def split(slot, w, loaded, used, p):
                pool.wait_ge(raw_loaded[slot], loaded)
                if used is not None:
                    pool.wait_ge(panel_done, used)
                pool.sem_inc(pool_seen, 1)
                nc.gpsimd.tensor_scalar(WH[:, w], RAW[:, slot], 1.0, 1.0, ALU.mult, ALU.mult).then_inc(w_hi, 1)
                pool.wait_ge(w_hi, p + 1)
                nc.gpsimd.tensor_tensor(WL[:, w], RAW[:, slot], WH[:, w].bitcast(F32), ALU.subtract).then_inc(w_ready, 1)

            PEEL = 5
            for p in range(PEEL):
                split(p % RAW_SLOTS, p % W_SLOTS, 16 * (p // RAW_SLOTS + 1), p - 1 if p >= 2 else None, p)
            with pool.Fori(0, (PANELS - PEEL) // RAW_SLOTS) as i:
                for j in range(RAW_SLOTS):
                    p = PEEL + j
                    split(p % RAW_SLOTS, p % W_SLOTS, i * 16 + 16 * (p // RAW_SLOTS + 1), i * RAW_SLOTS + (p - 1), i * RAW_SLOTS + p)

        @block.tensor
        def _(pe):
            mm = nc.tensor.matmul

            def slot_of(name, i):
                return (FIRST[name] + i) % 2

            def panel(name, i, at, rhs, ready, wide=False, rows=P, kc=KC, half=None, owner=None):
                s = slot_of(name, i)
                rh, rl = rhs
                if half in (None, 0):
                    pe.wait_ge(w_ready, at + (FIRST[name] + 1))
                    who = owner or OWNER[name]
                    if owner is None:
                        pe.wait_ge(freed[who], at + (LETGO[name][who] - 1))
                parts = [(WH, rh), (WH, rl), (WL, rh)]
                last = None
                ks = range(kc) if half is None else range(half * kc // 2, (half + 1) * kc // 2)
                for k in ks:
                    if ready is not None:
                        pe.wait_ge(ready[0], ready[1] + k + 1)
                    for n, (w, a) in enumerate(parts):
                        st, sp_ = k == 0 and n == 0, k == kc - 1 and n == 2
                        if wide:
                            for h in range(2):
                                last = mm(PJ[0:rows, s, h, 0:HALF], w[:, s, k, 0:rows], a[:, k, h * HALF:(h + 1) * HALF], start=st, stop=sp_)
                        else:
                            last = mm(PJ[0:rows, s, 0, 0:T], w[:, s, k, 0:rows], a[:, k, :], start=st, stop=sp_)
                if half in (None, 1):
                    last.then_inc(panel_done, 1)

            def enter(name):
                prev = ORDER[ORDER.index(name) - 1]
                if OWNER[prev] != OWNER[name]:
                    for who in ("act", "dve"):
                        pe.wait_ge(freed[who], LETGO[name][who])

            def stage(name, rhs, ready, lead=None, **kw):
                enter(name)
                first = 0
                if lead:
                    panel(name, 0, 0, rhs, ready, half=0, **kw)
                    lead()
                    panel(name, 0, 0, rhs, ready, half=1, **kw)
                    panel(name, 1, 1, rhs, ready, **kw)
                    first = 1
                with pe.Fori(0, COUNT[name] // 2 - first) as i:
                    for j in range(2):
                        panel(name, j, i * 2 + (2 * first + j), rhs, ready, **kw)

            def late_sum(name):
                pe.wait_ge(ss_added[name], KC + 2)
                mm(PX[:, 0, 0:T], ones[:], SS[:], start=True, stop=True).then_inc(ss_summed[name], 1)

            def norm(name, width):
                for k in range(KC):
                    pe.wait_ge(sq_ready[name], k + 1)
                    if width == N:
                        mm(PX[:, 0, 0:HALF], ones[:], SQ[:, k % 2, 0:HALF], start=k == 0, stop=k == KC - 1)
                        last = mm(PX[:, 1, 0:HALF], ones[:], SQ[:, k % 2, HALF:N], start=k == 0, stop=k == KC - 1)
                    else:
                        last = mm(PX[:, 0, 0:T], ones[:], SQ[:, k % 2, 0:T], start=k == 0, stop=k == KC - 1)
                    last.then_inc(ms_added[name], 1)

            a_wide = (AH[:, :, :], AL[:, :, :])
            a_x = (AH[:, :, META:N], AL[:, :, META:N])
            a_t = (AH[:, :, 0:T], AL[:, :, 0:T])
            b_t = (BH[:, :, :], BL[:, :, :])

            pe.wait_ge(consts_ready, 5)
            pe.wait_ge(vec_loaded, 16 * 15)
            for t, rows in enumerate((V_ROWS, 88, 88)):
                last = nc.tensor.transpose(PB6[:, t * P:t * P + rows], VR[0:rows, t, :], ident[0:rows, 0:rows])
            last.then_inc(vec_done, 1)
            pe.wait_ge(x_loaded, 16)
            pe.wait_ge(meta_loaded, 16)
            for k in range(KC):
                if k >= 2:
                    pe.wait_ge(h0_ready, k - 1)
                for t in range(QB):
                    nc.tensor.transpose(PJ[:, k % 2, 0, t * P:(t + 1) * P], XR[:, t, k * P:(k + 1) * P], ident[:])
                nc.tensor.transpose(PJ[:, k % 2, 1, 0:META], XM[:, k * P:(k + 1) * P], ident[0:META, 0:META]).then_inc(xt_done, 1)
            norm("mix", N)

            mix = (a_lo, A_USE["mix"])
            panel("ki", 0, 0, a_wide, mix, wide=True, rows=IDX_DIM + IDX_HEADS)
            stage("qi", a_x, mix)
            pe.wait_ge(freed["act"], LETGO["qi"]["act"])
            for b in range(QB):
                last = nc.tensor.transpose(PB6[:, b * 8:b * 8 + 8], WIT[64:72, META + b * P:META + (b + 1) * P], ident[64:72, 64:72])
            last.then_inc(wq_done, 1)
            pe.wait_ge(freed["act"], LETGO["q"]["act"])
            pe.wait_ge(ki_twin, 16)
            for b in range(QB):
                for h in range(IDX_HEADS):
                    n, r = b * IDX_HEADS + h, 64 * (h % 2)
                    if n >= 2:
                        pe.wait_ge(relu_done, n - 1)
                    dst = (PX_flat, PJ[:, 0].rearrange("p a n -> p (a n)"))[n % 2]
                    lhs = QI[r:r + 64, h // 2, b * P:(b + 1) * P]
                    last = mm(dst[:, 0:min(EXT[b], BANK)], lhs, KI[r:r + 64, 0:min(EXT[b], BANK)], start=True, stop=True)
                    if EXT[b] > BANK:
                        last = mm(dst[:, BANK:EXT[b]], lhs, KI[r:r + 64, BANK:EXT[b]], start=True, stop=True)
                    last.then_inc(idx_done, 1)
            pe.wait_ge(relu_done, QB * IDX_HEADS)
            stage("q", a_x, mix)
            stage("k", a_wide, mix, wide=True)
            with pe.Fori(0, 4) as i:
                for j in range(2):
                    panel("v", j, i * 2 + j, a_wide, mix, wide=True)
                for j in range(2):
                    pe.wait_ge(freed["act"], i * 2 + (LETGO["v"]["act"] + j + 1))
                    pe.wait_ge(v_ready, i * 2 + (j + 1))
                    for t in range(4):
                        nc.tensor.transpose(PX[:, 0, t * P:(t + 1) * P], VTT[:, j, t * P:(t + 1) * P], ident[:])
                    nc.tensor.transpose(PX[0:META, 1, 0:P], VTT[:, j, T:N], ident[:]).then_inc(v_turned, 1)
            stage("cu", a_wide, mix, wide=True)
            stage("cc", a_wide, mix, wide=True)

            enter("gates")
            pe.wait_ge(v_ready, HEADS + 1)
            units = [(j, b) for j in range(2) for b in range(QB)]
            NU = len(units)

            def qk(i, u):
                j, b = units[u]
                pe.wait_ge(qs_ready, i * NU + (u + 1))
                pe.wait_ge(logits_ready, i * NU + (u + 1))
                head = KT[:, bass.ds(i * 2 + j, 1), :].rearrange("p o n -> p (o n)")
                last = mm(PX[:, 0, 0:min(EXT[b], BANK)], QS[:, u % 2], head[:, 0:min(EXT[b], BANK)], start=True, stop=True)
                if EXT[b] > BANK:
                    last = mm(PX[:, 1, 0:EXT[b] - BANK], QS[:, u % 2], head[:, BANK:EXT[b]], start=True, stop=True)
                last.then_inc(qk_done, 1)

            def turn_p(i, u):
                j, b = units[u]
                pe.wait_ge(exp_done, i * NU + (u + 1))
                pe.wait_ge(pt_ready, i * NU + (u + 1))
                for t in range(b + 1):
                    nc.tensor.transpose(PB6[:, t * P:(t + 1) * P], LT[:, u % 2, t * P:(t + 1) * P], ident[:])
                nc.tensor.transpose(TAIL_P[0:META, 0:P], LT[:, u % 2, (b + 1) * P:EXT[b]], ident[:]).then_inc(p_turned, 1)

            def pv(i, u):
                j, b = units[u]
                pe.wait_ge(pt_ready, i * NU + (u + 2))
                pe.wait_ge(ys_ready, i * NU + (u + 1))
                for t in range(b + 1):
                    mm(PB7[:, 0:P], PT[:, u % 2, t * P:(t + 1) * P], V[:, t, bass.ds((i * 2 + j) * P, P)], start=t == 0, stop=False)
                mm(PB7[:, 0:P], PT[0:META, u % 2, 4 * P:5 * P], V[0:META, b + 1, bass.ds((i * 2 + j) * P, P)],
                   start=False, stop=True).then_inc(pv_done, 1)

            def turn_y(i, u):
                pe.wait_ge(ys_ready, i * NU + (u + 2))
                pe.wait_ge(y_ready, i * NU + (u + 1))
                nc.tensor.transpose(TURNED_Y[:, 0:P], YS[:, u % 2], ident[:]).then_inc(y_turned, 1)

            with pe.Fori(0, 4) as i:
                for half in range(12):
                    j = half // 2
                    if half % 2 == 0:
                        who = "dve" if j % 3 == 2 else "act"
                        base = LETGO["gates"]
                        if who == "dve":
                            pe.wait_ge(freed["dve"], i * 2 + (base["dve"] + j // 3 + 1))
                        else:
                            pe.wait_ge(freed["act"], i * 4 + (base["act"] + (0, 0, None, 1, 2)[j] - (1 if j == 0 else 0)))
                    panel("gates", j, i * 6 + j, a_x, mix, half=half % 2, owner="here")
                    if half - 3 >= 0 and half - 3 < NU:
                        turn_y(i, half - 3)
                    if half - 2 >= 0 and half - 2 < NU:
                        pv(i, half - 2)
                    if half - 1 >= 0 and half - 1 < NU:
                        turn_p(i, half - 1)
                    if half < NU:
                        qk(i, half)
            stage("co", a_t, (a_lo, A_USE["conv"]))
            stage("ao", b_t, (b_lo, B_USE["y"]))
            stage("wo", a_t, (a_lo, A_USE["mixed"]))
            for g, (c0, n) in enumerate(GROUPS):
                stage(f"gu{g}", b_t, (b_lo, B_USE["ffn"]), lead=(lambda: late_sum("ffn")) if g == 0 else None)
                stage(f"dn{g}", a_t, (a_lo, A_USE[f"act{g}"]), kc=n)
            norm("fin", T)
            norm("n1", T)

            n1 = (a_lo, A_USE["n1"])
            stage("dqk", a_t, n1)

            def turn_values(j):
                pe.wait_ge(freed["act"], LETGO[("dv", "sv")[j // 2]]["act"] + j % 2 + 1)
                if j >= 2:
                    pe.wait_ge(rg_tanh, 8)
                for t in range(QB):
                    last = nc.tensor.transpose(SIDE[j % 2][:, t * P:(t + 1) * P], VT2[:, j % 2, t * P:(t + 1) * P], ident[:])
                last.then_inc(v2_turned, 1)

            def df_scores(u):
                n, b = DF_UNITS[u]
                if u >= 1:
                    pe.wait_ge(df_lt, u)
                for m in range(2):
                    r = 32 * (2 * (n % 2) + m)
                    last = mm(PX[:, m, 0:(b + 1) * P], DQK[r:r + 32, n // 2, b * P:(b + 1) * P], DQK[r:r + 32, 2 + n // 2, 0:(b + 1) * P],
                              start=True, stop=True)
                last.then_inc(df_qk, 1)

            def df_turn(u):
                n, b = DF_UNITS[u]
                pe.wait_ge(df_p, u + 1)
                if u >= 1:
                    pe.wait_ge(df_pt, u)
                for t in range(b + 1):
                    last = nc.tensor.transpose(PB6[:, t * P:(t + 1) * P], L[:, u % 2, 0, t * P:(t + 1) * P], ident[:])
                last.then_inc(df_turned, 1)

            def df_out(u):
                n, b = DF_UNITS[u]
                pe.wait_ge(df_pt, u + 1)
                if u >= 1:
                    pe.wait_ge(df_o, u)
                for t in range(b + 1):
                    last = mm(PB7[:, 0:64], PT2[:, u % 2, t * P:(t + 1) * P], V2[:, t, 256 + n * 64:256 + (n + 1) * 64],
                              start=t == 0, stop=t == b)
                last.then_inc(df_pv, 1)

            def df_step(u):
                if u >= 2:
                    df_out(u - 2)
                if 1 <= u <= len(DF_UNITS):
                    df_turn(u - 1)
                if u + 1 < len(DF_UNITS):
                    df_scores(u + 1)

            enter("dv")
            panel("dv", 0, 0, a_t, n1)
            panel("dv", 1, 1, a_t, n1)
            df_scores(0)
            turn_values(0)
            pe.wait_ge(small_loaded, 16 * (5 + 4))
            for s, (name, c) in enumerate(BESIDE):
                panel(name, c, c, a_t, n1)
                if s == 0:
                    turn_values(1)
                if s == 2:
                    pe.wait_ge(v2_ready, 2)
                df_step(s)
                if name == "ya":
                    pe.wait_ge(xc_ready, c + 1)
                    if c >= 1:
                        pe.wait_ge(rg_tanh, 2 * c)
                    for g in range(2):
                        mm(SIDE[g], WR[:, g, c, :], XC[:, c, :], start=True, stop=True).then_inc(rg_done, 1)
            turn_values(2)

            def sb_logits(n):
                r, c = 64 * (n % 2), n // 2
                if n >= 1:
                    pe.wait_ge(z_ready, 3 * n)
                if n >= 2:
                    pe.wait_ge(b_lo, B_USE["m2"] + M2[f"sb{n - 2}"])
                for m, (i0, o, w) in enumerate(SB_BANKS):
                    for i in ((i0,) if m < 2 else (2, 3)):
                        at = SBO[i] - o
                        last = mm(SB_Z[m][:, at:at + SBW[i]], SQK[r:r + 64, 2 + c, i * P:(i + 1) * P], SQK[r:r + 64, c, i * P:T],
                                  start=i == i0, stop=True, skip_group_check=True)
                    last.then_inc(z_done, 1)

            def sb_tails(n):
                pe.wait_ge(sb_log, n + 1)
                if n >= 1:
                    pe.wait_ge(sb_sum, 3 * n)
                for m, (i0, o, w) in enumerate(SB_BANKS):
                    for i in ((i0,) if m < 2 else (2, 3)):
                        at = SBO[i] - o
                        last = mm(SB_TAIL[m][:, at:at + SBW[i]], tri[:], LG[:, SBO[i]:SBO[i] + SBW[i]],
                                  start=i == i0, stop=True, skip_group_check=True)
                        for j in range(i + 1, QB):
                            last = mm(SB_TAIL[m][:, at + (j - i) * P:at + SBW[i]], ones[:], LG[:, SBO[j]:SBO[j] + SBW[j]],
                                      start=False, stop=True, skip_group_check=True)
                    last.then_inc(tail_done, 1)

            def sb_out(n):
                r = 64 * (n % 2)
                pe.wait_ge(sb_masked, n + 1)
                pe.wait_ge(z_ready, 3 * min(n + 2, 4))
                if n >= 1:
                    pe.wait_ge(b_lo, B_USE["m2"] + M2[f"sb{n - 1}"])
                for i in range(QB):
                    last = mm(SB_OUT[r:r + 64, i * P:T], V2[:, i, n * 64:(n + 1) * 64], Z[:, n % 2, SBO[i]:SBO[i] + SBW[i]],
                              start=i == 0, stop=True, skip_group_check=True)
                last.then_inc(sb_pv, 1)

            lru_rows = (BH[:, 0:KC // 2, :], BL[:, 0:KC // 2, :])
            other_rows = (BH[:, KC // 2:KC, :], BL[:, KC // 2:KC, :])

            def pair_half(name, i, at, b, banks, rows):
                s = slot_of(name, i)
                if b == 0:
                    pe.wait_ge(w_ready, at + (FIRST[name] + 1))
                for k in range(KC // 2):
                    for n, (w, a) in enumerate(((WH, rows[0]), (WH, rows[1]), (WL, rows[0]))):
                        last = mm(banks[b], w[:, s, 2 * k + b, :], a[:, k, :], start=k == 0 and n == 0, stop=k == KC // 2 - 1 and n == 2)
                if b == 1:
                    last.then_inc(panel_done, 1)

            def lru_half(h):
                i, b = h // 2, h % 2
                if b == 0:
                    pe.wait_ge(freed["dve"], LETGO["wo2a"]["dve"] + i)
                pair_half("wo2a", i, i, b, (PJ[:, 0, 0, :], PJ[:, 1, 0, :]), lru_rows)

            enter("wo2a")
            df_step(14)
            turn_values(3)
            df_step(15)
            pe.wait_ge(b_lo, B_USE["m2"] + M2["lru"])
            lru_half(0)
            df_step(16)
            lru_half(1)
            df_step(17)
            pe.wait_ge(df_lt, 16)
            pe.wait_ge(df_pt, 16)
            sb_logits(0)
            lru_half(2)
            sb_logits(1)
            lru_half(3)
            pe.wait_ge(df_o, 16)
            pe.wait_ge(v2_ready, 4)
            for n in range(4):
                sb_tails(n)
                lru_half(4 + n)
                sb_out(n)
                if n == 1:
                    pe.wait_ge(oc_ready, 1)
                    pe.wait_ge(sb_sum, 6)
                    for c in range(2):
                        for b in range(QB):
                            last = nc.tensor.transpose(SIDE[c][:, b * P:(b + 1) * P], OC[:, b, c * P:(c + 1) * P], ident[:])
                        last.then_inc(oc_turned, 1)
                if n < 2:
                    sb_logits(n + 2)
                if n == 1:
                    pe.wait_ge(b_lo, B_USE["m2"] + M2["df1"])
            pe.wait_ge(b_lo, B_USE["m2"] + M2_PIECES)
            pe.wait_ge(freed["dve"], LETGO["wo2b"]["dve"])
            with pe.Fori(0, COUNT["wo2b"] // 2) as i:
                for j in range(2):
                    slot = slot_of("wo2b", j)
                    pe.wait_ge(freed["dve"], i * 2 + (LETGO["wo2b"]["dve"] - 1 + j))
                    for b in range(2):
                        pair_half("wo2b", j, i * 2 + j, b, (PJ[:, slot, 0, :], PJ[:, slot, 1, :]), other_rows)
            for g, (c0, n) in enumerate(GROUPS):
                stage(f"gv{g}", a_t, (a_lo, A_USE["n2"]), lead=(lambda: late_sum("n2")) if g == 0 else None)
                stage(f"ed{g}", b_t, (b_lo, B_USE[f"ff{g}"]), kc=n)
            late_sum("fin2")
            for b in range(QB):
                for k in range(KC):
                    pe.wait_ge(normed["fin2"], k + 1)
                    if b >= 2 and k == 0:
                        pe.wait_ge(out_ready, b - 1)
                    last = nc.tensor.transpose(PJ[:, b % 2, k // 4, k % 4 * P:(k % 4 + 1) * P], H[:, k, b * P:(b + 1) * P], ident[:])
                last.then_inc(out_turned, 1)

        @block.scalar
        def _(act):
            go = nc.scalar.activation
            for e, credit in ((freed["act"], CREDIT), (v_ready, 1), (pt_ready, 1), (y_ready, 1)):
                act.sem_inc(e, credit)

            def rows(at, tile, src, n):
                act.dma_start(VR[at:at + n, tile, :], src).then_inc(vec_loaded, 16)

            def flat(v):
                return v.rearrange("o (c p) -> (o c) p", p=P)

            for at, v in ((V_MIX, norm_mix_g), (V_FFN, norm_ffn_g), (V_N1, norm1_g), (V_CAB, conv_a_b), (V_BR, b_rgate),
                          (V_BI, b_igate), (V_LAM, lru_lambda), (V_N2, norm2_g)):
                rows(at, 0, flat(v), v.shape[1] // P)
            for at, v in ((V_FIN, norm_final_g), (V_FIN2, final_g)):
                rows(at, 0, v.rearrange("(c p) -> c p", p=P), KC)
            rows(V_CW, 0, conv_w.rearrange("o j (c p) -> (o j c) p", p=P), 3 * KC)
            rows(V_CAW, 0, conv_a_w.rearrange("o j (c p) -> (o j c) p", p=P), 4 * 4)
            taps = conv_ff_w.rearrange("o j (c p) -> (o j c) p", p=P)
            rows(0, 1, taps[0:4 * FFC], 4 * FFC)
            rows(0, 2, taps[4 * FFC:6 * FFC], 2 * FFC)
            rows(2 * FFC, 2, flat(conv_ff_b), 2 * FFC)
            act.dma_start(GSUB[:], subln_g[0].partition_broadcast(P)).then_inc(small_loaded, 16)
            for n, v in enumerate((lam_q1, lam_k1, lam_q2, lam_k2)):
                act.dma_start(LAMV[:, n, :], v[0].partition_broadcast(P)).then_inc(small_loaded, 16)

            act.wait_ge(vec_done, 1)
            for t, n in enumerate((V_ROWS, 4 * FFC, 4 * FFC)):
                last = go(VEC[:, t, 0:n], PB6[:, t * P:t * P + n], ACT.Copy)
            last.then_inc(vec_ready, 1)
            act.wait_ge(cl_ready, 1)
            go(small[:, 4:8], small[:, 0:4], ACT.Exp, scale=-1.0).then_inc(cl_exp, 1)
            act.wait_ge(lam_sum, 1)
            go(small[:, 42:44], small[:, 40:42], ACT.Exp).then_inc(lam_e, 1)
            for k in range(KC):
                act.wait_ge(xt_done, k + 1)
                go(H0[:, k, META:N], PJ[:, k % 2, 0, :], ACT.Copy)
                go(H0[:, k, 0:META], PJ[:, k % 2, 1, 0:META], ACT.Copy).then_inc(h0_ready, 1)
            act.wait_ge(h0_ready, KC)
            act.dma_start(h_scratch, H0[:, :, META:N]).then_inc(h_stored, 16)

            def norm(name, src, width, src_ready, split, per=1):
                for k in range(KC):
                    act.wait_ge(src_ready[0], src_ready[1] + k // per + 1)
                    if k >= 2:
                        act.wait_ge(ms_added[name], k - 1)
                    go(SQ[:, k % 2, 0:width], src[:, k, :], ACT.Square).then_inc(sq_ready[name], 1)
                act.wait_ge(ms_added[name], KC)
                ms = PX[:, :, 0:HALF] if width == N else PX[:, 0, 0:T]
                go(cols(RT[:, 0:width], width), ms, ACT.Sqrt, bias=eps_t[:], scale=1.0 / D).then_inc(rt_ready[name], 1)
                if split:
                    for k in range(KC):
                        act.wait_ge(normed[name], k + 1)
                        go(AH[:, k, 0:width], TN[:, k % 2, 0:width], ACT.Copy).then_inc(a_hi, 1)

            norm("mix", H0, N, (h0_ready, 0), True)

            def slot_of(name, i):
                return (FIRST[name] + i) % 2

            def after(name, at):
                act.wait_ge(panel_done, at + (FIRST[name] + 1))

            after("ki", 0)
            go(cols(KI[0:64, :], N), PJ[0:64, 0, :, 0:HALF], ACT.Copy).then_inc(ki_ready, 1)
            go(cols(WIT[64:72, :], N), PJ[64:72, 0, :, 0:HALF], ACT.Copy).then_inc(freed["act"], 1)
            act.wait_ge(ki_ready, 1)
            act.dma_start(KI[64:128, :], KI[0:64, :]).then_inc(ki_twin, 16)

            def copies(name, dst, wide=False):
                with act.Fori(0, COUNT[name] // 2) as i:
                    for j in range(2):
                        s = slot_of(name, j)
                        after(name, i * 2 + j)
                        if wide:
                            go(cols(dst(i * 2 + j), N), PJ[:, s, :, 0:HALF], ACT.Copy).then_inc(freed["act"], 1)
                        else:
                            go(dst(i * 2 + j), PJ[:, s, 0, :], ACT.Copy).then_inc(freed["act"], 1)

            copies("qi", lambda c: pick(QI, c))
            for n in range(QB * IDX_HEADS):
                b = n // IDX_HEADS
                act.wait_ge(idx_done, n + 1)
                if n >= 2:
                    act.wait_ge(score_step, n - 1)
                src = (PX_flat, PJ[:, 0].rearrange("p a n -> p (a n)"))[n % 2]
                go(RL[:, n % 2, 0:EXT[b]], src[:, 0:EXT[b]], ACT.Relu).then_inc(relu_done, 1)
            copies("q", lambda c: pick(QT, c))
            copies("k", lambda c: pick(KT, c), wide=True)
            with act.Fori(0, 4) as i:
                for j in range(2):
                    after("v", i * 2 + j)
                    go(cols(VTT[:, j, :], N), PJ[:, slot_of("v", j), :, 0:HALF], ACT.Copy).then_inc(freed["act"], 1)
                for j in range(2):
                    act.wait_ge(v_turned, i * 2 + (j + 1))
                    go(V[:, 0:4, bass.ds((i * 2 + j) * P, P)], PX[:, 0, :].rearrange("p (t d) -> p t d", t=4), ACT.Copy)
                    go(V[0:META, 4, bass.ds((i * 2 + j) * P, P)], PX[0:META, 1, 0:P], ACT.Copy).then_inc(v_ready, 1)
            copies("cu", lambda c: pick(U, c), wide=True)

            units = [(j, b) for j in range(2) for b in range(QB)]
            NU = len(units)
            act.wait_ge(h_stored, 16)
            with act.Fori(0, 4) as i:
                def stage_q(u):
                    j, b = units[u]
                    g = i * NU + u
                    if u >= 2:
                        act.wait_ge(qk_done, i * NU + (u - 1))
                    go(QS[:, u % 2], QT[:, bass.ds(i * 2 + j, 1), b * P:(b + 1) * P].rearrange("p o n -> p (o n)"),
                       ACT.Copy, scale=ATT_SCALE).then_inc(qs_ready, 1)

                stage_q(0)
                stage_q(1)
                for s in range(NU + 4):
                    j = s // 2
                    if s % 2 == 1 and j < 6 and j % 3 != 0:
                        act.wait_ge(panel_done, i * 6 + (FIRST["gates"] + j + 1))
                        go(pick(GA if j % 3 == 1 else GB, i * 2 + j // 3), PJ[:, slot_of("gates", j), 0, :],
                           ACT.Tanh, scale=0.5).then_inc(freed["act"], 1)
                    if 0 <= s - 3 < NU:
                        u = s - 3
                        act.wait_ge(y_turned, i * NU + (u + 1))
                        act.sem_inc(act_seen, 1)
                        go(QT[:, bass.ds(i * 2 + units[u][0], 1), units[u][1] * P:(units[u][1] + 1) * P].rearrange("p o n -> p (o n)"),
                           TURNED_Y[:, 0:P], ACT.Copy).then_inc(y_ready, 1)
                    if 0 <= s - 1 < NU:
                        u = s - 1
                        b = units[u][1]
                        act.wait_ge(p_turned, i * NU + (u + 1))
                        go(PT[:, u % 2, 0:(b + 1) * P], PB6[:, 0:(b + 1) * P], ACT.Copy)
                        go(PT[0:META, u % 2, 4 * P:5 * P], TAIL_P[0:META, 0:P], ACT.Copy).then_inc(pt_ready, 1)
                    if s < NU:
                        b = units[s][1]
                        act.wait_ge(max_ready, i * NU + (s + 1))
                        go(LT[:, s % 2, 0:EXT[b]], LT[:, s % 2, 0:EXT[b]], ACT.Exp, bias=NMX[:, s % 2:s % 2 + 1],
                           accum_out=RS[:, s % 2:s % 2 + 1]).then_inc(exp_done, 1)
                    if s + 2 < NU:
                        stage_q(s + 2)

            act.wait_ge(panel_done, FIRST["co"])
            act.wait_ge(freed["dve"], LETGO["co"]["dve"])
            for k in range(KC):
                go(AH[:, k, 0:T], U[:, k, META:N], ACT.Copy).then_inc(a_hi, 1)
            act.wait_ge(y_ready, 1 + HEADS * QB)
            for k in range(KC):
                go(BH[:, k], QT[:, k], ACT.Copy).then_inc(b_hi, 1)
            act.wait_ge(wr_cleared, 1)
            for g, w in enumerate((w_rgate, w_igate)):
                for r in range(2):
                    act.dma_start(WR[64 * r:64 * r + 64, g, :, 64 * r:64 * r + 64],
                                  w[0].rearrange("(c r) i o -> r i c o", r=2)[r]).then_inc(small_loaded, 16)
            with act.Fori(0, 4) as i:
                for j in range(2):
                    act.wait_ge(mixed_ready, i * 2 + (j + 1))
                    go(AH[:, bass.ds(i * 2 + j, 1), 0:T].rearrange("p o n -> p (o n)"), pick(GB, i * 2 + j), ACT.Copy).then_inc(a_hi, 1)

            def feed(norm_name, stage_name, gain, dst, hi, per=1):
                with act.Fori(0, KC // 2) as i:
                    for j in range(2):
                        c = i * 2 + j
                        if per == 1:
                            act.wait_ge(freed["dve"], c + (LETGO[stage_name]["dve"] + 1))
                        elif j == 0:
                            act.wait_ge(freed["dve"], i + (LETGO[stage_name]["dve"] + 1))
                        if dst is not None:
                            act.sem_inc(act_seen, 1)
                            go(chunk_of(dst, c), pick(H, c), ACT.Identity, bias=zero_t[:], scale=VEC[:, 0, bass.ds(c + gain, 1)]).then_inc(hi, 1)
                        act.wait_ge(ss_added[norm_name], c + 1)
                        act.sem_inc(act_seen, 1)
                        go(SQT[:, j], pick(H, c), ACT.Square).then_inc(sq_ready[norm_name], 1)

            def root(name):
                act.wait_ge(ss_summed[name], 1)
                go(ROOT[:], PX[:, 0, 0:T], ACT.Sqrt, bias=eps_t[:], scale=1.0 / D).then_inc(rt_ready[name], 1)

            feed("ffn", "wo", V_FFN, BH, b_hi)
            root("ffn")
            for g, (c0, n) in enumerate(GROUPS):
                name = f"gu{g}"
                with act.Fori(0, n // 2) as i:
                    for j in range(2):
                        q = i * 2 + j
                        act.wait_ge(gate_scaled, q + (c0 + 1))
                        go(SG[:, j], T1[:, j], ACT.Tanh, scale=0.5).then_inc(tanh_ready, 1)
                        act.wait_ge(ff_step, q + (c0 + 1))
                        act.sem_inc(act_seen, 1)
                        go(chunk_of(AH, q), T2[:, j], ACT.Copy).then_inc(a_hi, 1)
            norm("fin", H, T, (freed["dve"], LETGO["dn2"]["dve"]), False)
            norm("n1", H, T, (normed["fin"], 0), True)

            copies("dqk", lambda c: pick(DQK, c))

            def values(j):
                act.wait_ge(v2_turned, j + 1)
                c0 = (256, 256 + P, 0, P)[j]
                go(V2[:, :, c0:c0 + P], SIDE[j % 2].rearrange("p (t d) -> p t d", t=QB), ACT.Copy).then_inc(v2_ready, 1)

            def df_step(u):
                if u < len(DF_UNITS):
                    E = (DF_UNITS[u][1] + 1) * P
                    act.wait_ge(df_max, u + 1)
                    for m in range(2):
                        at = 2 * (u % 2) + m
                        go(L[:, u % 2, m, 0:E], L[:, u % 2, m, 0:E], ACT.Exp, bias=small[:, 48 + at:49 + at],
                           accum_out=small[:, 52 + at:53 + at]).then_inc(df_exp, 1)
                if u >= 2:
                    n, b = DF_UNITS[u - 2]
                    act.wait_ge(df_pv, u - 1)
                    go(OC[:, b, n * 64:(n + 1) * 64], PB7[:, 0:64], ACT.Copy).then_inc(df_o, 1)
                if 1 <= u <= len(DF_UNITS):
                    E = (DF_UNITS[u - 1][1] + 1) * P
                    act.wait_ge(df_turned, u)
                    go(PT2[:, (u - 1) % 2, 0:E], PB6[:, 0:E], ACT.Copy).then_inc(df_pt, 1)

            for j in range(2):
                after("dv", j)
                go(VT2[:, j], PJ[:, slot_of("dv", j), 0, :], ACT.Copy).then_inc(freed["act"], 1)
            values(0)
            places = {"xa": lambda c: XA[:, c, 3:T + 3], "ya": lambda c: YA[:, c], "sqk": lambda c: SQK[:, c], "sv": lambda c: VT2[:, c]}
            for s, (name, c) in enumerate(BESIDE):
                after(name, c)
                if name == "sv":
                    act.wait_ge(v2_turned, 2)
                go(places[name](c), PJ[:, slot_of(name, c), 0, :], ACT.Copy).then_inc(freed["act"], 1)
                if s == 0:
                    values(1)
                df_step(s)
                if name == "ya":
                    for g in range(2):
                        act.wait_ge(rg_done, 2 * c + g + 1)
                        go((RP, IP)[g][:, c], SIDE[g], ACT.Tanh, bias=small[:, 24 + 4 * g + c:25 + 4 * g + c], scale=0.5).then_inc(rg_tanh, 1)
                if 5 <= s < 9:
                    r = s - 5
                    act.wait_ge(rg_tanh, 2 * r + 2)
                    go(TH[:, r], RP[:, r], ACT.Tanh, bias=small[:, 20 + r:21 + r], scale=small[:, 20 + r:21 + r]).then_inc(lru_a, 1)
                    act.wait_ge(lru_a, 2 * r + 1)
                    go(RP[:, r], RP[:, r], ACT.Exp, bias=small[:, 16 + r:17 + r], scale=small[:, 16 + r:17 + r]).then_inc(lru_a, 1)
                if s == 10:
                    act.wait_ge(gelu_in, 2)
                    go(GY[:], GY[:], ACT.Tanh, scale=GELU_C).then_inc(gelu_t, 1)
                    act.wait_ge(lru_q, 4)
                    go(TH[:], TH[:], ACT.Sqrt, scale=0.25).then_inc(lru_root, 1)
            values(2)
            act.wait_ge(outa_ready, 1)
            go(BH[:, 0:4, :], XC[:], ACT.Copy).then_inc(b_hi, 1)

            def sb_hi(n):
                r, c = 64 * (n % 2), n // 2
                act.wait_ge(sb_pv, n + 1)
                go(BH[r:r + 64, 4 + c, :], SB_OUT[r:r + 64, :], ACT.Copy).then_inc(b_hi, 1)

            def sb_z(n):
                for m, (i0, o, w) in enumerate(SB_BANKS):
                    act.wait_ge(z_done, 3 * n + m + 1)
                    go(Z[:, n % 2, o:o + w], SB_Z[m][:, 0:w], ACT.Copy, scale=SB_SCALE).then_inc(z_ready, 1)
                act.wait_ge(z_ready, 3 * (n + 1))
                if n >= 1:
                    act.wait_ge(sb_log, n)
                go(LN[:], Z[:, n % 2], ACT.Abs).then_inc(act_step, 1)

            def sb_softplus(n):
                act.wait_ge(act_step, 2 * n + 1)
                go(LN[:], LN[:], ACT.Exp, scale=-1.0).then_inc(act_step, 1)
                act.wait_ge(act_step, 2 * n + 2)
                go(LN[:], LN[:], ACT.Ln, bias=ones[:, 0:1]).then_inc(sb_ln, 1)

            df_step(14)
            values(3)
            for u in (15, 16, 17):
                df_step(u)
            sb_z(0)
            sb_softplus(0)
            act.wait_ge(oc_sq, 1)
            go(small[:, 80:96], small[:, 64:80], ACT.Sqrt, bias=eps_t[:], scale=1.0 / 64).then_inc(oc_root, 1)
            sb_z(1)
            sb_softplus(1)
            for n in range(4):
                act.wait_ge(sb_sum, 3 * (n + 1))
                go(Z[:, n % 2], Z[:, n % 2], ACT.Exp).then_inc(sb_w, 1)
                sb_hi(n)
                if n == 1:
                    for c in range(2):
                        act.wait_ge(oc_turned, c + 1)
                        go(BH[:, 6 + c, :], SIDE[c], ACT.Copy).then_inc(b_hi, 1)
                if n < 2:
                    sb_z(n + 2)
                    sb_softplus(n + 2)

            feed("n2", "wo2b", V_N2, AH, a_hi, per=2)
            root("n2")
            for g, (c0, n) in enumerate(GROUPS):
                name = f"gv{g}"
                with act.Fori(0, n // 2) as i:
                    for j in range(2):
                        q = i * 2 + j
                        for m in range(2):
                            act.wait_ge(freed["dve"], i * 4 + (LETGO[name]["dve"] + 2 * j + m + 1))
                            act.sem_inc(act_seen, 1)
                            go(T1[:, 2 * j + m], US[:, 2 * j + m], ACT.Identity,
                               bias=VEC[:, 2, bass.ds(q + (2 * FFC + FFC * m + c0), 1)],
                               scale=VEC[:, 2, bass.ds(q + (FFC * m + c0), 1)]).then_inc(conv_base, 1)
                            if m == 0:
                                act.wait_ge(taps_done, i * 4 + (2 * c0 + 2 * j + 1))
                                go(SG[:, j], T1[:, 2 * j], ACT.Tanh, scale=0.5).then_inc(tanh_ready, 1)
                        act.wait_ge(ff_step, q + (FFC + c0 + 1))
                        go(pick(BH, q), T2[:, j], ACT.Copy).then_inc(b_hi, 1)
            feed("fin2", "ed2", None, None, None)
            root("fin2")
            for b in range(QB):
                act.wait_ge(out_turned, b + 1)
                go(OUT[:, b], PJ[:, b % 2].rearrange("p a n -> p (a n)"), ACT.Copy).then_inc(out_ready, 1)

        @block.vector
        def _(dve):
            ts, tt, stt = nc.vector.tensor_scalar, nc.vector.tensor_tensor, nc.vector.scalar_tensor_tensor
            for e, credit in ((freed["dve"], CREDIT), (logits_ready, 1), (ys_ready, 1)):
                dve.sem_inc(e, credit)
            steps = [0]

            def step(ins):
                ins.then_inc(dve_step, 1)
                steps[0] += 1

            def settled():
                dve.wait_ge(dve_step, steps[0])

            dve.wait_ge(consts_ready, 5)
            step(nc.vector.tensor_copy(DIST[:], DISTI[:]))
            settled()
            step(stt(out=DIST[:], in0=DIST[:], scalar=-1.0, in1=DIST[:], op0=ALU.mult, op1=ALU.max))
            dve.wait_ge(vec_ready, 1)
            lam = VEC[:, 0, V_LAM:V_LAM + 4]
            stt(out=small[:, 0:4], in0=lam, scalar=-1.0, in1=lam, op0=ALU.mult, op1=ALU.max).then_inc(cl_ready, 1)
            dve.wait_ge(small_loaded, 16 * 5)
            step(tt(LAMV[:, 0, :], LAMV[:, 0, :], LAMV[:, 1, :], ALU.mult))
            step(tt(LAMV[:, 2, :], LAMV[:, 2, :], LAMV[:, 3, :], ALU.mult))
            settled()
            nc.vector.tensor_reduce(small[:, 40:42], LAMV[:, 0:4:2, :], AX.X, ALU.add).then_inc(lam_sum, 1)
            dve.wait_ge(cl_exp, 1)
            e, z, z2, q = small[:, 4:8], small[:, 8:12], small[:, 12:16], small[:, 28:32]
            z = small[:, 32:36]
            z2 = small[:, 36:40]
            q = small[:, 8:12]
            step(ts(q, e, 2.0, None, ALU.add))
            settled()
            step(nc.vector.reciprocal(z, q))
            settled()
            step(tt(z, z, e, ALU.mult))
            settled()
            step(tt(z2, z, z, ALU.mult))
            settled()
            step(ts(q, z2, 1.0 / 15, None, ALU.mult))
            for m in (13, 11, 9, 7, 5, 3):
                settled()
                step(stt(out=q, in0=q, scalar=1.0 / m, in1=z2, op0=ALU.add, op1=ALU.mult))
            settled()
            step(stt(out=q, in0=q, scalar=1.0, in1=z, op0=ALU.add, op1=ALU.mult))
            step(ts(small[:, 12:16], lam, -1.0, 0.0, ALU.mult, ALU.max))
            settled()
            step(stt(out=q, in0=q, scalar=2.0, in1=small[:, 12:16], op0=ALU.mult, op1=ALU.add))
            settled()
            step(ts(small[:, 16:20], q, -4.0, None, ALU.mult))
            step(ts(small[:, 20:24], q, 4.0, None, ALU.mult))
            step(ts(small[:, 24:28], VEC[:, 0, V_BR:V_BR + 4], 0.5, None, ALU.mult))
            step(ts(small[:, 28:32], VEC[:, 0, V_BI:V_BI + 4], 0.5, None, ALU.mult))
            step(ts(GSUB[:], GSUB[:], 1.0 - LAM_INIT, None, ALU.mult))
            dve.wait_ge(lam_e, 1)
            step(tt(small[:, 44:45], small[:, 43:44], small[:, 42:43], ALU.subtract))
            settled()
            step(ts(small[:, 44:45], small[:, 44:45], LAM_INIT, None, ALU.subtract))
            settled()

            def norm(name, src, gain, width, split):
                dve.wait_ge(rt_ready[name], 1)
                nc.vector.reciprocal(RSTD[:, 0:width], RT[:, 0:width]).then_inc(rstd_ready[name], 1)
                dve.wait_ge(rstd_ready[name], 1)
                for k in range(KC + 1):
                    if k < KC:
                        dst = TN[:, k % 2, 0:width] if split else src[:, k, :]
                        if split and k >= 2:
                            dve.wait_ge(a_lo, A_USE[name] + k - 1)
                        stt(out=dst, in0=src[:, k, :], scalar=VEC[:, 0, gain + k:gain + k + 1], in1=RSTD[:, 0:width],
                            op0=ALU.mult, op1=ALU.mult).then_inc(normed[name], 1)
                    if k >= 1 and split:
                        dve.wait_ge(a_hi, A_USE[name] + k)
                        tt(AL[:, k - 1, 0:width], TN[:, (k - 1) % 2, 0:width], AH[:, k - 1, 0:width].bitcast(F32),
                           ALU.subtract).then_inc(a_lo, 1)

            norm("mix", H0, V_MIX, N, True)

            def slot_of(name, i):
                return (FIRST[name] + i) % 2

            def after(name, at):
                dve.wait_ge(panel_done, at + (FIRST[name] + 1))

            dve.wait_ge(wq_done, 1)
            ts(WQ[:].rearrange("p b h -> p (b h)"), PB6[:, 0:QB * IDX_HEADS], IDX_SCALE, None, ALU.mult).then_inc(wq_ready, 1)
            dve.wait_ge(wq_ready, 1)
            for b in range(QB):
                sc = S[:, b, PADS:PADS + EXT[b]]
                for h in range(IDX_HEADS):
                    n = b * IDX_HEADS + h
                    dve.wait_ge(relu_done, n + 1)
                    if h == 0:
                        ts(sc, RL[:, n % 2, 0:EXT[b]], WQ[:, b, h:h + 1], None, ALU.mult).then_inc(score_step, 1)
                    else:
                        dve.wait_ge(score_step, n)
                        stt(out=sc, in0=RL[:, n % 2, 0:EXT[b]], scalar=WQ[:, b, h:h + 1], in1=sc,
                            op0=ALU.mult, op1=ALU.add).then_inc(score_step, 1)
            dve.wait_ge(score_step, QB * IDX_HEADS)
            for b in range(QB):
                own = S[:, b, PADS + EXT[b] - P:PADS + EXT[b]]
                tt(own, own, hide[:], ALU.add).then_inc(topk_step, 1)
                nc.vector.memset(S[:, b, 0:PADS], SENTINEL).then_inc(topk_step, 1)
            for b in range(QB):
                base = 2 * QB + b * 2 * ROUNDS
                row = S[:, b, 0:PADS + EXT[b]]
                with dve.Fori(0, ROUNDS) as i:
                    dve.wait_ge(topk_step, i * 2 + base)
                    dve.sem_inc(dve_seen, 1)
                    nc.vector.max(MX8[:], row).then_inc(topk_step, 1)
                    dve.wait_ge(topk_step, i * 2 + (base + 1))
                    dve.sem_inc(dve_seen, 1)
                    nc.vector.match_replace(row, MX8[:], row, TAKEN).then_inc(topk_step, 1)
            dve.wait_ge(topk_step, 2 * QB * (1 + ROUNDS // 1))
            for b in range(QB):
                m = S[:, b, PADS:PADS + EXT[b]]
                ts(m, m, TAKEN / 1.5, HIDDEN, ALU.is_gt, ALU.mult).then_inc(mask_ready, 1)
            dve.wait_ge(mask_ready, QB)
            for b in range(QB):
                own = S[:, b, PADS + EXT[b] - P:PADS + EXT[b]]
                tt(own, own, hide[:], ALU.min).then_inc(mask_ready, 1)

            dve.wait_ge(freed["act"], LETGO["cc"]["act"])
            with dve.Fori(0, 4) as i:
                for j in range(2):
                    after("cc", i * 2 + j)
                    u = cols(pick(U, i * 2 + j), N)
                    tt(u, u, PJ[:, slot_of("cc", j), :, 0:HALF], ALU.mult).then_inc(freed["dve"], 1)

            dve.wait_ge(mask_ready, 2 * QB)
            dve.wait_ge(freed["dve"], LETGO["gates"]["dve"])
            units = [(j, b) for j in range(2) for b in range(QB)]
            NU = len(units)
            with dve.Fori(0, 4) as i:
                def conv(j):
                    c = i * 2 + j
                    def tap(t):
                        return VEC[:, 0, bass.ds(c + (V_CW + t * KC), 1)]
                    def seen(t):
                        return U[:, bass.ds(c, 1), META - 2 + t:N - 2 + t].rearrange("p o n -> p (o n)")
                    dve.wait_ge(freed["dve"], i * 2 + (LETGO["gates"]["dve"] - 1 + j))
                    ts(CT[:, j], seen(2), tap(2), None, ALU.mult).then_inc(conv_step, 1)
                    for t in (1, 0):
                        dve.wait_ge(conv_step, i * 6 + (3 * j + 2 - t))
                        stt(out=CT[:, j], in0=seen(t), scalar=tap(t), in1=CT[:, j], op0=ALU.mult, op1=ALU.add).then_inc(conv_step, 1)

                for s in range(NU + 2):
                    if s in (1, 7):
                        j = s // 6
                        after("gates", i * 6 + 3 * j)
                        dve.wait_ge(conv_step, i * 6 + 3 * (j + 1))
                        tt(U[:, bass.ds(i * 2 + j, 1), META:N].rearrange("p o n -> p (o n)"), CT[:, j],
                           PJ[:, slot_of("gates", 3 * j), 0, :], ALU.mult).then_inc(freed["dve"], 1)
                    if 0 <= s - 1 < NU:
                        u = s - 1
                        dve.wait_ge(exp_done, i * NU + (u + 1))
                        nc.vector.reciprocal(RINV[:, u % 4:u % 4 + 1], RS[:, u % 2:u % 2 + 1]).then_inc(rinv_ready, 1)
                    if 0 <= s - 2 < NU:
                        u = s - 2
                        dve.wait_ge(rinv_ready, i * NU + (u + 1))
                        dve.wait_ge(pv_done, i * NU + (u + 1))
                        ts(YS[:, u % 2], PB7[:, 0:P], RINV[:, u % 4:u % 4 + 1], None, ALU.mult).then_inc(ys_ready, 1)
                    if s < NU:
                        b = units[s][1]
                        dve.wait_ge(qk_done, i * NU + (s + 1))
                        tt(LT[:, s % 2, 0:EXT[b]], PX_flat[:, 0:EXT[b]], S[:, b, PADS:PADS + EXT[b]], ALU.add).then_inc(logits_ready, 1)
                        dve.wait_ge(logits_ready, i * NU + (s + 2))
                        nc.vector.tensor_reduce(NMX[:, s % 2:s % 2 + 1], LT[:, s % 2, 0:EXT[b]], AX.X, ALU.max, negate=True).then_inc(max_ready, 1)
                    if s in (0, 5):
                        conv(s // 5)

            for k in range(KC):
                dve.wait_ge(a_hi, A_USE["conv"] + k + 1)
                tt(AL[:, k, 0:T], U[:, k, META:N], AH[:, k, 0:T].bitcast(F32), ALU.subtract).then_inc(a_lo, 1)
            for k in range(KC):
                dve.wait_ge(b_hi, B_USE["y"] + k + 1)
                tt(BL[:, k], QT[:, k], BH[:, k].bitcast(F32), ALU.subtract).then_inc(b_lo, 1)
            dve.wait_ge(b_lo, B_USE["y"] + KC)
            nc.vector.memset(WR[:], 0.0).then_inc(wr_cleared, 1)
            step(nc.vector.memset(XA[:, :, 0:3], 0.0))

            with dve.Fori(0, 4) as i:
                for j in range(2):
                    after("co", i * 2 + j)
                    g = pick(GB, i * 2 + j)
                    stt(out=g, in0=g, scalar=1.0, in1=PJ[:, slot_of("co", j), 0, :], op0=ALU.add, op1=ALU.mult).then_inc(freed["dve"], 1)
            with dve.Fori(0, 4) as i:
                for j in range(2):
                    c = i * 2 + j
                    after("ao", c)
                    ga, gb = pick(GA, c), pick(GB, c)
                    stt(out=ga, in0=ga, scalar=1.0, in1=PJ[:, slot_of("ao", j), 0, :], op0=ALU.add, op1=ALU.mult).then_inc(freed["dve"], 1)
                    dve.wait_ge(freed["dve"], c + (LETGO["ao"]["dve"] + 1))
                    tt(gb, ga, gb, ALU.add).then_inc(mixed_ready, 1)
                    dve.wait_ge(a_hi, c + (A_USE["mixed"] + 1))
                    tt(AL[:, bass.ds(c, 1), 0:T].rearrange("p o n -> p (o n)"), gb,
                       AH[:, bass.ds(c, 1), 0:T].rearrange("p o n -> p (o n)").bitcast(F32), ALU.subtract).then_inc(a_lo, 1)

            def begin(norm_name):
                dve.sem_inc(ss_added[norm_name], 1)
                nc.vector.memset(SS[:], 0.0).then_inc(ss_added[norm_name], 1)

            def feed(norm_name, c, j, gain, hi_dst, lo_dst, hi, lo, use):
                if hi_dst is not None:
                    dve.wait_ge(hi, c + (use + 1))
                    stt(out=chunk_of(lo_dst, c), in0=pick(H, c), scalar=VEC[:, 0, bass.ds(c + gain, 1)], in1=chunk_of(hi_dst, c).bitcast(F32),
                        op0=ALU.mult, op1=ALU.subtract).then_inc(lo, 1)
                dve.wait_ge(sq_ready[norm_name], c + 1)
                dve.wait_ge(ss_added[norm_name], c + 2)
                tt(SS[:], SS[:], SQT[:, j], ALU.add).then_inc(ss_added[norm_name], 1)

            def residual(name, scale, to=None):
                if to:
                    begin(to[0])
                with dve.Fori(0, COUNT[name] // 2) as i:
                    for j in range(2):
                        after(name, i * 2 + j)
                        h = pick(H, i * 2 + j)
                        stt(out=h, in0=PJ[:, slot_of(name, j), 0, :], scalar=scale, in1=h, op0=ALU.mult, op1=ALU.add).then_inc(freed["dve"], 1)
                        if to:
                            feed(to[0], i * 2 + j, j, *to[1:])

            def late_scale(name):
                dve.wait_ge(rt_ready[name], 1)
                nc.vector.reciprocal(R[:], ROOT[:]).then_inc(rstd_ready[name], 1)
                dve.wait_ge(rstd_ready[name], 1)

            dve.wait_ge(h_loaded, 16)
            residual("wo", 0.5, ("ffn", V_FFN, BH, BL, b_hi, b_lo, B_USE["ffn"]))
            late_scale("ffn")
            for g, (c0, n) in enumerate(GROUPS):
                name = f"gu{g}"
                with dve.Fori(0, n // 2) as i:
                    for j in range(2):
                        q = i * 2 + j
                        after(name, i * 4 + 2 * j)
                        dve.wait_ge(a_lo, q + (A_USE[f"act{g}"] - 1))
                        tt(T1[:, j], PJ[:, slot_of(name, 0), 0, :], R[:], ALU.mult).then_inc(freed["dve"], 1)
                        dve.wait_ge(freed["dve"], i * 4 + (LETGO[name]["dve"] + 2 * j + 1))
                        dve.sem_inc(gate_scaled, 1)
                        after(name, i * 4 + (2 * j + 1))
                        tt(T2[:, j], PJ[:, slot_of(name, 1), 0, :], R[:], ALU.mult).then_inc(freed["dve"], 1)
                        dve.wait_ge(tanh_ready, q + (c0 + 1))
                        stt(out=T1[:, j], in0=SG[:, j], scalar=1.0, in1=T1[:, j], op0=ALU.add, op1=ALU.mult).then_inc(silu_ready, 1)
                        dve.wait_ge(silu_ready, q + (c0 + 1))
                        dve.wait_ge(freed["dve"], i * 4 + (LETGO[name]["dve"] + 2 * j + 2))
                        tt(T2[:, j], T1[:, j], T2[:, j], ALU.mult).then_inc(ff_step, 1)
                        dve.wait_ge(a_hi, q + (A_USE[f"act{g}"] + 1))
                        tt(chunk_of(AL, q), T2[:, j], chunk_of(AH, q).bitcast(F32), ALU.subtract).then_inc(a_lo, 1)
                residual(f"dn{g}", 0.5)
            norm("fin", H, V_FIN, T, False)
            dve.wait_ge(normed["fin"], KC)
            norm("n1", H, V_N1, T, True)

            def df_step(u):
                if u < len(DF_UNITS):
                    n, b = DF_UNITS[u]
                    E = (b + 1) * P
                    if b == 0:
                        step(ts(BIAS[:], DIST[:], -SLOPES[n], None, ALU.mult))
                        settled()
                        step(nc.vector.memset(BIAS[0:64, T - 64:T], HIDDEN))
                        settled()
                    at = 48 + 2 * (u % 2)
                    l = L[:, u % 2, :, 0:E]
                    dve.wait_ge(df_qk, u + 1)
                    stt(out=l, in0=PX[:, :, 0:E], scalar=DF_SCALE, in1=BIAS[:, T - E:T].unsqueeze(1).to_broadcast([P, 2, E]),
                        op0=ALU.mult, op1=ALU.add).then_inc(df_lt, 1)
                    dve.wait_ge(df_lt, u + 1)
                    nc.vector.tensor_reduce(small[:, at:at + 2], l, AX.X, ALU.max, negate=True).then_inc(df_max, 1)
                if 1 <= u <= len(DF_UNITS):
                    v = u - 1
                    E = (DF_UNITS[v][1] + 1) * P
                    at = 2 * (v % 2)
                    l1, l2 = L[:, v % 2, 0, 0:E], L[:, v % 2, 1, 0:E]
                    r1, r2 = small[:, 56 + at:57 + at], small[:, 57 + at:58 + at]
                    dve.wait_ge(df_exp, 2 * v + 2)
                    step(nc.vector.reciprocal(small[:, 56 + at:58 + at], small[:, 52 + at:54 + at]))
                    settled()
                    step(tt(r2, r2, small[:, 44:45], ALU.mult))
                    step(ts(l1, l1, r1, None, ALU.mult))
                    settled()
                    stt(out=l1, in0=l2, scalar=r2, in1=l1, op0=ALU.mult, op1=ALU.add).then_inc(df_p, 1)

            def conv_a(c):
                def tap(t):
                    return VEC[:, 0, V_CAW + 4 * t + c:V_CAW + 4 * t + c + 1]
                dve.wait_ge(freed["act"], LETGO["xa"]["act"] + c + 1)
                step(ts(XC[:, c], XA[:, c, 3:T + 3], tap(3), VEC[:, 0, V_CAB + c:V_CAB + c + 1], ALU.mult, ALU.add))
                for t in (2, 1, 0):
                    settled()
                    ins = stt(out=XC[:, c], in0=XA[:, c, t:T + t], scalar=tap(t), in1=XC[:, c], op0=ALU.mult, op1=ALU.add)
                    if t:
                        step(ins)
                    else:
                        ins.then_inc(xc_ready, 1)

            def gelu_inner(h):
                y, g = YA[:, 2 * h:2 * h + 2], GY[:, 2 * h:2 * h + 2]
                dve.wait_ge(freed["act"], LETGO["ya"]["act"] + 2 * h + 2)
                step(tt(g, y, y, ALU.mult))
                settled()
                step(ts(g, g, 0.044715, 1.0, ALU.mult, ALU.add))
                settled()
                tt(g, g, y, ALU.mult).then_inc(gelu_in, 1)

            def decay(c):
                dve.wait_ge(lru_a, 2 * c + 2)
                step(tt(A2[:, c % 2], RP[:, c], RP[:, c], ALU.mult))
                settled()
                stt(out=TH[:, c], in0=A2[:, c % 2], scalar=1.0, in1=TH[:, c], op0=ALU.add, op1=ALU.mult).then_inc(lru_q, 1)
                dve.wait_ge(xc_ready, c + 1)
                dve.wait_ge(lru_q, c + 1)
                step(stt(out=IP[:, c], in0=IP[:, c], scalar=1.0, in1=XC[:, c], op0=ALU.add, op1=ALU.mult))

            def recurrence():
                dve.wait_ge(lru_root, 1)
                settled()
                step(tt(IP[:], IP[:], TH[:], ALU.mult))
                settled()
                for c in range(4):
                    step(nc.vector.tensor_tensor_scan(XC[:, c], RP[:, c], IP[:, c], 0.0, ALU.mult, ALU.add))

            for s in range(len(BESIDE)):
                df_step(s)
                if 1 <= s < 5:
                    conv_a(s - 1)
                if 6 <= s < 10:
                    if s == 6:
                        dve.wait_ge(v2_turned, 2)
                    decay(s - 6)
                if s in (7, 9):
                    gelu_inner((s - 7) // 2)
                if s == 11:
                    dve.wait_ge(gelu_t, 1)
                    step(stt(out=GY[:], in0=GY[:], scalar=1.0, in1=YA[:], op0=ALU.add, op1=ALU.mult))
                if s == 12:
                    recurrence()
                if s == 13:
                    settled()
                    stt(out=XC[:], in0=XC[:], scalar=0.5, in1=GY[:], op0=ALU.mult, op1=ALU.mult).then_inc(outa_ready, 1)

            def sb_lo(n):
                r, c = 64 * (n % 2), n // 2
                dve.wait_ge(b_hi, B_USE["m2"] + M2[f"sb{n}"])
                tt(BL[r:r + 64, 4 + c, :], SB_OUT[r:r + 64, :], BH[r:r + 64, 4 + c, :].bitcast(F32), ALU.subtract).then_inc(b_lo, 1)

            def lru_residual(i):
                after("wo2a", i)
                tt(H[:, 2 * i], PJ[:, 0, 0, :], H[:, 2 * i], ALU.add)
                tt(H[:, 2 * i + 1], PJ[:, 1, 0, :], H[:, 2 * i + 1], ALU.add).then_inc(freed["dve"], 1)

            def sb_floor(n):
                dve.wait_ge(z_ready, 3 * (n + 1))
                step(ts(LG[:], Z[:, n % 2], 0.0, None, ALU.max))

            def sb_logs(n):
                settled()
                dve.wait_ge(sb_ln, n + 1)
                step(stt(out=LG[:], in0=LG[:], scalar=-1.0, in1=LN[:], op0=ALU.mult, op1=ALU.subtract))
                settled()
                for i in range(QB):
                    last = tt(LG[:, SBO[i]:SBO[i] + P], LG[:, SBO[i]:SBO[i] + P], before[:], ALU.mult)
                last.then_inc(sb_log, 1)

            oc = OC[:].rearrange("p b (n d) -> p (b n) d", d=64)
            osq = OSQ[:].rearrange("p b (n d) -> p (b n) d", d=64)

            df_step(14)
            dve.wait_ge(b_hi, B_USE["m2"] + M2["lru"])
            tt(BL[:, 0:4, :], XC[:], BH[:, 0:4, :].bitcast(F32), ALU.subtract).then_inc(b_lo, 1)
            df_step(15)
            df_step(16)
            lru_residual(0)
            sb_floor(0)
            sb_logs(0)
            dve.wait_ge(df_o, len(DF_UNITS))
            dve.wait_ge(v2_turned, 4)
            step(tt(osq, oc, oc, ALU.mult))
            settled()
            nc.vector.tensor_reduce(small[:, 64:80], osq, AX.X, ALU.add).then_inc(oc_sq, 1)
            lru_residual(1)
            for n in range(4):
                z = Z[:, n % 2]
                for m, (i0, o, w) in enumerate(SB_BANKS):
                    dve.wait_ge(tail_done, 3 * n + m + 1)
                    tt(z[:, o:o + w], SB_TAIL[m][:, 0:w], z[:, o:o + w], ALU.add).then_inc(sb_sum, 1)
                if n < 3:
                    sb_floor(n + 1)
                dve.wait_ge(sb_w, n + 1)
                for i in range(QB):
                    last = tt(z[:, SBO[i]:SBO[i] + P], z[:, SBO[i]:SBO[i] + P], before[:], ALU.mult)
                last.then_inc(sb_masked, 1)
                if n < 3:
                    sb_logs(n + 1)
                if n == 0:
                    dve.wait_ge(oc_root, 1)
                    step(nc.vector.reciprocal(small[:, 96:112], small[:, 80:96]))
                    settled()
                    step(tt(oc, oc, small[:, 96:112].unsqueeze(2).to_broadcast([P, 16, 64]), ALU.mult))
                sb_lo(n)
                if n == 0:
                    settled()
                    tt(oc, oc, GSUB[:].unsqueeze(1).to_broadcast([P, 16, 64]), ALU.mult).then_inc(oc_ready, 1)
                if n % 2 == 1:
                    lru_residual(2 + n // 2)
                if n == 1:
                    for c in range(2):
                        dve.wait_ge(b_hi, B_USE["m2"] + M2[f"df{c}"])
                        tt(BL[:, 6 + c, :], SIDE[c], BH[:, 6 + c, :].bitcast(F32), ALU.subtract).then_inc(b_lo, 1)

            begin("n2")
            with dve.Fori(0, COUNT["wo2b"] // 2) as i:
                for j in range(2):
                    after("wo2b", i * 2 + j)
                    h = H[:, bass.ds(i * 4 + 2 * j, 2), :]
                    tt(h, PJ[:, slot_of("wo2b", j)], h, ALU.add).then_inc(freed["dve"], 1)
                    for b in range(2):
                        feed("n2", i * 4 + (2 * j + b), b, V_N2, AH, AL, a_hi, a_lo, A_USE["n2"])
            late_scale("n2")
            for g, (c0, n) in enumerate(GROUPS):
                name = f"gv{g}"
                with dve.Fori(0, n // 2) as i:
                    for j in range(2):
                        q = i * 2 + j
                        dve.wait_ge(b_lo, q + (B_USE[f"ff{g}"] - 1))
                        for m in range(2):
                            t1, us = T1[:, 2 * j + m], US[:, 2 * j + m]
                            after(name, i * 4 + (2 * j + m))
                            tt(us, PJ[:, slot_of(name, m), 0, :], R[:], ALU.mult).then_inc(freed["dve"], 1)
                            dve.wait_ge(conv_base, i * 4 + (2 * c0 + 2 * j + m + 1))
                            stt(out=t1[:, 1:T], in0=us[:, 0:T - 1], scalar=VEC[:, 1, bass.ds(q + (2 * FFC + FFC * m + c0), 1)],
                                in1=t1[:, 1:T], op0=ALU.mult, op1=ALU.add).then_inc(conv_step, 1)
                            dve.wait_ge(conv_step, i * 4 + (24 + 2 * c0 + 2 * j + m + 1))
                            stt(out=t1[:, 2:T], in0=us[:, 0:T - 2], scalar=VEC[:, 1, bass.ds(q + (FFC * m + c0), 1)],
                                in1=t1[:, 2:T], op0=ALU.mult, op1=ALU.add).then_inc(taps_done, 1)
                        dve.wait_ge(tanh_ready, q + (FFC + c0 + 1))
                        stt(out=SG[:, j], in0=SG[:, j], scalar=1.0, in1=T1[:, 2 * j], op0=ALU.add, op1=ALU.mult).then_inc(silu_ready, 1)
                        dve.wait_ge(silu_ready, q + (FFC + c0 + 1))
                        dve.wait_ge(taps_done, i * 4 + (2 * c0 + 2 * j + 2))
                        tt(T2[:, j], SG[:, j], T1[:, 2 * j + 1], ALU.mult).then_inc(ff_step, 1)
                        dve.wait_ge(b_hi, q + (B_USE[f"ff{g}"] + 1))
                        tt(pick(BL, q), T2[:, j], pick(BH, q).bitcast(F32), ALU.subtract).then_inc(b_lo, 1)
                residual(f"ed{g}", 0.5, ("fin2", None, None, None, None, None, None) if g == 2 else None)
            late_scale("fin2")
            for k in range(KC):
                stt(out=H[:, k, :], in0=H[:, k, :], scalar=VEC[:, 0, V_FIN2 + k:V_FIN2 + k + 1], in1=R[:],
                    op0=ALU.mult, op1=ALU.mult).then_inc(normed["fin2"], 1)


_INS = ["x", "meta_tokens", "norm_mix_g", "w_in", "w_attn_out", "conv_w", "w_conv_out", "w_out", "norm_ffn_g", "w_gate",
        "w_up", "w_down", "norm_final_g", "norm1_g_2", "w_in_2", "conv_a_w_2", "conv_a_b_2", "w_rgate_2", "b_rgate_2",
        "w_igate_2", "b_igate_2", "lru_lambda_2", "lam_q1_2", "lam_k1_2", "lam_q2_2", "lam_k2_2", "subln_g_2",
        "w_out_2", "norm2_g_2", "w_ff_up_2", "conv_ff_w_2", "conv_ff_b_2", "w_ff_down_2", "final_g_2"]


def kernel(**inputs):
    import concourse.bacc as _bacc
    from concourse.bass_utils import run_bass_kernel_spmd as _run

    nc = _bacc.Bacc("TRN2", target_bir_lowering=False, num_devices=1)
    arrays, args = {}, []
    for name in _INS:
        a = np.ascontiguousarray(inputs[name])
        arrays[f"in_{name}_dram"] = a
        args.append(nc.dram_tensor(f"in_{name}_dram", a.shape, mybir.dt.from_np(a.dtype), kind="ExternalInput").ap())
    args.append(nc.dram_tensor("out_0_dram", (1, T, D), F32, kind="ExternalOutput").ap())
    two_blocks(nc, *args)
    r = _run(nc, [arrays], core_ids=[0])
    return r.results[0]["out_0_dram"]
```

```python
from contextlib import ExitStack

import numpy as np
import concourse.bass as bass
from concourse import mybir

F32 = mybir.dt.float32
F32R = mybir.dt.float32r
I32 = mybir.dt.int32
ALU = mybir.AluOpType
ACT = mybir.ActivationFunctionType
AX = mybir.AxisListType

P = 128
D = 1024
KC = D // P
T = 512
META = 16
N = T + META
HALF = N // 2
BANK = 512
QB = T // P
HEADS = 8
IDX_HEADS, IDX_DIM = 8, 64
TOPK = min(256, N // 4)
PADS = -TOPK % 8
ROUNDS = (TOPK + PADS) // 8
IDX_SCALE = (IDX_HEADS ** -0.5) * (IDX_DIM ** -0.5)
ATT_SCALE = P ** -0.5
EPS = 1e-6
FF = 2816
FFC = FF // P
GROUPS = [(0, 8), (8, 8), (16, 6)]
DF_SCALE = 32 ** -0.5
SB_SCALE = 64 ** -0.5
LAM_INIT = 0.8 - 0.6 * float(np.exp(-0.3 * 0))
SLOPES = [2.0 ** (-8.0 * (h + 1) / 4) for h in range(4)]
GELU_C = float(np.sqrt(2.0 / np.pi))
HIDDEN = -1e30
TAKEN = -3e38
SENTINEL = 3e38

C_Q, C_K, C_V, C_QI, C_KI, C_CU, C_CB, C_CC, C_GA, C_GB = 0, 1024, 2048, 3072, 3584, 3656, 4680, 5704, 6728, 7752

STAGES = [("ki", 1, "act"), ("qi", 4, "act"), ("q", 8, "act"), ("k", 8, "act"), ("v", 8, "act"),
          ("cu", 8, "act"), ("cc", 8, "dve"), ("gates", 24, "both"), ("co", 8, "dve"), ("ao", 8, "dve"), ("wo", 8, "dve"),
          ("gu0", 16, "dve"), ("dn0", 8, "dve"), ("gu1", 16, "dve"), ("dn1", 8, "dve"), ("gu2", 12, "dve"), ("dn2", 8, "dve"),
          ("dqk", 4, "dve"), ("dv", 2, "dve"), ("xa", 4, "dve"), ("ya", 4, "dve"), ("sqk", 4, "dve"), ("sv", 2, "dve"),
          ("wo2a", 4, "dve"), ("wo2b", 4, "dve"),
          ("gv0", 16, "dve"), ("ed0", 8, "dve"), ("gv1", 16, "dve"), ("ed1", 8, "dve"), ("gv2", 12, "dve"), ("ed2", 8, "dve")]
FIRST, COUNT, OWNER, LETGO = {}, {}, {}, {}
CREDIT = 2
_p, _n = 0, {"act": CREDIT, "dve": CREDIT}
for _name, _count, _owner in STAGES:
    FIRST[_name], COUNT[_name], OWNER[_name] = _p, _count, _owner
    LETGO[_name] = dict(_n)
    if _owner == "both":
        _n["dve"] += _count // 3
        _n["act"] += _count * 2 // 3
    else:
        _n[_owner] += _count
    _p += _count
PANELS = _p
ORDER = [s[0] for s in STAGES]
RAW_SLOTS, W_SLOTS = 4, 2

BESIDE = [(n, c) for n, k in (("xa", 4), ("ya", 4), ("sqk", 4), ("sv", 2)) for c in range(k)]
DF_UNITS = [(n, b) for n in range(4) for b in range(QB)]

EXT = [META + P * (b + 1) for b in range(QB)]
SBW = [T - P * i for i in range(QB)]
SBO = [sum(SBW[:i]) for i in range(QB)]
SBT = sum(SBW)
SB_BANKS = [(0, SBO[0], SBW[0]), (1, SBO[1], SBW[1]), (2, SBO[2], SBW[2] + SBW[3])]

V_MIX, V_CW, V_FFN, V_FIN, V_N1, V_CAW, V_CAB, V_BR, V_BI, V_LAM, V_N2, V_FIN2, V_ROWS = 0, 8, 32, 40, 48, 56, 72, 76, 80, 84, 88, 96, 104


def two_blocks(nc, x, meta_tokens, norm_mix_g, w_in, w_attn_out, conv_w, w_conv_out, w_out, norm_ffn_g, w_gate,
               w_up, w_down, norm_final_g, norm1_g, w_in_2, conv_a_w, conv_a_b, w_rgate, b_rgate,
               w_igate, b_igate, lru_lambda, lam_q1, lam_k1, lam_q2, lam_k2, subln_g,
               w_out_2, norm2_g, w_ff_up, conv_ff_w, conv_ff_b, w_ff_down, final_g, out):
    with ExitStack() as ctx:
        def sem(name):
            return ctx.enter_context(nc.semaphore(name))

        top = [(nc.sbuf_base + 63) // 64 * 64]

        def region(nbytes):
            at = top[0]
            top[0] += (nbytes + 31) // 32 * 32
            return [at, top[0]]

        def place(reg, name, shape, dt=F32):
            nbytes = int(np.prod(shape[1:])) * 4
            t = nc.alloc_sbuf_tensor_at(name, shape, dt, offset=reg[0])
            reg[0] += (nbytes + 31) // 32 * 32
            assert reg[0] <= reg[1], (name, reg)
            return t

        def again(reg, start):
            return [start, reg[1]]

        def solo(name, shape, dt=F32):
            return place(region(int(np.prod(shape[1:])) * 4), name, shape, dt)

        r_weights = region(4 * (RAW_SLOTS + 2 * W_SLOTS) * KC * P)
        RAW = place(r_weights, "RAW", [P, RAW_SLOTS, KC, P])
        WH = place(r_weights, "WH", [P, W_SLOTS, KC, P], F32R)
        WL = place(r_weights, "WL", [P, W_SLOTS, KC, P], F32R)
        ident = solo("ident", [P, P])
        ones = solo("ones", [P, P])
        tri = solo("tri", [P, P])
        before = solo("before", [P, P])
        hide = solo("hide", [P, P])
        VEC = solo("VEC", [P, 3, P])
        eps_t = solo("eps_t", [P, 1])
        zero_t = solo("zero_t", [P, 1])
        eps2_t = solo("eps2_t", [P, 1])
        GF1 = solo("GF1", [P, KC])
        WQ = solo("WQ", [P, QB, IDX_HEADS])
        MX8 = solo("MX8", [P, 8])
        NMX = solo("NMX", [P, 2])
        RS = solo("RS", [P, 2])
        RINV = solo("RINV", [P, 4])
        small = solo("small", [P, 128])
        DIST = solo("DIST", [P, T])
        GSUB = solo("GSUB", [P, 64])
        LAMV = solo("LAMV", [P, 4, 32])

        r_a = region(2 * 4 * KC * N)
        a0 = r_a[0]
        AH = place(r_a, "AH", [P, KC, N], F32R)
        AL = place(r_a, "AL", [P, KC, N], F32R)
        ra2 = again(r_a, a0)
        Z = place(ra2, "Z", [P, 2, SBT])
        LN = place(ra2, "LN", [P, SBT])
        LG = place(ra2, "LG", [P, SBT])
        ra3 = again(r_a, a0)
        RP = place(ra3, "RP", [P, 4, T])
        IP = place(ra3, "IP", [P, 4, T])
        TH = place(ra3, "TH", [P, 4, T])


        r_b = region(4 * (HEADS * N + 5 * D))
        b0 = r_b[0]
        KT = place(r_b, "KT", [P, HEADS, N])
        V = place(r_b, "V", [P, 5, D])
        rb2 = again(r_b, b0)
        XR = place(rb2, "XR", [P, QB, D])
        XM = place(rb2, "XM", [META, D])
        VR = place(rb2, "VR", [P, 3, P])
        rb3 = again(r_b, b0)
        BH = place(rb3, "BH", [P, KC, T], F32R)
        BL = place(rb3, "BL", [P, KC, T], F32R)
        PT2_AT = b0 + 2 * 4 * KC * T
        PT2 = place(again(r_b, PT2_AT), "PT2", [P, 2, T])
        rb4 = again(r_b, b0)
        OUT = place(rb4, "OUT", [P, QB, D])

        r_q = region(4 * KC * T + 64)
        q0 = r_q[0]
        QT = place(r_q, "QT", [P, HEADS, T])
        rq2 = again(r_q, q0)
        XA = place(rq2, "XA", [P, 4, T + 3])
        YA = place(rq2, "YA", [P, 4, T])

        r_x = region(4 * KC * N)
        x0 = r_x[0]
        H0 = place(r_x, "H0", [P, KC, N])
        rx2 = again(r_x, x0)
        GB = place(rx2, "GB", [P, KC, T])
        rx3 = again(r_x, x0)
        SQK = place(rx3, "SQK", [P, 4, T])
        DQK = place(rx3, "DQK", [P, 4, T])

        r_u = region(4 * KC * N)
        u0 = r_u[0]
        U = place(r_u, "U", [P, KC, N])
        ru2 = again(r_u, u0)
        H = place(ru2, "H", [P, KC, T])

        r_g = region(4 * KC * T)
        g0 = r_g[0]
        GA = place(r_g, "GA", [P, KC, T])
        rg2 = again(r_g, g0)
        QI = place(rg2, "QI", [P, 4, T])
        KI = place(rg2, "KI", [P, N])
        WIT = place(rg2, "WIT", [P, N])
        rg3 = again(r_g, g0)
        V2 = place(rg3, "V2", [P, QB, 512])
        GY = place(rg3, "GY", [P, 4, T])
        HG = place(again(r_g, g0), "HG", [P, KC, T])

        r_s = region(4 * QB * (PADS + N))
        s0 = r_s[0]
        S = place(r_s, "S", [P, QB, PADS + N])
        rs2 = again(r_s, s0)
        BIAS = place(rs2, "BIAS", [P, T])
        WR = place(rs2, "WR", [P, 2, 4, P])
        R = place(rs2, "R", [P, T])

        r_t = region(4 * (4 * T + QB * 256 + 2 * T + 4 * T))
        t0 = r_t[0]
        SQ = place(r_t, "SQ", [P, 2, N])
        TN = place(r_t, "TN", [P, 2, N])
        RT = place(r_t, "RT", [P, N])
        RSTD = place(r_t, "RSTD", [P, N])
        SSM = place(r_t, "SSM", [P, N])
        rt2 = again(r_t, t0)
        RL = place(rt2, "RL", [P, 2, N])
        VTT = place(rt2, "VTT", [P, 2, N])
        rt3 = again(r_t, t0)
        LT = place(rt3, "LT", [P, 2, N])
        CT = place(rt3, "CT", [P, 2, T])
        PT = place(rt3, "PT", [P, 2, 5 * P])
        QS = place(rt3, "QS", [P, 2, P])
        YS = place(rt3, "YS", [P, 2, P])
        rt4 = again(r_t, t0)
        SG = place(rt4, "SG", [P, 2, T])
        T1 = place(rt4, "T1", [P, 4, T])
        T2 = place(rt4, "T2", [P, 2, T])
        rt9 = again(r_t, t0)
        RF = place(rt9, "RF", [P, T])
        SQB = place(rt9, "SQB", [P, 2, T])
        SSB = place(rt9, "SSB", [P, T])
        US = place(again(r_t, rt4[0]), "US", [P, 4, T])
        SQT = place(rt4, "SQT", [P, 2, T])
        SS = place(rt4, "SS", [P, T])
        ROOT = place(rt4, "ROOT", [P, T])
        rt5 = again(r_t, t0)
        XC = place(rt5, "XC", [P, 4, T])
        OC = place(rt5, "OC", [P, QB, 256])
        L = place(rt5, "L", [P, 2, 2, T])
        rt6 = again(r_t, rt5[0])
        A2 = place(again(r_t, rt5[0]), "A2", [P, 2, T])
        OSQ = place(rt5, "OSQ", [P, QB, 256])
        VT2 = place(rt6, "VT2", [P, 2, T])
        rt8 = again(r_t, t0 + 4 * 10 * T)
        DISTI = place(rt8, "DISTI", [P, T], I32)
        assert top[0] <= nc.sbuf_usable_end, top

        PJ = ctx.enter_context(nc.psum_tensor("PJ", [P, 2, 2, BANK], F32))
        PX = ctx.enter_context(nc.psum_tensor("PX", [P, 2, BANK], F32))
        PB = ctx.enter_context(nc.psum_tensor("PB", [P, 2, BANK], F32))
        PB6, PB7 = PB[:, 0, :], PB[:, 1, :]
        OUT_BANKS = [PJ[:, 0], PJ[:, 1], PX[:, :, :], PJ[:, 0]]
        INDEX_BANKS = [PX[:, :, :].rearrange("p a n -> p (a n)"), PB[:, :, :].rearrange("p a n -> p (a n)")]
        TURNED_Y, TAIL_P = PJ[:, 0, 1, :], PJ[:, 1, 1, :]
        SB_Z = [PX[:, 0, :], PX[:, 1, :], PB6]
        SB_TAIL = [PB7, PJ[:, 0, 1, :], PJ[:, 1, 1, :]]
        SB_OUT = PX[:, 0, :]
        SIDE = [PJ[:, 0, 1, :], PJ[:, 1, 1, :]]
        PX_flat = PX[:, :, :].rearrange("p a n -> p (a n)")

        h_scratch = nc.dram_tensor("h_scratch", (P, KC, T), F32).ap()

        raw_loaded = [sem(f"raw_loaded{i}") for i in range(RAW_SLOTS)]
        w_hi = sem("w_hi")
        w_ready = sem("w_ready")
        pool_seen = sem("pool_seen")
        dve_seen, act_seen = sem("dve_seen"), sem("act_seen")
        panel_done = sem("panel_done")
        freed = {"act": sem("freed_act"), "dve": sem("freed_dve")}
        consts_ready = sem("consts_ready")
        const_step = sem("const_step")
        x_loaded = [sem(f"x_loaded{h}") for h in range(2)]
        meta_loaded, vec_loaded, mix_summed = sem("meta_loaded"), sem("vec_loaded"), sem("mix_summed")
        xt_done, h0_ready = sem("xt_done"), sem("h0_ready")
        vec_done, vec_ready = sem("vec_done"), sem("vec_ready")
        NORMS = ["mix", "ffn", "n1", "n2", "fin2"]
        sq_ready = {n: sem(f"sq_ready_{n}") for n in NORMS}
        ms_added = {n: sem(f"ms_added_{n}") for n in NORMS}
        rt_ready = {n: sem(f"rt_ready_{n}") for n in NORMS}
        rstd_ready = {n: sem(f"rstd_ready_{n}") for n in NORMS}
        normed = {n: sem(f"normed_{n}") for n in NORMS}
        LATE = ["ffn", "n1", "n2", "fin2"]
        ss_added = {n: sem(f"ss_added_{n}") for n in LATE}
        ss_summed = {n: sem(f"ss_summed_{n}") for n in LATE}
        fin_ms = sem("fin_ms")
        gate_scaled, silu_ready, taps_done = sem("gate_scaled"), sem("silu_ready"), sem("taps_done")
        a_hi, a_lo = sem("a_hi"), sem("a_lo")
        b_hi, b_lo = sem("b_hi"), sem("b_lo")
        h_stored, h_loaded = sem("h_stored"), sem("h_loaded")
        ki_ready, ki_twin = sem("ki_ready"), sem("ki_twin")
        wq_done, wq_ready = sem("wq_done"), sem("wq_ready")
        idx_done, relu_done, score_step = sem("idx_done"), sem("relu_done"), sem("score_step")
        topk_step, mask_ready = sem("topk_step"), sem("mask_ready")
        v_turned, v_ready = sem("v_turned"), sem("v_ready")
        conv_step = sem("conv_step")
        qs_ready, qk_done, logits_ready, max_ready = sem("qs_ready"), sem("qk_done"), sem("logits_ready"), sem("max_ready")
        exp_done, rinv_ready, p_turned, pt_ready = sem("exp_done"), sem("rinv_ready"), sem("p_turned"), sem("pt_ready")
        pv_done, ys_ready, y_turned, y_ready = sem("pv_done"), sem("ys_ready"), sem("y_turned"), sem("y_ready")
        mixed_ready = sem("mixed_ready")
        tanh_ready, ff_step, conv_base = sem("tanh_ready"), sem("ff_step"), sem("conv_base")
        small_loaded, wr_cleared = sem("small_loaded"), sem("wr_cleared")
        act_step, dve_step = sem("act_step"), sem("dve_step")
        cl_ready, lam_e = sem("cl_ready"), sem("lam_e")
        lam_sum, cl_exp = sem("lam_sum"), sem("cl_exp")
        xc_ready, rg_done, rg_tanh = sem("xc_ready"), sem("rg_done"), sem("rg_tanh")
        lru_a, lru_q, lru_root = sem("lru_a"), sem("lru_q"), sem("lru_root")
        v2_turned, v2_ready = sem("v2_turned"), sem("v2_ready")
        gelu_in, gelu_t = sem("gelu_in"), sem("gelu_t")
        outa_ready = sem("outa_ready")
        z_done, z_ready, sb_ln, sb_log, tail_done, sb_sum, sb_w, sb_masked, sb_pv = (
            sem(n) for n in ("z_done", "z_ready", "sb_ln", "sb_log", "tail_done", "sb_sum", "sb_w", "sb_masked", "sb_pv"))
        df_qk, df_max, df_exp, df_p, df_turned, df_pt, df_pv, df_o = (
            sem(n) for n in ("df_qk", "df_max", "df_exp", "df_p", "df_turned", "df_pt", "df_pv", "df_o"))
        df_lt = sem("df_lt")
        oc_sq, oc_root, oc_ready, oc_turned = sem("oc_sq"), sem("oc_root"), sem("oc_ready"), sem("oc_turned")
        hg_ready, out_ready_dve = sem("hg_ready"), sem("out_ready_dve")
        out_turned, out_ready, stored = sem("out_turned"), sem("out_ready"), sem("stored")

        block = ctx.enter_context(nc.Block())

        def pick(t, i):
            return t[:, bass.ds(i, 1)].rearrange("p o n -> p (o n)")

        def chunk_of(t, i):
            return t[:, bass.ds(i, 1), 0:T].rearrange("p o n -> p (o n)")

        def cols(ap, w):
            return ap.rearrange("p (a n) -> p a n", a=2) if w == N else ap

        A_USE, B_USE = {}, {}
        for _use, _pieces in ((A_USE, [("mix", KC), ("conv", KC), ("mixed", KC), ("act0", 8), ("act1", 8), ("act2", 6), ("n2", KC)]),
                              (B_USE, [("y", KC), ("ffn", KC), ("n1", KC), ("m2", 7), ("ff0", 8), ("ff1", 8), ("ff2", 6)])):
            _b = 0
            for _n_, _c in _pieces:
                _use[_n_] = _b
                _b += _c
        M2 = {piece: i + 1 for i, piece in enumerate(["lru", "sb0", "sb1", "df0", "df1", "sb2", "sb3"])}
        M2_PIECES = len(M2)

        @block.sync
        def _(sp):
            sp.dma_start(XM[:], meta_tokens).then_inc(meta_loaded, 16)
            for h in range(2):
                half_d = slice(h * (D // 2), (h + 1) * (D // 2))
                sp.dma_start(XR[:, :, half_d], x[0].rearrange("(t p) d -> p t d", p=P)[:, :, half_d]).then_inc(x_loaded[h], 16)

            def rows(at, tile, src, n):
                sp.dma_start(VR[at:at + n, tile, :], src).then_inc(vec_loaded, 16)

            def flat(v):
                return v.rearrange("o (c p) -> (o c) p", p=P)

            for at, v in ((V_MIX, norm_mix_g), (V_FFN, norm_ffn_g), (V_N1, norm1_g), (V_CAB, conv_a_b), (V_BR, b_rgate),
                          (V_BI, b_igate), (V_LAM, lru_lambda), (V_N2, norm2_g)):
                rows(at, 0, flat(v), v.shape[1] // P)
            for at, v in ((V_FIN, norm_final_g), (V_FIN2, final_g)):
                rows(at, 0, v.rearrange("(c p) -> c p", p=P), KC)
            rows(V_CW, 0, conv_w.rearrange("o j (c p) -> (o j c) p", p=P), 3 * KC)
            rows(V_CAW, 0, conv_a_w.rearrange("o j (c p) -> (o j c) p", p=P), 4 * 4)
            taps = conv_ff_w.rearrange("o j (c p) -> (o j c) p", p=P)
            rows(0, 1, taps[0:4 * FFC], 4 * FFC)
            rows(0, 2, taps[4 * FFC:6 * FFC], 2 * FFC)
            rows(2 * FFC, 2, flat(conv_ff_b), 2 * FFC)
            sp.dma_start(GSUB[:], subln_g[0].partition_broadcast(P)).then_inc(small_loaded, 16)
            for n, v in enumerate((lam_q1, lam_k1, lam_q2, lam_k2)):
                sp.dma_start(LAMV[:, n, :], v[0].partition_broadcast(P)).then_inc(small_loaded, 16)
            sp.wait_ge(x_loaded[0], 16)

            def load(slot, src, free):
                if free is not None:
                    sp.wait_ge(w_ready, free)
                k, b = src.shape[0] // P, src.shape[1] // P
                sp.dma_start(RAW[:, slot, 0:k * b].rearrange("p (k b) c -> p k (b c)", b=b),
                             src.rearrange("(k p) c -> p k c", p=P)).then_inc(raw_loaded[slot], 16)

            def run(first, blocks, src):
                with sp.Fori(0, blocks) as i:
                    for j in range(RAW_SLOTS):
                        load((first + j) % RAW_SLOTS, src(i, j), first - RAW_SLOTS + 1 + j + i * RAW_SLOTS)

            def columns(w, c0, width=P):
                return lambda i, j: w[:, bass.ds(i * (4 * width) + (c0 + j * width), width)]

            def pairs(wa, ca, wb, cb):
                return lambda i, j: (wa if j % 2 == 0 else wb)[:, bass.ds(i * (2 * P) + ((ca if j % 2 == 0 else cb) + j // 2 * P), P)]

            def gate_up(name, wa, ca, wb, cb, g):
                c0, n = GROUPS[g]
                run(FIRST[name], n // 2, pairs(wa, ca + c0 * P, wb, cb + c0 * P))

            def down(name, w, g):
                c0, n = GROUPS[g]
                run(FIRST[name], 2, columns(w[c0 * P:(c0 + n) * P], 0))

            w1, w2 = w_in[0], w_in_2[0]
            load(0, w1[:, C_KI:C_KI + P], None)
            for p in range(1, 5):
                load(p % RAW_SLOTS, w1[:, C_QI + (p - 1) * P:C_QI + p * P], p - RAW_SLOTS + 1 if p >= RAW_SLOTS else None)
            for name, c0 in (("q", C_Q), ("k", C_K), ("v", C_V), ("cu", C_CU), ("cc", C_CC)):
                run(FIRST[name], 2, columns(w1, c0))
            with sp.Fori(0, 2) as i:
                for j in range(12):
                    c0 = (C_CB, C_GA, C_GB)[j % 3]
                    load((FIRST["gates"] + j) % RAW_SLOTS, w1[:, bass.ds(i * (4 * P) + (c0 + j // 3 * P), P)],
                         FIRST["gates"] + j - RAW_SLOTS + 1 + i * 12)
            for name, w in (("co", w_conv_out), ("ao", w_attn_out), ("wo", w_out)):
                run(FIRST[name], 2, columns(w[0], 0))
                if name == "co":
                    sp.wait_ge(h_stored, 16)
                    sp.wait_ge(a_lo, A_USE["conv"] + KC)
                    sp.dma_start(H[:], h_scratch).then_inc(h_loaded, 16)
            for g in range(3):
                gate_up(f"gu{g}", w_gate[0], 0, w_up[0], 0, g)
                down(f"dn{g}", w_down[0], g)
            def two(name, c0):
                for j in range(2):
                    p = FIRST[name] + j
                    load(p % RAW_SLOTS, w2[:, c0 + j * P:c0 + (j + 1) * P], p - RAW_SLOTS + 1)

            run(FIRST["dqk"], 1, columns(w2, 1792))
            two("dv", 2304)
            run(FIRST["xa"], 2, columns(w2, 0))
            run(FIRST["sqk"], 1, columns(w2, 1024))
            two("sv", 1536)
            run(FIRST["wo2a"], 1, columns(w_out_2[0][0:D // 2], 0, 2 * P))
            run(FIRST["wo2b"], 1, columns(w_out_2[0][D // 2:D], 0, 2 * P))
            for g in range(3):
                gate_up(f"gv{g}", w_ff_up[0], 0, w_ff_up[0], FF, g)
                down(f"ed{g}", w_ff_down[0], g)
            for b in range(QB):
                sp.wait_ge((out_ready, out_ready_dve)[b % 2], b // 2 + 1)
                sp.dma_start(out[0, b * P:(b + 1) * P, :], OUT[:, b]).then_inc(stored, 16)
            sp.wait_ge(stored, 16 * QB)

        @block.gpsimd
        def _(pool):
            pool.memset(ident[:], 0.0).then_inc(const_step, 1)
            pool.memset(ones[:], 1.0).then_inc(const_step, 1)
            pool.memset(hide[:], 0.0).then_inc(const_step, 1)
            pool.memset(eps_t[:], EPS).then_inc(const_step, 1)
            pool.memset(zero_t[:], 0.0).then_inc(const_step, 1)
            pool.memset(eps2_t[:], EPS * EPS).then_inc(const_step, 1)
            pool.wait_ge(const_step, 6)
            pool.iota(DISTI[:], [[-1, T]], base=T - P, channel_multiplier=1).then_inc(consts_ready, 1)
            pool.affine_select(out=ident[:], in_=ident[:], compare_op=ALU.not_equal, fill=1.0, base=0,
                               pattern=[[-1, P]], channel_multiplier=1).then_inc(consts_ready, 1)
            pool.affine_select(out=tri[:], in_=ones[:], compare_op=ALU.is_ge, fill=0.0, base=0,
                               pattern=[[-1, P]], channel_multiplier=1).then_inc(consts_ready, 1)
            pool.affine_select(out=before[:], in_=ones[:], compare_op=ALU.is_gt, fill=0.0, base=0,
                               pattern=[[1, P]], channel_multiplier=-1).then_inc(consts_ready, 1)
            pool.affine_select(out=hide[:], in_=hide[:], compare_op=ALU.is_ge, fill=HIDDEN, base=0,
                               pattern=[[-1, P]], channel_multiplier=1).then_inc(consts_ready, 1)

            def split(slot, w, loaded, used, p):
                pool.wait_ge(raw_loaded[slot], loaded)
                if used is not None:
                    pool.wait_ge(panel_done, used)
                pool.sem_inc(pool_seen, 1)
                nc.gpsimd.tensor_scalar(WH[:, w], RAW[:, slot], 1.0, 1.0, ALU.mult, ALU.mult).then_inc(w_hi, 1)
                pool.wait_ge(w_hi, p + 1)
                nc.gpsimd.tensor_tensor(WL[:, w], RAW[:, slot], WH[:, w].bitcast(F32), ALU.subtract).then_inc(w_ready, 1)

            PEEL = 5
            for p in range(PEEL):
                split(p % RAW_SLOTS, p % W_SLOTS, 16 * (p // RAW_SLOTS + 1), p - 1 if p >= 2 else None, p)
            with pool.Fori(0, (PANELS - PEEL) // RAW_SLOTS) as i:
                for j in range(RAW_SLOTS):
                    p = PEEL + j
                    split(p % RAW_SLOTS, p % W_SLOTS, i * 16 + 16 * (p // RAW_SLOTS + 1), i * RAW_SLOTS + (p - 1), i * RAW_SLOTS + p)

        @block.tensor
        def _(pe):
            mm = nc.tensor.matmul

            def slot_of(name, i):
                return (FIRST[name] + i) % 2

            def panel(name, i, at, rhs, ready, wide=False, rows=P, kc=KC, half=None, owner=None):
                s = slot_of(name, i)
                rh, rl = rhs
                ks = range(kc) if half is None else range(half * kc // 2, (half + 1) * kc // 2)
                if ks[0] == 0:
                    pe.wait_ge(w_ready, at + (FIRST[name] + 1))
                    who = owner or OWNER[name]
                    if owner is None:
                        pe.wait_ge(freed[who], at + (LETGO[name][who] - 1))
                parts = [(WH, rh), (WL, rh), (WH, rl)]
                last = None
                for k in ks:
                    for n, (w, a) in enumerate(parts):
                        if ready is not None and n == 0 and k == kc - 1:
                            pe.wait_ge(a_hi if ready[0] is a_lo else b_hi, ready[1] + k + 1)
                        elif ready is not None and (n == 0 or n == 2 and k == kc - 1):
                            pe.wait_ge(ready[0], ready[1] + k + 1)
                        st, sp_ = k == 0 and n == 0, k == kc - 1 and n == 2
                        if wide:
                            for h in range(2):
                                last = mm(PJ[0:rows, s, h, 0:HALF], w[:, s, k, 0:rows], a[:, k, h * HALF:(h + 1) * HALF], start=st, stop=sp_)
                        else:
                            last = mm(PJ[0:rows, s, 0, 0:T], w[:, s, k, 0:rows], a[:, k, :], start=st, stop=sp_)
                if ks[-1] == kc - 1:
                    last.then_inc(panel_done, 1)

            def enter(name):
                prev = ORDER[ORDER.index(name) - 1]
                if OWNER[prev] != OWNER[name]:
                    for who in ("act", "dve"):
                        pe.wait_ge(freed[who], LETGO[name][who])

            def stage(name, rhs, ready, lead=None, **kw):
                enter(name)
                first = 0
                if lead:
                    panel(name, 0, 0, rhs, ready, half=0, **kw)
                    lead()
                    panel(name, 0, 0, rhs, ready, half=1, **kw)
                    panel(name, 1, 1, rhs, ready, **kw)
                    first = 1
                with pe.Fori(0, COUNT[name] // 2 - first) as i:
                    for j in range(2):
                        panel(name, j, i * 2 + (2 * first + j), rhs, ready, **kw)

            def late_sum(name):
                pe.wait_ge(ss_added[name], KC + 2)
                mm(PX[:, 0, 0:T], ones[:], SS[:], start=True, stop=True).then_inc(ss_summed[name], 1)

            a_wide = (AH[:, :, :], AL[:, :, :])
            a_x = (AH[:, :, META:N], AL[:, :, META:N])
            a_t = (AH[:, :, 0:T], AL[:, :, 0:T])
            b_t = (BH[:, :, :], BL[:, :, :])

            pe.wait_ge(consts_ready, 5)
            pe.wait_ge(meta_loaded, 16)
            for k in range(KC):
                if k % (KC // 2) == 0:
                    pe.wait_ge(x_loaded[k // (KC // 2)], 16)
                if k >= 2:
                    pe.wait_ge(h0_ready, k - 1)
                for t in range(QB):
                    nc.tensor.transpose(PJ[:, k % 2, 0, t * P:(t + 1) * P], XR[:, t, k * P:(k + 1) * P], ident[:])
                nc.tensor.transpose(PJ[:, k % 2, 1, 0:META], XM[:, k * P:(k + 1) * P], ident[0:META, 0:META]).then_inc(xt_done, 1)
            pe.wait_ge(vec_loaded, 16 * 15)
            for t, rows in enumerate((V_ROWS, 88, 88)):
                last = nc.tensor.transpose(PB6[:, t * P:t * P + rows], VR[0:rows, t, :], ident[0:rows, 0:rows])
            last.then_inc(vec_done, 1)
            pe.wait_ge(ms_added["mix"], KC)
            for h in range(2):
                last = mm(PX[:, h, 0:HALF], ones[:], SSM[:, h * HALF:(h + 1) * HALF], start=True, stop=True)
            last.then_inc(mix_summed, 1)

            mix = (a_lo, A_USE["mix"])
            panel("ki", 0, 0, a_wide, mix, wide=True, rows=IDX_DIM + IDX_HEADS)
            stage("qi", a_x, mix)
            pe.wait_ge(freed["act"], LETGO["qi"]["act"])
            for b in range(QB):
                last = nc.tensor.transpose(PB6[:, b * 8:b * 8 + 8], WIT[64:72, META + b * P:META + (b + 1) * P], ident[64:72, 64:72])
            last.then_inc(wq_done, 1)
            def index_product(n):
                b, h = n // IDX_HEADS, n % IDX_HEADS
                r = 64 * (h % 2)
                if n >= 2:
                    pe.wait_ge(relu_done, n - 1)
                dst = INDEX_BANKS[n % 2]
                lhs = QI[r:r + 64, h // 2, b * P:(b + 1) * P]
                last = mm(dst[:, 0:min(EXT[b], BANK)], lhs, KI[r:r + 64, 0:min(EXT[b], BANK)], start=True, stop=True)
                if EXT[b] > BANK:
                    last = mm(dst[:, BANK:EXT[b]], lhs, KI[r:r + 64, BANK:EXT[b]], start=True, stop=True)
                last.then_inc(idx_done, 1)

            enter("q")
            per_half = QB * IDX_HEADS // (2 * COUNT["q"])
            for h in range(2 * COUNT["q"]):
                panel("q", h // 2, h // 2, a_x, mix, half=h % 2)
                if h == 0:
                    pe.wait_ge(freed["act"], LETGO["q"]["act"])
                    pe.wait_ge(ki_twin, 16)
                    pe.wait_ge(wq_ready, 1)
                for n in range(h * per_half, (h + 1) * per_half):
                    index_product(n)
            stage("k", a_wide, mix, wide=True)
            pe.wait_ge(relu_done, QB * IDX_HEADS)
            def v_panel(par, c):
                panel("v", par, c, a_wide, mix, wide=True)

            def v_turn(par, c):
                pe.wait_ge(freed["act"], c + (LETGO["v"]["act"] + 1))
                pe.wait_ge(v_ready, c + 1)
                for t in range(4):
                    nc.tensor.transpose(PX[:, 0, t * P:(t + 1) * P], VTT[:, par, t * P:(t + 1) * P], ident[:])
                nc.tensor.transpose(PX[0:META, 1, 0:P], VTT[:, par, T:N], ident[:]).then_inc(v_turned, 1)

            v_panel(0, 0)
            with pe.Fori(0, HEADS // 2 - 1) as i:
                v_panel(1, i * 2 + 1)
                v_turn(0, i * 2)
                v_panel(0, i * 2 + 2)
                v_turn(1, i * 2 + 1)
            v_panel(1, HEADS - 1)
            v_turn(0, HEADS - 2)
            v_turn(1, HEADS - 1)
            stage("cu", a_wide, mix, wide=True)
            stage("cc", a_wide, mix, wide=True)

            enter("gates")
            pe.wait_ge(v_ready, HEADS + 1)
            units = [(j, b) for j in range(2) for b in range(QB)]
            NU = len(units)

            def qk(i, u):
                j, b = units[u]
                pe.wait_ge(qs_ready, i * NU + (u + 1))
                pe.wait_ge(logits_ready, i * NU + (u + 1))
                head = KT[:, bass.ds(i * 2 + j, 1), :].rearrange("p o n -> p (o n)")
                last = mm(PX[:, 0, 0:min(EXT[b], BANK)], QS[:, u % 2], head[:, 0:min(EXT[b], BANK)], start=True, stop=True)
                if EXT[b] > BANK:
                    last = mm(PX[:, 1, 0:EXT[b] - BANK], QS[:, u % 2], head[:, BANK:EXT[b]], start=True, stop=True)
                last.then_inc(qk_done, 1)

            def turn_p(i, u):
                j, b = units[u]
                pe.wait_ge(exp_done, i * NU + (u + 1))
                pe.wait_ge(pt_ready, i * NU + (u + 1))
                for t in range(b + 1):
                    nc.tensor.transpose(PB6[:, t * P:(t + 1) * P], LT[:, u % 2, t * P:(t + 1) * P], ident[:])
                nc.tensor.transpose(TAIL_P[0:META, 0:P], LT[:, u % 2, (b + 1) * P:EXT[b]], ident[:]).then_inc(p_turned, 1)

            def pv(i, u):
                j, b = units[u]
                pe.wait_ge(pt_ready, i * NU + (u + 2))
                pe.wait_ge(ys_ready, i * NU + (u + 1))
                for t in range(b + 1):
                    mm(PB7[:, 0:P], PT[:, u % 2, t * P:(t + 1) * P], V[:, t, bass.ds((i * 2 + j) * P, P)], start=t == 0, stop=False)
                mm(PB7[:, 0:P], PT[0:META, u % 2, 4 * P:5 * P], V[0:META, b + 1, bass.ds((i * 2 + j) * P, P)],
                   start=False, stop=True).then_inc(pv_done, 1)

            def turn_y(i, u):
                pe.wait_ge(ys_ready, i * NU + (u + 2))
                pe.wait_ge(y_ready, i * NU + (u + 1))
                nc.tensor.transpose(TURNED_Y[:, 0:P], YS[:, u % 2], ident[:]).then_inc(y_turned, 1)

            with pe.Fori(0, 4) as i:
                for half in range(12):
                    j = half // 2
                    if half % 2 == 0:
                        who = "dve" if j % 3 == 2 else "act"
                        base = LETGO["gates"]
                        if who == "dve":
                            pe.wait_ge(freed["dve"], i * 2 + (base["dve"] + j // 3 + 1))
                        else:
                            pe.wait_ge(freed["act"], i * 4 + (base["act"] + (0, 0, None, 1, 2)[j] - (1 if j == 0 else 0)))
                    panel("gates", j, i * 6 + j, a_x, mix, half=half % 2, owner="here")
                    if half - 3 >= 0 and half - 3 < NU:
                        turn_y(i, half - 3)
                    if half - 2 >= 0 and half - 2 < NU:
                        pv(i, half - 2)
                    if half - 1 >= 0 and half - 1 < NU:
                        turn_p(i, half - 1)
                    if half < NU:
                        qk(i, half)
            stage("co", a_t, (a_lo, A_USE["conv"]))
            stage("ao", b_t, (b_lo, B_USE["y"]))
            stage("wo", a_t, (a_lo, A_USE["mixed"]))
            for g, (c0, n) in enumerate(GROUPS):
                stage(f"gu{g}", b_t, (b_lo, B_USE["ffn"]), lead=(lambda: late_sum("ffn")) if g == 0 else None)
                stage(f"dn{g}", a_t, (a_lo, A_USE[f"act{g}"]), kc=n)

            n1 = (b_lo, B_USE["n1"])

            def between_sums():
                pe.wait_ge(ss_added["n1"], KC + 2)
                mm(PX[:, 0, 0:T], ones[:], SS[:], start=True, stop=True)
                mm(PX[:, 1, 0:T], ones[:], SSB[:], start=True, stop=True).then_inc(ss_summed["n1"], 1)

            stage("dqk", b_t, n1, lead=between_sums)

            def turn_values(j):
                pe.wait_ge(freed["dve"], LETGO[("dv", "sv")[j // 2]]["dve"] + j % 2 + 1)
                if j >= 2:
                    pe.wait_ge(rg_tanh, 8)
                for t in range(QB):
                    last = nc.tensor.transpose(SIDE[j % 2][:, t * P:(t + 1) * P], VT2[:, j % 2, t * P:(t + 1) * P], ident[:])
                last.then_inc(v2_turned, 1)

            def df_scores(u):
                n, b = DF_UNITS[u]
                if u >= 1:
                    pe.wait_ge(df_lt, u)
                for m in range(2):
                    r = 32 * (2 * (n % 2) + m)
                    last = mm(PX[:, m, 0:(b + 1) * P], DQK[r:r + 32, n // 2, b * P:(b + 1) * P], DQK[r:r + 32, 2 + n // 2, 0:(b + 1) * P],
                              start=True, stop=True)
                last.then_inc(df_qk, 1)

            def df_turn(u):
                n, b = DF_UNITS[u]
                pe.wait_ge(df_p, u + 1)
                if u >= 1:
                    pe.wait_ge(df_pt, u)
                for t in range(b + 1):
                    last = nc.tensor.transpose(PB6[:, t * P:(t + 1) * P], L[:, u % 2, 0, t * P:(t + 1) * P], ident[:])
                last.then_inc(df_turned, 1)

            def df_out(u):
                n, b = DF_UNITS[u]
                pe.wait_ge(df_pt, u + 1)
                if u >= 1:
                    pe.wait_ge(df_o, u)
                for t in range(b + 1):
                    last = mm(PB7[:, 0:64], PT2[:, u % 2, t * P:(t + 1) * P], V2[:, t, 256 + n * 64:256 + (n + 1) * 64],
                              start=t == 0, stop=t == b)
                last.then_inc(df_pv, 1)

            def df_step(u):
                if u >= 2:
                    df_out(u - 2)
                if 1 <= u <= len(DF_UNITS):
                    df_turn(u - 1)
                if u + 1 < len(DF_UNITS):
                    df_scores(u + 1)

            enter("dv")
            panel("dv", 0, 0, b_t, n1)
            panel("dv", 1, 1, b_t, n1)
            pe.wait_ge(freed["dve"], LETGO["dv"]["dve"])
            pe.wait_ge(rt_ready["n1"], 2)
            df_scores(0)
            turn_values(0)
            pe.wait_ge(small_loaded, 16 * (5 + 4))
            for s, (name, c) in enumerate(BESIDE):
                panel(name, c, c, b_t, n1)
                if s == 0:
                    turn_values(1)
                if s == 2:
                    pe.wait_ge(v2_ready, 2)
                df_step(s)
                if name == "ya":
                    pe.wait_ge(xc_ready, c + 1)
                    if c >= 1:
                        pe.wait_ge(rg_tanh, 2 * c)
                    for g in range(2):
                        mm(SIDE[g], WR[:, g, c, :], XC[:, c, :], start=True, stop=True).then_inc(rg_done, 1)
            turn_values(2)

            def sb_logits(n):
                r, c = 64 * (n % 2), n // 2
                if n >= 1:
                    pe.wait_ge(z_ready, 3 * n)
                if n >= 2:
                    pe.wait_ge(b_lo, B_USE["m2"] + M2[f"sb{n - 2}"])
                for m, (i0, o, w) in enumerate(SB_BANKS):
                    for i in ((i0,) if m < 2 else (2, 3)):
                        at = SBO[i] - o
                        last = mm(SB_Z[m][:, at:at + SBW[i]], SQK[r:r + 64, 2 + c, i * P:(i + 1) * P], SQK[r:r + 64, c, i * P:T],
                                  start=i == i0, stop=True, skip_group_check=True)
                    last.then_inc(z_done, 1)

            def sb_tails(n):
                pe.wait_ge(sb_log, n + 1)
                if n >= 1:
                    pe.wait_ge(sb_sum, 3 * n)
                for m, (i0, o, w) in enumerate(SB_BANKS):
                    for i in ((i0,) if m < 2 else (2, 3)):
                        at = SBO[i] - o
                        last = mm(SB_TAIL[m][:, at:at + SBW[i]], tri[:], LG[:, SBO[i]:SBO[i] + SBW[i]],
                                  start=i == i0, stop=True, skip_group_check=True)
                        for j in range(i + 1, QB):
                            last = mm(SB_TAIL[m][:, at + (j - i) * P:at + SBW[i]], ones[:], LG[:, SBO[j]:SBO[j] + SBW[j]],
                                      start=False, stop=True, skip_group_check=True)
                    last.then_inc(tail_done, 1)

            def sb_out(n):
                r = 64 * (n % 2)
                pe.wait_ge(sb_masked, n + 1)
                pe.wait_ge(z_ready, 3 * min(n + 2, 4))
                if n >= 1:
                    pe.wait_ge(b_lo, B_USE["m2"] + M2[f"sb{n - 1}"])
                for i in range(QB):
                    last = mm(SB_OUT[r:r + 64, i * P:T], V2[:, i, n * 64:(n + 1) * 64], Z[:, n % 2, SBO[i]:SBO[i] + SBW[i]],
                              start=i == 0, stop=True, skip_group_check=True)
                last.then_inc(sb_pv, 1)

            lru_rows = (BH[:, 0:KC // 2, :], BL[:, 0:KC // 2, :])
            other_rows = (BH[:, KC // 2:KC, :], BL[:, KC // 2:KC, :])

            def pair_half(name, i, at, b, banks, rows):
                s = slot_of(name, i)
                if b == 0:
                    pe.wait_ge(w_ready, at + (FIRST[name] + 1))
                for k in range(KC // 2):
                    for n, (w, a) in enumerate(((WH, rows[0]), (WH, rows[1]), (WL, rows[0]))):
                        last = mm(banks[b], w[:, s, 2 * k + b, :], a[:, k, :], start=k == 0 and n == 0, stop=k == KC // 2 - 1 and n == 2)
                if b == 1:
                    last.then_inc(panel_done, 1)

            def lru_half(h):
                i, b = h // 2, h % 2
                if b == 0:
                    pe.wait_ge(freed["dve"], LETGO["wo2a"]["dve"] + i)
                pair_half("wo2a", i, i, b, (PJ[:, 0, 0, :], PJ[:, 1, 0, :]), lru_rows)

            enter("wo2a")
            df_step(14)
            turn_values(3)
            df_step(15)
            pe.wait_ge(b_lo, B_USE["m2"] + M2["lru"])
            lru_half(0)
            df_step(16)
            lru_half(1)
            df_step(17)
            pe.wait_ge(df_lt, 16)
            pe.wait_ge(df_pt, 16)
            sb_logits(0)
            lru_half(2)
            sb_logits(1)
            lru_half(3)
            pe.wait_ge(df_o, 16)
            pe.wait_ge(v2_ready, 4)
            for n in range(4):
                sb_tails(n)
                lru_half(4 + n)
                sb_out(n)
                if n == 1:
                    pe.wait_ge(oc_ready, 1)
                    pe.wait_ge(sb_sum, 6)
                    for c in range(2):
                        for b in range(QB):
                            last = nc.tensor.transpose(SIDE[c][:, b * P:(b + 1) * P], OC[:, b, c * P:(c + 1) * P], ident[:])
                        last.then_inc(oc_turned, 1)
                if n < 2:
                    sb_logits(n + 2)
                if n == 1:
                    pe.wait_ge(b_lo, B_USE["m2"] + M2["df1"])
            pe.wait_ge(b_lo, B_USE["m2"] + M2_PIECES)
            pe.wait_ge(freed["dve"], LETGO["wo2b"]["dve"])
            with pe.Fori(0, COUNT["wo2b"] // 2) as i:
                for j in range(2):
                    slot = slot_of("wo2b", j)
                    pe.wait_ge(freed["dve"], i * 2 + (LETGO["wo2b"]["dve"] - 1 + j))
                    for b in range(2):
                        pair_half("wo2b", j, i * 2 + j, b, (PJ[:, slot, 0, :], PJ[:, slot, 1, :]), other_rows)
            for g, (c0, n) in enumerate(GROUPS):
                stage(f"gv{g}", a_t, (a_lo, A_USE["n2"]), lead=(lambda: late_sum("n2")) if g == 0 else None)
                stage(f"ed{g}", b_t, (b_lo, B_USE[f"ff{g}"]), kc=n)
            pe.wait_ge(ss_added["fin2"], KC + 2)
            for b in range(QB):
                last = mm(PB6[:, b:b + 1], SS[:, b * P:(b + 1) * P], ones[:, 0:1], start=b == 0, stop=True, skip_group_check=True)
            last.then_inc(ss_summed["fin2"], 1)
            pe.wait_ge(hg_ready, KC)
            for b in range(QB):
                if b == 3:
                    pe.wait_ge(out_ready, 1)
                for k in range(KC):
                    last = nc.tensor.transpose(OUT_BANKS[b][:, k // 4, k % 4 * P:(k % 4 + 1) * P], HG[:, k, b * P:(b + 1) * P], ident[:])
                last.then_inc(out_turned, 1)

        @block.scalar
        def _(act):
            go = nc.scalar.activation
            for e, credit in ((freed["act"], CREDIT), (v_ready, 1), (pt_ready, 1), (y_ready, 1)):
                act.sem_inc(e, credit)

            def square(k):
                act.wait_ge(h0_ready, k + 1)
                if k >= 2:
                    act.wait_ge(ms_added["mix"], k - 1)
                go(SQ[:, k % 2], H0[:, k], ACT.Square).then_inc(sq_ready["mix"], 1)

            for k in range(KC):
                act.wait_ge(xt_done, k + 1)
                go(H0[:, k, META:N], PJ[:, k % 2, 0, :], ACT.Copy)
                go(H0[:, k, 0:META], PJ[:, k % 2, 1, 0:META], ACT.Copy).then_inc(h0_ready, 1)
                if k >= 1:
                    square(k - 1)
            square(KC - 1)
            act.dma_start(h_scratch, H0[:, :, META:N]).then_inc(h_stored, 16)
            act.wait_ge(vec_done, 1)
            for t, n in enumerate((V_ROWS, 4 * FFC, 4 * FFC)):
                last = go(VEC[:, t, 0:n], PB6[:, t * P:t * P + n], ACT.Copy)
            last.then_inc(vec_ready, 1)
            act.wait_ge(mix_summed, 1)
            go(cols(RT[:], N), PX[:, :, 0:HALF], ACT.Sqrt, bias=eps_t[:], scale=1.0 / D).then_inc(rt_ready["mix"], 1)
            for k in range(KC):
                act.wait_ge(normed["mix"], k + 1)
                go(AH[:, k], TN[:, k % 2], ACT.Copy).then_inc(a_hi, 1)

            def slot_of(name, i):
                return (FIRST[name] + i) % 2

            def after(name, at):
                act.wait_ge(panel_done, at + (FIRST[name] + 1))

            after("ki", 0)
            go(cols(KI[0:64, :], N), PJ[0:64, 0, :, 0:HALF], ACT.Copy).then_inc(ki_ready, 1)
            go(cols(WIT[64:72, :], N), PJ[64:72, 0, :, 0:HALF], ACT.Copy).then_inc(freed["act"], 1)
            act.wait_ge(ki_ready, 1)
            act.dma_start(KI[64:128, :], KI[0:64, :]).then_inc(ki_twin, 16)

            def copies(name, dst, wide=False):
                with act.Fori(0, COUNT[name] // 2) as i:
                    for j in range(2):
                        s = slot_of(name, j)
                        after(name, i * 2 + j)
                        if wide:
                            go(cols(dst(i * 2 + j), N), PJ[:, s, :, 0:HALF], ACT.Copy).then_inc(freed["act"], 1)
                        else:
                            go(dst(i * 2 + j), PJ[:, s, 0, :], ACT.Copy).then_inc(freed["act"], 1)

            copies("qi", lambda c: pick(QI, c))
            per_half = QB * IDX_HEADS // (2 * COUNT["q"])
            for h in range(2 * COUNT["q"]):
                for n in range(h * per_half, (h + 1) * per_half):
                    E = EXT[n // IDX_HEADS]
                    act.wait_ge(idx_done, n + 1)
                    if n >= 2:
                        act.wait_ge(score_step, n - 1)
                    go(RL[:, n % 2, 0:E], INDEX_BANKS[n % 2][:, 0:E], ACT.Relu).then_inc(relu_done, 1)
                if h % 2 == 1:
                    after("q", h // 2)
                    go(QT[:, h // 2], PJ[:, slot_of("q", h // 2), 0, :], ACT.Copy).then_inc(freed["act"], 1)
            copies("k", lambda c: pick(KT, c), wide=True)
            def v_copy(par, c):
                after("v", c)
                go(cols(VTT[:, par, :], N), PJ[:, slot_of("v", par), :, 0:HALF], ACT.Copy).then_inc(freed["act"], 1)

            def v_values(c):
                act.wait_ge(v_turned, c + 1)
                at = bass.ds(c * P, P)
                go(V[:, 0:4, at], PX[:, 0, :].rearrange("p (t d) -> p t d", t=4), ACT.Copy)
                go(V[0:META, 4, at], PX[0:META, 1, 0:P], ACT.Copy).then_inc(v_ready, 1)

            v_copy(0, 0)
            with act.Fori(0, HEADS // 2 - 1) as i:
                v_copy(1, i * 2 + 1)
                v_values(i * 2)
                v_copy(0, i * 2 + 2)
                v_values(i * 2 + 1)
            v_copy(1, HEADS - 1)
            v_values(HEADS - 2)
            v_values(HEADS - 1)
            act.wait_ge(cl_ready, 1)
            go(small[:, 4:8], small[:, 0:4], ACT.Exp, scale=-1.0).then_inc(cl_exp, 1)
            act.wait_ge(lam_sum, 1)
            go(small[:, 42:44], small[:, 40:42], ACT.Exp).then_inc(lam_e, 1)
            copies("cu", lambda c: pick(U, c), wide=True)

            units = [(j, b) for j in range(2) for b in range(QB)]
            NU = len(units)
            act.wait_ge(h_stored, 16)
            with act.Fori(0, 4) as i:
                def stage_q(u):
                    j, b = units[u]
                    g = i * NU + u
                    if u >= 2:
                        act.wait_ge(qk_done, i * NU + (u - 1))
                    go(QS[:, u % 2], QT[:, bass.ds(i * 2 + j, 1), b * P:(b + 1) * P].rearrange("p o n -> p (o n)"),
                       ACT.Copy, scale=ATT_SCALE).then_inc(qs_ready, 1)

                stage_q(0)
                stage_q(1)
                for s in range(NU + 4):
                    j = s // 2
                    if s % 2 == 1 and j < 6 and j % 3 != 0:
                        act.wait_ge(panel_done, i * 6 + (FIRST["gates"] + j + 1))
                        go(pick(GA if j % 3 == 1 else GB, i * 2 + j // 3), PJ[:, slot_of("gates", j), 0, :],
                           ACT.Tanh, scale=0.5).then_inc(freed["act"], 1)
                    if 0 <= s - 3 < NU:
                        u = s - 3
                        act.wait_ge(y_turned, i * NU + (u + 1))
                        act.sem_inc(act_seen, 1)
                        go(QT[:, bass.ds(i * 2 + units[u][0], 1), units[u][1] * P:(units[u][1] + 1) * P].rearrange("p o n -> p (o n)"),
                           TURNED_Y[:, 0:P], ACT.Copy).then_inc(y_ready, 1)
                    if 0 <= s - 1 < NU:
                        u = s - 1
                        b = units[u][1]
                        act.wait_ge(p_turned, i * NU + (u + 1))
                        go(PT[:, u % 2, 0:(b + 1) * P], PB6[:, 0:(b + 1) * P], ACT.Copy)
                        go(PT[0:META, u % 2, 4 * P:5 * P], TAIL_P[0:META, 0:P], ACT.Copy).then_inc(pt_ready, 1)
                    if s < NU:
                        b = units[s][1]
                        act.wait_ge(max_ready, i * NU + (s + 1))
                        go(LT[:, s % 2, 0:EXT[b]], LT[:, s % 2, 0:EXT[b]], ACT.Exp, bias=NMX[:, s % 2:s % 2 + 1],
                           accum_out=RS[:, s % 2:s % 2 + 1]).then_inc(exp_done, 1)
                    if s + 2 < NU:
                        stage_q(s + 2)

            act.wait_ge(panel_done, FIRST["co"])
            act.wait_ge(freed["dve"], LETGO["co"]["dve"])
            for k in range(KC):
                go(AH[:, k, 0:T], U[:, k, META:N], ACT.Copy).then_inc(a_hi, 1)
            act.wait_ge(y_ready, 1 + HEADS * QB)
            for k in range(KC):
                go(BH[:, k], QT[:, k], ACT.Copy).then_inc(b_hi, 1)
            act.wait_ge(wr_cleared, 1)
            for g, w in enumerate((w_rgate, w_igate)):
                for r in range(2):
                    act.dma_start(WR[64 * r:64 * r + 64, g, :, 64 * r:64 * r + 64],
                                  w[0].rearrange("(c r) i o -> r i c o", r=2)[r]).then_inc(small_loaded, 16)
            with act.Fori(0, 4) as i:
                for j in range(2):
                    act.wait_ge(mixed_ready, i * 2 + (j + 1))
                    go(AH[:, bass.ds(i * 2 + j, 1), 0:T].rearrange("p o n -> p (o n)"), pick(GB, i * 2 + j), ACT.Copy).then_inc(a_hi, 1)

            def feed(norm_name, stage_name, gain, dst, hi, per=1):
                with act.Fori(0, KC // 2) as i:
                    for j in range(2):
                        c = i * 2 + j
                        if per == 1:
                            act.wait_ge(freed["dve"], c + (LETGO[stage_name]["dve"] + 1))
                        elif j == 0:
                            act.wait_ge(freed["dve"], i + (LETGO[stage_name]["dve"] + 1))
                        if dst is not None:
                            act.sem_inc(act_seen, 1)
                            go(chunk_of(dst, c), pick(H, c), ACT.Identity, bias=zero_t[:], scale=VEC[:, 0, bass.ds(c + gain, 1)]).then_inc(hi, 1)
                        act.wait_ge(ss_added[norm_name], c + 1)
                        act.sem_inc(act_seen, 1)
                        go(SQT[:, j], pick(H, c), ACT.Square).then_inc(sq_ready[norm_name], 1)

            def root(name):
                act.wait_ge(ss_summed[name], 1)
                go(ROOT[:], PX[:, 0, 0:T], ACT.Sqrt, bias=eps_t[:], scale=1.0 / D).then_inc(rt_ready[name], 1)

            feed("ffn", "wo", V_FFN, BH, b_hi)
            root("ffn")
            for g, (c0, n) in enumerate(GROUPS):
                name = f"gu{g}"
                with act.Fori(0, n // 2) as i:
                    for j in range(2):
                        q = i * 2 + j
                        act.wait_ge(gate_scaled, q + (c0 + 1))
                        go(SG[:, j], T1[:, j], ACT.Tanh, scale=0.5).then_inc(tanh_ready, 1)
                        act.wait_ge(ff_step, q + (c0 + 1))
                        act.sem_inc(act_seen, 1)
                        go(chunk_of(AH, q), T2[:, j], ACT.Copy).then_inc(a_hi, 1)
            with act.Fori(0, KC // 2) as i:
                for j in range(2):
                    c = i * 2 + j
                    act.wait_ge(freed["dve"], c + (LETGO["dn2"]["dve"] + 1))
                    act.sem_inc(act_seen, 1)
                    go(pick(BH, c), pick(H, c), ACT.Identity, bias=zero_t[:], scale=GF1[:, bass.ds(c, 1)]).then_inc(b_hi, 1)
                    act.wait_ge(ss_added["n1"], c + 1)
                    act.sem_inc(act_seen, 1)
                    go(SQT[:, j], pick(H, c), ACT.Square)
                    go(SQB[:, j], pick(H, c), ACT.Square, scale=VEC[:, 0, bass.ds(c + V_FIN, 1)]).then_inc(sq_ready["n1"], 1)
            act.wait_ge(fin_ms, 1)
            go(ROOT[:], R[:], ACT.Sqrt, bias=eps2_t[:], scale=1.0 / D).then_inc(rt_ready["n1"], 1)
            go(RF[:], PX[:, 0, 0:T], ACT.Sqrt, bias=eps_t[:], scale=1.0 / D).then_inc(rt_ready["n1"], 1)

            def values(j):
                act.wait_ge(v2_turned, j + 1)
                c0 = (256, 256 + P, 0, P)[j]
                go(V2[:, :, c0:c0 + P], SIDE[j % 2].rearrange("p (t d) -> p t d", t=QB), ACT.Copy).then_inc(v2_ready, 1)

            def df_step(u):
                if u < len(DF_UNITS):
                    E = (DF_UNITS[u][1] + 1) * P
                    act.wait_ge(df_max, u + 1)
                    for m in range(2):
                        at = 2 * (u % 2) + m
                        go(L[:, u % 2, m, 0:E], L[:, u % 2, m, 0:E], ACT.Exp, bias=small[:, 48 + at:49 + at],
                           accum_out=small[:, 52 + at:53 + at]).then_inc(df_exp, 1)
                if u >= 2:
                    n, b = DF_UNITS[u - 2]
                    act.wait_ge(df_pv, u - 1)
                    go(OC[:, b, n * 64:(n + 1) * 64], PB7[:, 0:64], ACT.Copy).then_inc(df_o, 1)
                if 1 <= u <= len(DF_UNITS):
                    E = (DF_UNITS[u - 1][1] + 1) * P
                    act.wait_ge(df_turned, u)
                    go(PT2[:, (u - 1) % 2, 0:E], PB6[:, 0:E], ACT.Copy).then_inc(df_pt, 1)

            values(0)
            for s, (name, c) in enumerate(BESIDE):
                if s == 0:
                    values(1)
                df_step(s)
                if name == "ya":
                    for g in range(2):
                        act.wait_ge(rg_done, 2 * c + g + 1)
                        go((RP, IP)[g][:, c], SIDE[g], ACT.Tanh, bias=small[:, 24 + 4 * g + c:25 + 4 * g + c], scale=0.5).then_inc(rg_tanh, 1)
                if 5 <= s < 9:
                    r = s - 5
                    act.wait_ge(rg_tanh, 2 * r + 2)
                    go(TH[:, r], RP[:, r], ACT.Tanh, bias=small[:, 20 + r:21 + r], scale=small[:, 20 + r:21 + r]).then_inc(lru_a, 1)
                    act.wait_ge(lru_a, 2 * r + 1)
                    go(RP[:, r], RP[:, r], ACT.Exp, bias=small[:, 16 + r:17 + r], scale=small[:, 16 + r:17 + r]).then_inc(lru_a, 1)
                if s == 10:
                    act.wait_ge(gelu_in, 2)
                    go(GY[:], GY[:], ACT.Tanh, scale=GELU_C).then_inc(gelu_t, 1)
                    act.wait_ge(lru_q, 4)
                    go(TH[:], TH[:], ACT.Sqrt, scale=0.25).then_inc(lru_root, 1)
            values(2)
            act.wait_ge(outa_ready, 1)
            after("sv", 1)
            go(BH[:, 0:4, :], XC[:], ACT.Copy).then_inc(b_hi, 1)

            def sb_hi(n):
                r, c = 64 * (n % 2), n // 2
                act.wait_ge(sb_pv, n + 1)
                go(BH[r:r + 64, 4 + c, :], SB_OUT[r:r + 64, :], ACT.Copy).then_inc(b_hi, 1)

            def sb_z(n):
                for m, (i0, o, w) in enumerate(SB_BANKS):
                    act.wait_ge(z_done, 3 * n + m + 1)
                    go(Z[:, n % 2, o:o + w], SB_Z[m][:, 0:w], ACT.Copy, scale=SB_SCALE).then_inc(z_ready, 1)
                act.wait_ge(z_ready, 3 * (n + 1))
                if n >= 1:
                    act.wait_ge(sb_log, n)
                go(LN[:], Z[:, n % 2], ACT.Abs).then_inc(act_step, 1)

            def sb_softplus(n):
                act.wait_ge(act_step, 2 * n + 1)
                go(LN[:], LN[:], ACT.Exp, scale=-1.0).then_inc(act_step, 1)
                act.wait_ge(act_step, 2 * n + 2)
                go(LN[:], LN[:], ACT.Ln, bias=ones[:, 0:1]).then_inc(sb_ln, 1)

            df_step(14)
            values(3)
            for u in (15, 16, 17):
                df_step(u)
            sb_z(0)
            sb_softplus(0)
            sb_z(1)
            for n in range(4):
                act.wait_ge(sb_sum, 3 * (n + 1))
                go(Z[:, n % 2], Z[:, n % 2], ACT.Exp).then_inc(sb_w, 1)
                if n == 0:
                    sb_softplus(1)
                    act.wait_ge(oc_sq, 1)
                    go(small[:, 80:96], small[:, 64:80], ACT.Sqrt, bias=eps_t[:], scale=1.0 / 64).then_inc(oc_root, 1)
                sb_hi(n)
                if n == 1:
                    for c in range(2):
                        act.wait_ge(oc_turned, c + 1)
                        go(BH[:, 6 + c, :], SIDE[c], ACT.Copy).then_inc(b_hi, 1)
                if n < 2:
                    sb_z(n + 2)
                    sb_softplus(n + 2)

            feed("n2", "wo2b", V_N2, AH, a_hi, per=2)
            root("n2")
            for g, (c0, n) in enumerate(GROUPS):
                name = f"gv{g}"
                with act.Fori(0, n // 2) as i:
                    for j in range(2):
                        q = i * 2 + j
                        for m in range(2):
                            act.wait_ge(freed["dve"], i * 4 + (LETGO[name]["dve"] + 2 * j + m + 1))
                            act.sem_inc(act_seen, 1)
                            go(T1[:, 2 * j + m], US[:, 2 * j + m], ACT.Identity,
                               bias=VEC[:, 2, bass.ds(q + (2 * FFC + FFC * m + c0), 1)],
                               scale=VEC[:, 2, bass.ds(q + (FFC * m + c0), 1)]).then_inc(conv_base, 1)
                            if m == 0:
                                act.wait_ge(taps_done, i * 4 + (2 * c0 + 2 * j + 1))
                                go(SG[:, j], T1[:, 2 * j], ACT.Tanh, scale=0.5).then_inc(tanh_ready, 1)
                        act.wait_ge(ff_step, q + (FFC + c0 + 1))
                        go(pick(BH, q), T2[:, j], ACT.Copy).then_inc(b_hi, 1)
            feed("fin2", "ed2", None, None, None)
            act.wait_ge(ss_summed["fin2"], 1)
            go(small[:, 112:116], PB6[:, 0:QB], ACT.Sqrt, bias=eps_t[:], scale=1.0 / D).then_inc(rt_ready["fin2"], 1)
            act.wait_ge(rstd_ready["fin2"], 1)
            for b in (0, 2):
                act.wait_ge(out_turned, b + 1)
                go(OUT[:, b], OUT_BANKS[b].rearrange("p a n -> p (a n)"), ACT.Identity, bias=zero_t[:],
                   scale=small[:, 116 + b:117 + b]).then_inc(out_ready, 1)

        @block.vector
        def _(dve):
            ts, tt, stt = nc.vector.tensor_scalar, nc.vector.tensor_tensor, nc.vector.scalar_tensor_tensor
            for e, credit in ((freed["dve"], CREDIT), (logits_ready, 1), (ys_ready, 1)):
                dve.sem_inc(e, credit)
            steps = [0]

            def step(ins):
                ins.then_inc(dve_step, 1)
                steps[0] += 1

            def settled():
                dve.wait_ge(dve_step, steps[0])

            dve.wait_ge(consts_ready, 5)
            step(nc.vector.tensor_copy(DIST[:], DISTI[:]))
            settled()
            step(stt(out=DIST[:], in0=DIST[:], scalar=-1.0, in1=DIST[:], op0=ALU.mult, op1=ALU.max))
            for k in range(KC):
                dve.wait_ge(sq_ready["mix"], k + 1)
                if k == 0:
                    nc.vector.tensor_copy(SSM[:], SQ[:, 0]).then_inc(ms_added["mix"], 1)
                else:
                    dve.wait_ge(ms_added["mix"], k)
                    tt(SSM[:], SSM[:], SQ[:, k % 2], ALU.add).then_inc(ms_added["mix"], 1)
            dve.wait_ge(vec_ready, 1)
            dve.wait_ge(rt_ready["mix"], 1)
            nc.vector.reciprocal(RSTD[:], RT[:]).then_inc(rstd_ready["mix"], 1)
            dve.wait_ge(rstd_ready["mix"], 1)
            for k in range(KC + 1):
                if k < KC:
                    if k >= 2:
                        dve.wait_ge(a_lo, A_USE["mix"] + k - 1)
                    stt(out=TN[:, k % 2], in0=H0[:, k], scalar=VEC[:, 0, V_MIX + k:V_MIX + k + 1], in1=RSTD[:],
                        op0=ALU.mult, op1=ALU.mult).then_inc(normed["mix"], 1)
                if k >= 1:
                    dve.wait_ge(a_hi, A_USE["mix"] + k)
                    tt(AL[:, k - 1], TN[:, (k - 1) % 2], AH[:, k - 1].bitcast(F32), ALU.subtract).then_inc(a_lo, 1)

            def slot_of(name, i):
                return (FIRST[name] + i) % 2

            def after(name, at):
                dve.wait_ge(panel_done, at + (FIRST[name] + 1))

            dve.wait_ge(wq_done, 1)
            ts(WQ[:].rearrange("p b h -> p (b h)"), PB6[:, 0:QB * IDX_HEADS], IDX_SCALE, None, ALU.mult).then_inc(wq_ready, 1)
            dve.wait_ge(wq_ready, 1)
            for b in range(QB):
                sc = S[:, b, PADS:PADS + EXT[b]]
                for h in range(IDX_HEADS):
                    n = b * IDX_HEADS + h
                    dve.wait_ge(relu_done, n + 1)
                    if h == 0:
                        ts(sc, RL[:, n % 2, 0:EXT[b]], WQ[:, b, h:h + 1], None, ALU.mult).then_inc(score_step, 1)
                    else:
                        dve.wait_ge(score_step, n)
                        stt(out=sc, in0=RL[:, n % 2, 0:EXT[b]], scalar=WQ[:, b, h:h + 1], in1=sc,
                            op0=ALU.mult, op1=ALU.add).then_inc(score_step, 1)
            dve.wait_ge(score_step, QB * IDX_HEADS)
            for b in range(QB):
                own = S[:, b, PADS + EXT[b] - P:PADS + EXT[b]]
                tt(own, own, hide[:], ALU.add).then_inc(topk_step, 1)
                nc.vector.memset(S[:, b, 0:PADS], SENTINEL).then_inc(topk_step, 1)
            for b in range(QB):
                base = 2 * QB + b * 2 * ROUNDS
                row = S[:, b, 0:PADS + EXT[b]]
                with dve.Fori(0, ROUNDS) as i:
                    dve.wait_ge(topk_step, i * 2 + base)
                    dve.sem_inc(dve_seen, 1)
                    nc.vector.max(MX8[:], row).then_inc(topk_step, 1)
                    dve.wait_ge(topk_step, i * 2 + (base + 1))
                    dve.sem_inc(dve_seen, 1)
                    nc.vector.match_replace(row, MX8[:], row, TAKEN).then_inc(topk_step, 1)
            dve.wait_ge(topk_step, 2 * QB * (1 + ROUNDS // 1))
            for b in range(QB):
                m = S[:, b, PADS:PADS + EXT[b]]
                ts(m, m, TAKEN / 1.5, HIDDEN, ALU.is_gt, ALU.mult).then_inc(mask_ready, 1)
            dve.wait_ge(mask_ready, QB)
            for b in range(QB):
                own = S[:, b, PADS + EXT[b] - P:PADS + EXT[b]]
                tt(own, own, hide[:], ALU.min).then_inc(mask_ready, 1)

            dve.wait_ge(vec_ready, 1)
            step(tt(GF1[:], VEC[:, 0, V_FIN:V_FIN + KC], VEC[:, 0, V_N1:V_N1 + KC], ALU.mult))
            lam = VEC[:, 0, V_LAM:V_LAM + 4]
            stt(out=small[:, 0:4], in0=lam, scalar=-1.0, in1=lam, op0=ALU.mult, op1=ALU.max).then_inc(cl_ready, 1)
            dve.wait_ge(small_loaded, 16 * 5)
            step(tt(LAMV[:, 0, :], LAMV[:, 0, :], LAMV[:, 1, :], ALU.mult))
            step(tt(LAMV[:, 2, :], LAMV[:, 2, :], LAMV[:, 3, :], ALU.mult))
            settled()
            nc.vector.tensor_reduce(small[:, 40:42], LAMV[:, 0:4:2, :], AX.X, ALU.add).then_inc(lam_sum, 1)
            dve.wait_ge(cl_exp, 1)
            e, q, z, z2 = small[:, 4:8], small[:, 8:12], small[:, 32:36], small[:, 36:40]
            step(ts(q, e, 2.0, None, ALU.add))
            settled()
            step(nc.vector.reciprocal(z, q))
            settled()
            step(tt(z, z, e, ALU.mult))
            settled()
            step(tt(z2, z, z, ALU.mult))
            settled()
            step(ts(q, z2, 1.0 / 15, None, ALU.mult))
            for m in (13, 11, 9, 7, 5, 3):
                settled()
                step(stt(out=q, in0=q, scalar=1.0 / m, in1=z2, op0=ALU.add, op1=ALU.mult))
            settled()
            step(stt(out=q, in0=q, scalar=1.0, in1=z, op0=ALU.add, op1=ALU.mult))
            step(ts(small[:, 12:16], lam, -1.0, 0.0, ALU.mult, ALU.max))
            settled()
            step(stt(out=q, in0=q, scalar=2.0, in1=small[:, 12:16], op0=ALU.mult, op1=ALU.add))
            settled()
            step(ts(small[:, 16:20], q, -4.0, None, ALU.mult))
            step(ts(small[:, 20:24], q, 4.0, None, ALU.mult))
            step(ts(small[:, 24:28], VEC[:, 0, V_BR:V_BR + 4], 0.5, None, ALU.mult))
            step(ts(small[:, 28:32], VEC[:, 0, V_BI:V_BI + 4], 0.5, None, ALU.mult))
            step(ts(GSUB[:], GSUB[:], 1.0 - LAM_INIT, None, ALU.mult))
            dve.wait_ge(lam_e, 1)
            step(tt(small[:, 44:45], small[:, 43:44], small[:, 42:43], ALU.subtract))
            settled()
            step(ts(small[:, 44:45], small[:, 44:45], LAM_INIT, None, ALU.subtract))
            settled()

            dve.wait_ge(freed["act"], LETGO["cc"]["act"])
            with dve.Fori(0, 4) as i:
                for j in range(2):
                    after("cc", i * 2 + j)
                    u = cols(pick(U, i * 2 + j), N)
                    tt(u, u, PJ[:, slot_of("cc", j), :, 0:HALF], ALU.mult).then_inc(freed["dve"], 1)

            dve.wait_ge(mask_ready, 2 * QB)
            dve.wait_ge(freed["dve"], LETGO["gates"]["dve"])
            units = [(j, b) for j in range(2) for b in range(QB)]
            NU = len(units)
            with dve.Fori(0, 4) as i:
                def conv(j):
                    c = i * 2 + j
                    def tap(t):
                        return VEC[:, 0, bass.ds(c + (V_CW + t * KC), 1)]
                    def seen(t):
                        return U[:, bass.ds(c, 1), META - 2 + t:N - 2 + t].rearrange("p o n -> p (o n)")
                    dve.wait_ge(freed["dve"], i * 2 + (LETGO["gates"]["dve"] - 1 + j))
                    ts(CT[:, j], seen(2), tap(2), None, ALU.mult).then_inc(conv_step, 1)
                    for t in (1, 0):
                        dve.wait_ge(conv_step, i * 6 + (3 * j + 2 - t))
                        stt(out=CT[:, j], in0=seen(t), scalar=tap(t), in1=CT[:, j], op0=ALU.mult, op1=ALU.add).then_inc(conv_step, 1)

                for s in range(NU + 2):
                    if s in (1, 7):
                        j = s // 6
                        after("gates", i * 6 + 3 * j)
                        dve.wait_ge(conv_step, i * 6 + 3 * (j + 1))
                        tt(U[:, bass.ds(i * 2 + j, 1), META:N].rearrange("p o n -> p (o n)"), CT[:, j],
                           PJ[:, slot_of("gates", 3 * j), 0, :], ALU.mult).then_inc(freed["dve"], 1)
                    if 0 <= s - 1 < NU:
                        u = s - 1
                        dve.wait_ge(exp_done, i * NU + (u + 1))
                        nc.vector.reciprocal(RINV[:, u % 4:u % 4 + 1], RS[:, u % 2:u % 2 + 1]).then_inc(rinv_ready, 1)
                    if 0 <= s - 2 < NU:
                        u = s - 2
                        dve.wait_ge(rinv_ready, i * NU + (u + 1))
                        dve.wait_ge(pv_done, i * NU + (u + 1))
                        ts(YS[:, u % 2], PB7[:, 0:P], RINV[:, u % 4:u % 4 + 1], None, ALU.mult).then_inc(ys_ready, 1)
                    if s < NU:
                        b = units[s][1]
                        dve.wait_ge(qk_done, i * NU + (s + 1))
                        tt(LT[:, s % 2, 0:EXT[b]], PX_flat[:, 0:EXT[b]], S[:, b, PADS:PADS + EXT[b]], ALU.add).then_inc(logits_ready, 1)
                        dve.wait_ge(logits_ready, i * NU + (s + 2))
                        nc.vector.tensor_reduce(NMX[:, s % 2:s % 2 + 1], LT[:, s % 2, 0:EXT[b]], AX.X, ALU.max, negate=True).then_inc(max_ready, 1)
                    if s in (0, 5):
                        conv(s // 5)

            for k in range(KC):
                dve.wait_ge(a_hi, A_USE["conv"] + k + 1)
                tt(AL[:, k, 0:T], U[:, k, META:N], AH[:, k, 0:T].bitcast(F32), ALU.subtract).then_inc(a_lo, 1)
            for k in range(KC):
                dve.wait_ge(b_hi, B_USE["y"] + k + 1)
                tt(BL[:, k], QT[:, k], BH[:, k].bitcast(F32), ALU.subtract).then_inc(b_lo, 1)
            dve.wait_ge(b_lo, B_USE["y"] + KC)
            nc.vector.memset(WR[:], 0.0).then_inc(wr_cleared, 1)
            step(nc.vector.memset(XA[:, :, 0:3], 0.0))

            with dve.Fori(0, 4) as i:
                for j in range(2):
                    after("co", i * 2 + j)
                    g = pick(GB, i * 2 + j)
                    stt(out=g, in0=g, scalar=1.0, in1=PJ[:, slot_of("co", j), 0, :], op0=ALU.add, op1=ALU.mult).then_inc(freed["dve"], 1)
            with dve.Fori(0, 4) as i:
                for j in range(2):
                    c = i * 2 + j
                    after("ao", c)
                    ga, gb = pick(GA, c), pick(GB, c)
                    stt(out=ga, in0=ga, scalar=1.0, in1=PJ[:, slot_of("ao", j), 0, :], op0=ALU.add, op1=ALU.mult).then_inc(freed["dve"], 1)
                    dve.wait_ge(freed["dve"], c + (LETGO["ao"]["dve"] + 1))
                    tt(gb, ga, gb, ALU.add).then_inc(mixed_ready, 1)
                    dve.wait_ge(a_hi, c + (A_USE["mixed"] + 1))
                    tt(AL[:, bass.ds(c, 1), 0:T].rearrange("p o n -> p (o n)"), gb,
                       AH[:, bass.ds(c, 1), 0:T].rearrange("p o n -> p (o n)").bitcast(F32), ALU.subtract).then_inc(a_lo, 1)

            def begin(norm_name):
                dve.sem_inc(ss_added[norm_name], 1)
                nc.vector.memset(SS[:], 0.0).then_inc(ss_added[norm_name], 1)

            def feed(norm_name, c, j, gain, hi_dst, lo_dst, hi, lo, use):
                if hi_dst is not None:
                    dve.wait_ge(hi, c + (use + 1))
                    stt(out=chunk_of(lo_dst, c), in0=pick(H, c), scalar=VEC[:, 0, bass.ds(c + gain, 1)], in1=chunk_of(hi_dst, c).bitcast(F32),
                        op0=ALU.mult, op1=ALU.subtract).then_inc(lo, 1)
                dve.wait_ge(sq_ready[norm_name], c + 1)
                dve.wait_ge(ss_added[norm_name], c + 2)
                tt(SS[:], SS[:], SQT[:, j], ALU.add).then_inc(ss_added[norm_name], 1)

            def residual(name, scale, to=None):
                if to:
                    begin(to[0])
                with dve.Fori(0, COUNT[name] // 2) as i:
                    for j in range(2):
                        after(name, i * 2 + j)
                        h = pick(H, i * 2 + j)
                        stt(out=h, in0=PJ[:, slot_of(name, j), 0, :], scalar=scale, in1=h, op0=ALU.mult, op1=ALU.add).then_inc(freed["dve"], 1)
                        if to:
                            feed(to[0], i * 2 + j, j, *to[1:])
                        if to and to[0] == "fin2":
                            dve.wait_ge(freed["dve"], i * 2 + (LETGO[name]["dve"] + j + 1))
                            ts(pick(HG, i * 2 + j), h, VEC[:, 0, bass.ds(i * 2 + (V_FIN2 + j), 1)], None, ALU.mult).then_inc(hg_ready, 1)

            def late_scale(name):
                dve.wait_ge(rt_ready[name], 1)
                nc.vector.reciprocal(R[:], ROOT[:]).then_inc(rstd_ready[name], 1)
                dve.wait_ge(rstd_ready[name], 1)

            dve.wait_ge(h_loaded, 16)
            residual("wo", 0.5, ("ffn", V_FFN, BH, BL, b_hi, b_lo, B_USE["ffn"]))
            late_scale("ffn")
            for g, (c0, n) in enumerate(GROUPS):
                name = f"gu{g}"
                with dve.Fori(0, n // 2) as i:
                    for j in range(2):
                        q = i * 2 + j
                        after(name, i * 4 + 2 * j)
                        dve.wait_ge(a_lo, q + (A_USE[f"act{g}"] - 1))
                        tt(T1[:, j], PJ[:, slot_of(name, 0), 0, :], R[:], ALU.mult).then_inc(freed["dve"], 1)
                        dve.wait_ge(freed["dve"], i * 4 + (LETGO[name]["dve"] + 2 * j + 1))
                        dve.sem_inc(gate_scaled, 1)
                        after(name, i * 4 + (2 * j + 1))
                        tt(T2[:, j], PJ[:, slot_of(name, 1), 0, :], R[:], ALU.mult).then_inc(freed["dve"], 1)
                        dve.wait_ge(tanh_ready, q + (c0 + 1))
                        stt(out=T1[:, j], in0=SG[:, j], scalar=1.0, in1=T1[:, j], op0=ALU.add, op1=ALU.mult).then_inc(silu_ready, 1)
                        dve.wait_ge(silu_ready, q + (c0 + 1))
                        dve.wait_ge(freed["dve"], i * 4 + (LETGO[name]["dve"] + 2 * j + 2))
                        tt(T2[:, j], T1[:, j], T2[:, j], ALU.mult).then_inc(ff_step, 1)
                        dve.wait_ge(a_hi, q + (A_USE[f"act{g}"] + 1))
                        tt(chunk_of(AL, q), T2[:, j], chunk_of(AH, q).bitcast(F32), ALU.subtract).then_inc(a_lo, 1)
                if g < 2:
                    residual(f"dn{g}", 0.5)
            dve.wait_ge(a_lo, A_USE["act2"] + GROUPS[2][1])
            step(nc.vector.memset(SSB[:], 0.0))
            begin("n1")
            settled()
            with dve.Fori(0, KC // 2) as i:
                for j in range(2):
                    c = i * 2 + j
                    after("dn2", c)
                    h = pick(H, c)
                    stt(out=h, in0=PJ[:, slot_of("dn2", j), 0, :], scalar=0.5, in1=h, op0=ALU.mult, op1=ALU.add).then_inc(freed["dve"], 1)
                    dve.wait_ge(b_hi, c + (B_USE["n1"] + 1))
                    stt(out=pick(BL, c), in0=h, scalar=GF1[:, bass.ds(c, 1)], in1=pick(BH, c).bitcast(F32),
                        op0=ALU.mult, op1=ALU.subtract).then_inc(b_lo, 1)
                    dve.wait_ge(sq_ready["n1"], c + 1)
                    dve.wait_ge(ss_added["n1"], c + 2)
                    tt(SSB[:], SSB[:], SQB[:, j], ALU.add)
                    tt(SS[:], SS[:], SQT[:, j], ALU.add).then_inc(ss_added["n1"], 1)

            dve.wait_ge(ss_summed["n1"], 1)
            step(ts(R[:], PX[:, 0, 0:T], EPS, None, ALU.mult))
            settled()
            tt(R[:], R[:], PX[:, 1, 0:T], ALU.add).then_inc(fin_ms, 1)
            dve.wait_ge(rt_ready["n1"], 1)
            nc.vector.reciprocal(R[:], ROOT[:]).then_inc(rstd_ready["n1"], 1)
            dve.wait_ge(rstd_ready["n1"], 1)

            def scaled(name, c, dst):
                after(name, c)
                tt(dst, PJ[:, slot_of(name, c), 0, :], R[:], ALU.mult).then_inc(freed["dve"], 1)

            for c in range(4):
                scaled("dqk", c, DQK[:, c])
            dve.wait_ge(rt_ready["n1"], 2)
            step(nc.vector.reciprocal(RF[:], RF[:]))
            settled()
            for c in range(KC):
                step(stt(out=H[:, c], in0=H[:, c], scalar=VEC[:, 0, V_FIN + c:V_FIN + c + 1], in1=RF[:], op0=ALU.mult, op1=ALU.mult))
            for j in range(2):
                scaled("dv", j, VT2[:, j])
            settled()
            places = {"xa": lambda c: XA[:, c, 3:T + 3], "ya": lambda c: YA[:, c], "sqk": lambda c: SQK[:, c], "sv": lambda c: VT2[:, c]}

            def df_step(u):
                if u < len(DF_UNITS):
                    n, b = DF_UNITS[u]
                    E = (b + 1) * P
                    if b == 0:
                        step(ts(BIAS[:], DIST[:], -SLOPES[n], None, ALU.mult))
                        settled()
                        step(nc.vector.memset(BIAS[0:64, T - 64:T], HIDDEN))
                        settled()
                    at = 48 + 2 * (u % 2)
                    l = L[:, u % 2, :, 0:E]
                    dve.wait_ge(df_qk, u + 1)
                    stt(out=l, in0=PX[:, :, 0:E], scalar=DF_SCALE, in1=BIAS[:, T - E:T].unsqueeze(1).to_broadcast([P, 2, E]),
                        op0=ALU.mult, op1=ALU.add).then_inc(df_lt, 1)
                    dve.wait_ge(df_lt, u + 1)
                    nc.vector.tensor_reduce(small[:, at:at + 2], l, AX.X, ALU.max, negate=True).then_inc(df_max, 1)
                if 1 <= u <= len(DF_UNITS):
                    v = u - 1
                    E = (DF_UNITS[v][1] + 1) * P
                    at = 2 * (v % 2)
                    l1, l2 = L[:, v % 2, 0, 0:E], L[:, v % 2, 1, 0:E]
                    r1, r2 = small[:, 56 + at:57 + at], small[:, 57 + at:58 + at]
                    dve.wait_ge(df_exp, 2 * v + 2)
                    step(nc.vector.reciprocal(small[:, 56 + at:58 + at], small[:, 52 + at:54 + at]))
                    settled()
                    step(tt(r2, r2, small[:, 44:45], ALU.mult))
                    step(ts(l1, l1, r1, None, ALU.mult))
                    settled()
                    stt(out=l1, in0=l2, scalar=r2, in1=l1, op0=ALU.mult, op1=ALU.add).then_inc(df_p, 1)

            def conv_a(c):
                def tap(t):
                    return VEC[:, 0, V_CAW + 4 * t + c:V_CAW + 4 * t + c + 1]
                dve.wait_ge(freed["dve"], LETGO["xa"]["dve"] + c + 1)
                step(ts(XC[:, c], XA[:, c, 3:T + 3], tap(3), VEC[:, 0, V_CAB + c:V_CAB + c + 1], ALU.mult, ALU.add))
                for t in (2, 1, 0):
                    settled()
                    ins = stt(out=XC[:, c], in0=XA[:, c, t:T + t], scalar=tap(t), in1=XC[:, c], op0=ALU.mult, op1=ALU.add)
                    if t:
                        step(ins)
                    else:
                        ins.then_inc(xc_ready, 1)

            def gelu_inner(h):
                y, g = YA[:, 2 * h:2 * h + 2], GY[:, 2 * h:2 * h + 2]
                dve.wait_ge(freed["dve"], LETGO["ya"]["dve"] + 2 * h + 2)
                step(tt(g, y, y, ALU.mult))
                settled()
                step(ts(g, g, 0.044715, 1.0, ALU.mult, ALU.add))
                settled()
                tt(g, g, y, ALU.mult).then_inc(gelu_in, 1)

            def decay(c):
                dve.wait_ge(lru_a, 2 * c + 2)
                step(tt(A2[:, c % 2], RP[:, c], RP[:, c], ALU.mult))
                settled()
                stt(out=TH[:, c], in0=A2[:, c % 2], scalar=1.0, in1=TH[:, c], op0=ALU.add, op1=ALU.mult).then_inc(lru_q, 1)
                dve.wait_ge(xc_ready, c + 1)
                dve.wait_ge(lru_q, c + 1)
                step(stt(out=IP[:, c], in0=IP[:, c], scalar=1.0, in1=XC[:, c], op0=ALU.add, op1=ALU.mult))

            def recurrence():
                dve.wait_ge(lru_root, 1)
                settled()
                step(tt(IP[:], IP[:], TH[:], ALU.mult))
                settled()
                for c in range(4):
                    step(nc.vector.tensor_tensor_scan(XC[:, c], RP[:, c], IP[:, c], 0.0, ALU.mult, ALU.add))

            for s, (name, c) in enumerate(BESIDE):
                df_step(s)
                if 1 <= s < 5:
                    conv_a(s - 1)
                if 6 <= s < 10:
                    if s == 6:
                        dve.wait_ge(v2_turned, 2)
                    decay(s - 6)
                if s in (7, 9):
                    gelu_inner((s - 7) // 2)
                if s == 11:
                    dve.wait_ge(gelu_t, 1)
                    step(stt(out=GY[:], in0=GY[:], scalar=1.0, in1=YA[:], op0=ALU.add, op1=ALU.mult))
                if s == 12:
                    recurrence()
                if s == 13:
                    settled()
                    stt(out=XC[:], in0=XC[:], scalar=0.5, in1=GY[:], op0=ALU.mult, op1=ALU.mult).then_inc(outa_ready, 1)
                scaled(name, c, places[name](c))

            def sb_lo(n):
                r, c = 64 * (n % 2), n // 2
                dve.wait_ge(b_hi, B_USE["m2"] + M2[f"sb{n}"])
                tt(BL[r:r + 64, 4 + c, :], SB_OUT[r:r + 64, :], BH[r:r + 64, 4 + c, :].bitcast(F32), ALU.subtract).then_inc(b_lo, 1)

            def lru_residual(i):
                after("wo2a", i)
                tt(H[:, 2 * i], PJ[:, 0, 0, :], H[:, 2 * i], ALU.add)
                tt(H[:, 2 * i + 1], PJ[:, 1, 0, :], H[:, 2 * i + 1], ALU.add).then_inc(freed["dve"], 1)

            def sb_floor(n):
                dve.wait_ge(z_ready, 3 * (n + 1))
                step(ts(LG[:], Z[:, n % 2], 0.0, None, ALU.max))

            def sb_logs(n):
                settled()
                dve.wait_ge(sb_ln, n + 1)
                step(stt(out=LG[:], in0=LG[:], scalar=-1.0, in1=LN[:], op0=ALU.mult, op1=ALU.subtract))
                settled()
                for i in range(QB):
                    last = tt(LG[:, SBO[i]:SBO[i] + P], LG[:, SBO[i]:SBO[i] + P], before[:], ALU.mult)
                last.then_inc(sb_log, 1)

            oc = OC[:].rearrange("p b (n d) -> p (b n) d", d=64)
            osq = OSQ[:].rearrange("p b (n d) -> p (b n) d", d=64)

            df_step(14)
            dve.wait_ge(b_hi, B_USE["m2"] + M2["lru"])
            tt(BL[:, 0:4, :], XC[:], BH[:, 0:4, :].bitcast(F32), ALU.subtract).then_inc(b_lo, 1)
            df_step(15)
            df_step(16)
            lru_residual(0)
            sb_floor(0)
            sb_logs(0)
            dve.wait_ge(df_o, len(DF_UNITS))
            dve.wait_ge(v2_turned, 4)
            step(tt(osq, oc, oc, ALU.mult))
            settled()
            nc.vector.tensor_reduce(small[:, 64:80], osq, AX.X, ALU.add).then_inc(oc_sq, 1)
            lru_residual(1)
            for n in range(4):
                z = Z[:, n % 2]
                for m, (i0, o, w) in enumerate(SB_BANKS):
                    dve.wait_ge(tail_done, 3 * n + m + 1)
                    tt(z[:, o:o + w], SB_TAIL[m][:, 0:w], z[:, o:o + w], ALU.add).then_inc(sb_sum, 1)
                if n < 3:
                    sb_floor(n + 1)
                dve.wait_ge(sb_w, n + 1)
                for i in range(QB):
                    last = tt(z[:, SBO[i]:SBO[i] + P], z[:, SBO[i]:SBO[i] + P], before[:], ALU.mult)
                last.then_inc(sb_masked, 1)
                if n < 3:
                    sb_logs(n + 1)
                if n == 0:
                    dve.wait_ge(oc_root, 1)
                    step(nc.vector.reciprocal(small[:, 96:112], small[:, 80:96]))
                    settled()
                    step(tt(oc, oc, small[:, 96:112].unsqueeze(2).to_broadcast([P, 16, 64]), ALU.mult))
                sb_lo(n)
                if n == 0:
                    settled()
                    tt(oc, oc, GSUB[:].unsqueeze(1).to_broadcast([P, 16, 64]), ALU.mult).then_inc(oc_ready, 1)
                if n % 2 == 1:
                    lru_residual(2 + n // 2)
                if n == 1:
                    for c in range(2):
                        dve.wait_ge(b_hi, B_USE["m2"] + M2[f"df{c}"])
                        tt(BL[:, 6 + c, :], SIDE[c], BH[:, 6 + c, :].bitcast(F32), ALU.subtract).then_inc(b_lo, 1)

            begin("n2")
            with dve.Fori(0, COUNT["wo2b"] // 2) as i:
                for j in range(2):
                    after("wo2b", i * 2 + j)
                    h = H[:, bass.ds(i * 4 + 2 * j, 2), :]
                    tt(h, PJ[:, slot_of("wo2b", j)], h, ALU.add).then_inc(freed["dve"], 1)
                    for b in range(2):
                        feed("n2", i * 4 + (2 * j + b), b, V_N2, AH, AL, a_hi, a_lo, A_USE["n2"])
            late_scale("n2")
            for g, (c0, n) in enumerate(GROUPS):
                name = f"gv{g}"
                with dve.Fori(0, n // 2) as i:
                    for j in range(2):
                        q = i * 2 + j
                        t1, us = T1[:, 2 * j:2 * j + 2], US[:, 2 * j:2 * j + 2]

                        def scale_product(m):
                            after(name, i * 4 + (2 * j + m))
                            tt(us[:, m], PJ[:, slot_of(name, m), 0, :], R[:], ALU.mult).then_inc(freed["dve"], 1)

                        def earlier_taps(m):
                            dve.wait_ge(conv_base, i * 4 + (2 * c0 + 2 * j + m + 1))
                            stt(out=t1[:, m, 1:T], in0=us[:, m, 0:T - 1], scalar=VEC[:, 1, bass.ds(q + (2 * FFC + FFC * m + c0), 1)],
                                in1=t1[:, m, 1:T], op0=ALU.mult, op1=ALU.add).then_inc(conv_step, 1)
                            dve.wait_ge(conv_step, i * 4 + (24 + 2 * c0 + 2 * j + m + 1))
                            stt(out=t1[:, m, 2:T], in0=us[:, m, 0:T - 2], scalar=VEC[:, 1, bass.ds(q + (FFC * m + c0), 1)],
                                in1=t1[:, m, 2:T], op0=ALU.mult, op1=ALU.add).then_inc(taps_done, 1)

                        def low_part(j):
                            dve.wait_ge(b_hi, i * 2 + (j + B_USE[f"ff{g}"] + 1))
                            tt(pick(BL, i * 2 + j), T2[:, j], pick(BH, i * 2 + j).bitcast(F32), ALU.subtract).then_inc(b_lo, 1)

                        dve.wait_ge(b_lo, q + (B_USE[f"ff{g}"] - 1))
                        scale_product(0)
                        if j == 1:
                            low_part(0)
                        earlier_taps(0)
                        scale_product(1)
                        dve.wait_ge(tanh_ready, q + (FFC + c0 + 1))
                        stt(out=SG[:, j], in0=SG[:, j], scalar=1.0, in1=t1[:, 0], op0=ALU.add, op1=ALU.mult).then_inc(silu_ready, 1)
                        earlier_taps(1)
                        dve.wait_ge(silu_ready, q + (FFC + c0 + 1))
                        dve.wait_ge(taps_done, i * 4 + (2 * c0 + 2 * j + 2))
                        tt(T2[:, j], SG[:, j], t1[:, 1], ALU.mult).then_inc(ff_step, 1)
                        if j == 1:
                            low_part(1)
                residual(f"ed{g}", 0.5, ("fin2", None, None, None, None, None, None) if g == 2 else None)
            dve.wait_ge(rt_ready["fin2"], 1)
            nc.vector.reciprocal(small[:, 116:120], small[:, 112:116]).then_inc(rstd_ready["fin2"], 1)
            dve.wait_ge(rstd_ready["fin2"], 1)
            for b in (1, 3):
                dve.wait_ge(out_turned, b + 1)
                ts(OUT[:, b], OUT_BANKS[b].rearrange("p a n -> p (a n)"), small[:, 116 + b:117 + b], None, ALU.mult).then_inc(out_ready_dve, 1)


_INS = ["x", "meta_tokens", "norm_mix_g", "w_in", "w_attn_out", "conv_w", "w_conv_out", "w_out", "norm_ffn_g", "w_gate",
        "w_up", "w_down", "norm_final_g", "norm1_g_2", "w_in_2", "conv_a_w_2", "conv_a_b_2", "w_rgate_2", "b_rgate_2",
        "w_igate_2", "b_igate_2", "lru_lambda_2", "lam_q1_2", "lam_k1_2", "lam_q2_2", "lam_k2_2", "subln_g_2",
        "w_out_2", "norm2_g_2", "w_ff_up_2", "conv_ff_w_2", "conv_ff_b_2", "w_ff_down_2", "final_g_2"]


def kernel(**inputs):
    import concourse.bacc as _bacc
    from concourse.bass_utils import run_bass_kernel_spmd as _run

    nc = _bacc.Bacc("TRN2", target_bir_lowering=False, num_devices=1)
    arrays, args = {}, []
    for name in _INS:
        a = np.ascontiguousarray(inputs[name])
        arrays[f"in_{name}_dram"] = a
        args.append(nc.dram_tensor(f"in_{name}_dram", a.shape, mybir.dt.from_np(a.dtype), kind="ExternalInput").ap())
    args.append(nc.dram_tensor("out_0_dram", (1, T, D), F32, kind="ExternalOutput").ap())
    two_blocks(nc, *args)
    r = _run(nc, [arrays], core_ids=[0])
    return r.results[0]["out_0_dram"]
```
